# Optimizing a Trainium2 kernel written in Bass

```python
import math
import jax, jax.numpy as jnp
from jax import lax
import numpy as np
import jax
import jax.numpy as jnp

D_MODEL = 1024
BATCH = 1
SEQ = 512
DEPTH = 1

HEAD_DIM = 64
MIX_WIDTH = D_MODEL
N_GROUPS = 4
GROUP_WIDTH = MIX_WIDTH // N_GROUPS
HEADS_PER_GROUP = GROUP_WIDTH // HEAD_DIM
FOX_HEADS = HEADS_PER_GROUP
MOBA_HEADS = HEADS_PER_GROUP
SB_HEADS = HEADS_PER_GROUP
SWA_HEADS = HEADS_PER_GROUP
SWA_KV_HEADS = SWA_HEADS // 2
SWA_KV_WIDTH = SWA_KV_HEADS * HEAD_DIM
QUERY_BLOCK = 128
MOBA_BLOCK = 256
MOBA_TOPK = 3
MOBA_QUERY_CHUNK = 32
SWA_WINDOW = 128
NUM_BUCKETS = 32
REL_MAX_DISTANCE = 1024
RMS_EPS = 1e-6
FORGET_BIAS_INIT = 2.0
NEG_INF = -1e30
ATTN_SCALE = HEAD_DIM ** -0.5
SPLIT_SIZES = (
    GROUP_WIDTH, GROUP_WIDTH, GROUP_WIDTH, FOX_HEADS, GROUP_WIDTH,
    GROUP_WIDTH, GROUP_WIDTH, GROUP_WIDTH, GROUP_WIDTH,
    GROUP_WIDTH, GROUP_WIDTH, GROUP_WIDTH, GROUP_WIDTH,
    GROUP_WIDTH, SWA_KV_WIDTH, SWA_KV_WIDTH, GROUP_WIDTH,
)
IN_WIDTH = sum(SPLIT_SIZES)


def rms_norm(x, gain):
    xf = x.astype(jnp.float32)
    y = xf * lax.rsqrt(jnp.mean(xf * xf, axis=-1, keepdims=True) + RMS_EPS)
    return (y * gain.astype(jnp.float32)).astype(x.dtype)

def split_columns(proj):
    parts, off = [], 0
    for w in SPLIT_SIZES:
        parts.append(proj[..., off:off + w])
        off += w
    return parts

def to_heads(t, n):
    b, s, _ = t.shape
    return t.reshape(b, s, n, HEAD_DIM).transpose(0, 2, 1, 3)

def from_heads(o):
    b, h, s, d = o.shape
    return o.transpose(0, 2, 1, 3).reshape(b, s, h * d)

def unblock(out):
    nb, b, h, qb, d = out.shape
    return out.transpose(1, 2, 0, 3, 4).reshape(b, h, nb * qb, d)

def rel_bucket(dist):
    max_exact = NUM_BUCKETS // 2
    d = jnp.maximum(dist, 0)
    log_ratio = jnp.log(jnp.maximum(d, 1).astype(jnp.float32) / max_exact) / math.log(REL_MAX_DISTANCE / max_exact)
    large = max_exact + (log_ratio * (NUM_BUCKETS - max_exact)).astype(jnp.int32)
    large = jnp.minimum(large, NUM_BUCKETS - 1)
    return jnp.where(d < max_exact, d, large)

def forgetting_attention(q, k, v, log_f):
    b, h, t_len, d = q.shape
    c = jnp.cumsum(log_f, axis=-1)
    pos = jnp.arange(t_len)

    def block(i):
        start = i * QUERY_BLOCK
        q_i = lax.dynamic_slice_in_dim(q, start, QUERY_BLOCK, axis=2)
        c_i = lax.dynamic_slice_in_dim(c, start, QUERY_BLOCK, axis=2)
        t = start + jnp.arange(QUERY_BLOCK)
        s = jnp.einsum('bhqd,bhkd->bhqk', q_i, k).astype(jnp.float32) * ATTN_SCALE
        s = s + c_i[..., :, None] - c[..., None, :]
        s = jnp.where(t[:, None] >= pos[None, :], s, NEG_INF)
        p = jax.nn.softmax(s, axis=-1).astype(v.dtype)
        return jnp.einsum('bhqk,bhkd->bhqd', p, v)

    return unblock(lax.map(block, jnp.arange(t_len // QUERY_BLOCK)))

def moba_attention(q, k, v, rel_bias_h):
    b, h, t_len, d = q.shape
    t_pad = -(-t_len // MOBA_BLOCK) * MOBA_BLOCK
    if t_pad != t_len:
        padw = ((0, 0), (0, 0), (0, t_pad - t_len), (0, 0))
        q, k, v = jnp.pad(q, padw), jnp.pad(k, padw), jnp.pad(v, padw)
    nblk = t_pad // MOBA_BLOCK
    k_eff = min(MOBA_TOPK, nblk)
    k_blocks = k.reshape(b, h, nblk, MOBA_BLOCK, d)
    v_blocks = v.reshape(b, h, nblk, MOBA_BLOCK, d)
    k_mean = jnp.mean(k_blocks.astype(jnp.float32), axis=3)
    gate = jnp.einsum('bhtd,bhnd->bhtn', q.astype(jnp.float32), k_mean)
    q_blk = jnp.arange(t_pad) // MOBA_BLOCK
    past = jnp.arange(nblk)[None, :] < q_blk[:, None]
    gate = jnp.where(past, gate, NEG_INF)
    _, sel = lax.top_k(gate, k_eff)
    n_valid = jnp.minimum(q_blk, k_eff)
    sel_valid = jnp.arange(k_eff)[None, :] < n_valid[:, None]
    b_idx = jnp.arange(b)[:, None, None, None]
    h_idx = jnp.arange(h)[None, :, None, None]
    h_idx5 = h_idx[..., None]
    blk_off = jnp.arange(MOBA_BLOCK)

    def chunk(ci):
        start = ci * MOBA_QUERY_CHUNK
        q_c = lax.dynamic_slice_in_dim(q, start, MOBA_QUERY_CHUNK, axis=2)
        sel_c = lax.dynamic_slice_in_dim(sel, start, MOBA_QUERY_CHUNK, axis=2)
        valid_c = lax.dynamic_slice_in_dim(sel_valid, start, MOBA_QUERY_CHUNK, axis=0)
        t = start + jnp.arange(MOBA_QUERY_CHUNK)
        k_sel = k_blocks[b_idx, h_idx, sel_c]
        v_sel = v_blocks[b_idx, h_idx, sel_c]
        s_sel = jnp.einsum('bhqd,bhqnkd->bhqnk', q_c, k_sel).astype(jnp.float32) * ATTN_SCALE
        key_pos = sel_c[..., None] * MOBA_BLOCK + blk_off
        dist = t[None, None, :, None, None] - key_pos
        s_sel = s_sel + rel_bias_h[h_idx5, rel_bucket(dist)].astype(jnp.float32)
        s_sel = jnp.where(valid_c[None, None, :, :, None], s_sel, NEG_INF)
        own_start = (start // MOBA_BLOCK) * MOBA_BLOCK
        k_own = lax.dynamic_slice_in_dim(k, own_start, MOBA_BLOCK, axis=2)
        v_own = lax.dynamic_slice_in_dim(v, own_start, MOBA_BLOCK, axis=2)
        s_own = jnp.einsum('bhqd,bhkd->bhqk', q_c, k_own).astype(jnp.float32) * ATTN_SCALE
        dist_own = t[:, None] - (own_start + blk_off)[None, :]
        s_own = s_own + rel_bias_h[:, rel_bucket(dist_own)][None].astype(jnp.float32)
        s_own = jnp.where(dist_own >= 0, s_own, NEG_INF)
        n_sel = k_eff * MOBA_BLOCK
        s_all = jnp.concatenate([s_sel.reshape(b, h, MOBA_QUERY_CHUNK, n_sel), s_own], axis=-1)
        p = jax.nn.softmax(s_all, axis=-1).astype(v.dtype)
        p_sel = p[..., :n_sel].reshape(b, h, MOBA_QUERY_CHUNK, k_eff, MOBA_BLOCK)
        p_own = p[..., n_sel:]
        return (jnp.einsum('bhqnk,bhqnkd->bhqd', p_sel, v_sel)
                + jnp.einsum('bhqk,bhkd->bhqd', p_own, v_own))

    out = unblock(lax.map(chunk, jnp.arange(t_pad // MOBA_QUERY_CHUNK)))
    return out[:, :, :t_len]

def stick_breaking_attention(q, k, v):
    b, h, t_len, d = q.shape
    pos = jnp.arange(t_len)

    def block(i):
        start = i * QUERY_BLOCK
        q_i = lax.dynamic_slice_in_dim(q, start, QUERY_BLOCK, axis=2)
        t = start + jnp.arange(QUERY_BLOCK)
        z = jnp.einsum('bhqd,bhkd->bhqk', q_i, k).astype(jnp.float32) * ATTN_SCALE
        strict = pos[None, :] < t[:, None]
        log_keep = jnp.where(strict, jax.nn.log_sigmoid(-z), 0.0)
        suffix = lax.cumsum(log_keep, axis=3, reverse=True) - log_keep
        a = jnp.where(strict, jnp.exp(jax.nn.log_sigmoid(z) + suffix), 0.0)
        return jnp.einsum('bhqk,bhkd->bhqd', a.astype(v.dtype), v)

    return unblock(lax.map(block, jnp.arange(t_len // QUERY_BLOCK)))

def swa_sink_attention(q, k, v, sinks, rel_bias_h):
    b, h, t_len, d = q.shape
    hkv = k.shape[1]
    g = h // hkv
    w = SWA_WINDOW
    nb = t_len // w
    qb = q.reshape(b, hkv, g, nb, w, d)

    def band(a):
        ab = a.reshape(b, hkv, nb, w, d)
        prev = jnp.pad(ab, ((0, 0), (0, 0), (1, 0), (0, 0), (0, 0)))[:, :, :-1]
        return jnp.concatenate([prev, ab], axis=3)

    kb, vb = band(k), band(v)
    s = jnp.einsum('bkgnqd,bknsd->bkgnqs', qb, kb).astype(jnp.float32) * ATTN_SCALE
    qi = jnp.arange(w)
    kj = jnp.arange(2 * w)
    dist = qi[:, None] + w - kj[None, :]
    bias = rel_bias_h[:, rel_bucket(dist)].astype(jnp.float32).reshape(hkv, g, 1, w, 2 * w)
    key_pos = jnp.arange(nb)[:, None] * w - w + kj[None, :]
    allowed = ((dist >= 0) & (dist < w))[None] & (key_pos >= 0)[:, None, :]
    s = jnp.where(allowed, s + bias, NEG_INF)
    sink = jnp.broadcast_to(sinks.astype(jnp.float32).reshape(1, hkv, g, 1, 1, 1), s.shape[:-1] + (1,))
    p = jax.nn.softmax(jnp.concatenate([s, sink], axis=-1), axis=-1)[..., :-1]
    o = jnp.einsum('bkgnqs,bknsd->bkgnqd', p.astype(v.dtype), vb)
    return o.reshape(b, h, t_len, d)

def hybrid_layer(x, norm_gain, w_in, b_forget, fox_qk_gain, moba_qk_gain, swa_qk_gain, sinks, w_out, rel_bias):
    hn = rms_norm(x, norm_gain)
    proj = jnp.einsum('btd,de->bte', hn, w_in)
    (fq, fk, fv, ff, fg, mq, mk, mv, mg, sq, sk, sv, sg, wq, wk, wv, wg) = split_columns(proj)
    log_f = jax.nn.log_sigmoid((ff + b_forget).astype(jnp.float32)).transpose(0, 2, 1)
    o_fox = forgetting_attention(rms_norm(to_heads(fq, FOX_HEADS), fox_qk_gain[0]),
                                 rms_norm(to_heads(fk, FOX_HEADS), fox_qk_gain[1]),
                                 to_heads(fv, FOX_HEADS), log_f)
    o_moba = moba_attention(rms_norm(to_heads(mq, MOBA_HEADS), moba_qk_gain[0]),
                            rms_norm(to_heads(mk, MOBA_HEADS), moba_qk_gain[1]),
                            to_heads(mv, MOBA_HEADS), rel_bias[:, :MOBA_HEADS].T)
    o_sb = stick_breaking_attention(to_heads(sq, SB_HEADS), to_heads(sk, SB_HEADS), to_heads(sv, SB_HEADS))
    o_swa = swa_sink_attention(rms_norm(to_heads(wq, SWA_HEADS), swa_qk_gain[0]),
                               rms_norm(to_heads(wk, SWA_KV_HEADS), swa_qk_gain[1]),
                               to_heads(wv, SWA_KV_HEADS), sinks, rel_bias[:, MOBA_HEADS:].T)
    y = jnp.concatenate([from_heads(o_fox) * jax.nn.silu(fg),
                         from_heads(o_moba) * jax.nn.silu(mg),
                         from_heads(o_sb) * jax.nn.silu(sg),
                         from_heads(o_swa) * jax.nn.silu(wg)], axis=-1)
    return x + jnp.einsum('bte,ed->btd', y, w_out)

def first_inputs(seed: int = 0) -> dict:
    key = jax.random.key(seed)
    ks = jax.random.split(key, 10)
    x = jax.random.normal(ks[0], (BATCH, SEQ, D_MODEL), jnp.float32)
    norm_gain = 1.0 + 0.02 * jax.random.normal(ks[1], (DEPTH, D_MODEL), jnp.float32)
    w_in = jax.random.normal(ks[2], (DEPTH, D_MODEL, IN_WIDTH), jnp.float32) * D_MODEL ** -0.5
    b_forget = FORGET_BIAS_INIT + 0.1 * jax.random.normal(ks[3], (DEPTH, FOX_HEADS), jnp.float32)
    fox_qk_gain = 1.0 + 0.02 * jax.random.normal(ks[4], (DEPTH, 2, HEAD_DIM), jnp.float32)
    moba_qk_gain = 1.0 + 0.02 * jax.random.normal(ks[5], (DEPTH, 2, HEAD_DIM), jnp.float32)
    swa_qk_gain = 1.0 + 0.02 * jax.random.normal(ks[6], (DEPTH, 2, HEAD_DIM), jnp.float32)
    sinks = 0.5 * jax.random.normal(ks[7], (DEPTH, SWA_HEADS), jnp.float32)
    w_out = jax.random.normal(ks[8], (DEPTH, MIX_WIDTH, D_MODEL), jnp.float32) * MIX_WIDTH ** -0.5
    rel_bias = 0.1 * jax.random.normal(ks[9], (NUM_BUCKETS, MOBA_HEADS + SWA_HEADS), jnp.float32)
    return {'x': x, 'norm_gain': norm_gain, 'w_in': w_in, 'b_forget': b_forget,
            'fox_qk_gain': fox_qk_gain, 'moba_qk_gain': moba_qk_gain, 'swa_qk_gain': swa_qk_gain,
            'sinks': sinks, 'w_out': w_out, 'rel_bias': rel_bias}

def first_block(x, norm_gain, w_in, b_forget, fox_qk_gain, moba_qk_gain, swa_qk_gain, sinks, w_out, rel_bias):
    for layer in range(DEPTH):
        x = hybrid_layer(x, norm_gain[layer], w_in[layer], b_forget[layer], fox_qk_gain[layer],
                         moba_qk_gain[layer], swa_qk_gain[layer], sinks[layer], w_out[layer], rel_bias)
    return x


N_NSA_HEADS = 8
N_KV_HEADS = 2
GQA_GROUP = N_NSA_HEADS // N_KV_HEADS
NSA_WIDTH = N_NSA_HEADS * HEAD_DIM
KV_WIDTH = N_KV_HEADS * HEAD_DIM
N_BRANCHES = 3
N_GATES = N_BRANCHES * N_NSA_HEADS
CMP_BLOCK = 32
CMP_STRIDE = 16
CMP_HIDDEN = 4 * HEAD_DIM
SLC_BLOCK = 64
SLC_TOPK = 16
N_LOCAL_BLOCKS = 2
WINDOW = 512
Q_BLOCK = 128
GMLP_WIDTH = D_MODEL - NSA_WIDTH
N_GMLP_GROUPS = 8
GMLP_GROUP_DIM = GMLP_WIDTH // N_GMLP_GROUPS
GMLP_CHUNK = 128
IN_WIDTH_2 = NSA_WIDTH + 6 * KV_WIDTH + N_GATES + 2 * GMLP_WIDTH
D_FF = ((8 * D_MODEL + 3 * 256 - 1) // (3 * 256)) * 256
N_BUCKETS = 32
REL_MAX_DISTANCE_2 = 128
LN_EPS = 1e-5


def rms_norm_2(x, g):
    xf = x.astype(jnp.float32)
    y = xf * lax.rsqrt(jnp.mean(xf * xf, axis=-1, keepdims=True) + RMS_EPS)
    return (y * g.astype(jnp.float32)).astype(x.dtype)

def layer_norm(x, g, b):
    xf = x.astype(jnp.float32)
    mu = jnp.mean(xf, axis=-1, keepdims=True)
    var = jnp.mean(jnp.square(xf - mu), axis=-1, keepdims=True)
    y = (xf - mu) * lax.rsqrt(var + LN_EPS)
    return (y * g.astype(jnp.float32) + b.astype(jnp.float32)).astype(x.dtype)

def t5_bucket(dist):
    n = jnp.maximum(dist, 0)
    max_exact = N_BUCKETS // 2
    nf = jnp.maximum(n, max_exact).astype(jnp.float32)
    large = max_exact + (jnp.log(nf / max_exact) / math.log(REL_MAX_DISTANCE_2 / max_exact)
                         * (N_BUCKETS - max_exact)).astype(jnp.int32)
    return jnp.where(n < max_exact, n, jnp.minimum(large, N_BUCKETS - 1))

def bias_shared(table, dist):
    b = table.astype(jnp.float32)[t5_bucket(dist)]
    return b.transpose(2, 0, 1).reshape(N_KV_HEADS, GQA_GROUP, *dist.shape)

def bias_grouped(table, dist):
    tab = table.astype(jnp.float32).reshape(N_BUCKETS, N_KV_HEADS, GQA_GROUP)
    b = jax.vmap(lambda t, d: t[d], in_axes=(1, 1), out_axes=1)(tab, t5_bucket(dist))
    return b.transpose(0, 1, 4, 2, 3)

def masked_softmax(logits, mask):
    lg = jnp.where(mask, logits.astype(jnp.float32), -jnp.inf)
    m = jnp.max(lg, axis=-1, keepdims=True)
    m = jnp.where(jnp.isfinite(m), m, 0.0)
    e = jnp.where(mask, jnp.exp(lg - m), 0.0)
    return e / jnp.maximum(jnp.sum(e, axis=-1, keepdims=True), 1e-30)

def compress_tokens(t, pos_emb, w1, w2):
    B, G, S, dh = t.shape
    r = CMP_BLOCK // CMP_STRIDE
    n_chunks = S // CMP_STRIDE
    n_cmp = n_chunks - r + 1
    chunks = t.reshape(B, G, n_chunks, CMP_STRIDE, dh)
    blocks = jnp.concatenate([chunks[:, :, i:i + n_cmp] for i in range(r)], axis=3)
    blocks = (blocks + pos_emb).reshape(B, G, n_cmp, CMP_BLOCK * dh)
    return jax.nn.gelu(blocks @ w1) @ w2

gather_blocks = jax.vmap(jax.vmap(lambda blocks, ix: blocks[ix]))

def nsa_gmlp_mixer(h, w_in, cmp_pos_k, cmp_w1_k, cmp_w2_k, cmp_pos_v, cmp_w1_v, cmp_w2_v,
                   gmlp_ln_g, gmlp_ln_b, gmlp_w_s, gmlp_b_s, w_out, rel_bias):
    B, S, _ = h.shape
    G, R, dh = N_KV_HEADS, GQA_GROUP, HEAD_DIM
    proj = jnp.einsum("bsd,de->bse", h, w_in)
    sizes = [NSA_WIDTH] + [KV_WIDTH] * 6 + [N_GATES, GMLP_WIDTH]
    points = [sum(sizes[:i + 1]) for i in range(len(sizes))]
    q, k_c, v_c, k_s, v_s, k_w, v_w, gate_logits, u, v = jnp.split(proj, points, axis=-1)

    def heads_kv(t):
        return t.reshape(B, S, G, dh).transpose(0, 2, 1, 3)

    q = q.reshape(B, S, G, R, dh).transpose(0, 2, 3, 1, 4) * (HEAD_DIM ** -0.5)
    gates = jax.nn.sigmoid(gate_logits.astype(jnp.float32)).reshape(B, S, G, R, N_BRANCHES)
    gates = gates.transpose(0, 2, 3, 1, 4)

    kc = compress_tokens(heads_kv(k_c), cmp_pos_k, cmp_w1_k, cmp_w2_k)
    vc = compress_tokens(heads_kv(v_c), cmp_pos_v, cmp_w1_v, cmp_w2_v)
    n_cmp = kc.shape[2]
    cmp_start = jnp.arange(n_cmp, dtype=jnp.int32) * CMP_STRIDE
    cmp_end = cmp_start + (CMP_BLOCK - 1)

    n_slc = S // SLC_BLOCK
    ks_blocks = heads_kv(k_s).reshape(B, G, n_slc, SLC_BLOCK, dh)
    vs_blocks = heads_kv(v_s).reshape(B, G, n_slc, SLC_BLOCK, dh)
    slc_start = jnp.arange(n_slc, dtype=jnp.int32) * SLC_BLOCK
    ov = (jnp.minimum(cmp_start[:, None] + CMP_BLOCK, slc_start[None, :] + SLC_BLOCK)
          - jnp.maximum(cmp_start[:, None], slc_start[None, :]))
    overlap = jnp.maximum(ov, 0).astype(jnp.float32) / CMP_BLOCK
    k_sel = min(SLC_TOPK, n_slc)

    pad = ((0, 0), (0, 0), (WINDOW, 0), (0, 0))
    kw_pad = jnp.pad(heads_kv(k_w), pad)
    vw_pad = jnp.pad(heads_kv(v_w), pad)

    def query_block(qi):
        s0 = qi * Q_BLOCK
        tq = s0 + jnp.arange(Q_BLOCK, dtype=jnp.int32)
        qb = lax.dynamic_slice_in_dim(q, s0, Q_BLOCK, axis=3)
        gb = lax.dynamic_slice_in_dim(gates, s0, Q_BLOCK, axis=3)

        d_c = tq[:, None] - cmp_end[None, :]
        lg_c = jnp.einsum("bgrqd,bgkd->bgrqk", qb, kc).astype(jnp.float32) + bias_shared(rel_bias, d_c)
        p_c = masked_softmax(lg_c, d_c >= 0)
        o_c = jnp.einsum("bgrqk,bgkd->bgrqd", p_c.astype(vc.dtype), vc)

        imp = jnp.einsum("bgrqk,kn->bgqn", p_c, overlap)
        jq = (tq // SLC_BLOCK)[:, None]
        blk = jnp.arange(n_slc, dtype=jnp.int32)[None, :]
        forced = (blk == 0) | ((blk <= jq) & (blk > jq - N_LOCAL_BLOCKS))
        score = jnp.where(forced, jnp.inf, jnp.where(blk <= jq, imp, -jnp.inf))
        _, idx = lax.top_k(score, k_sel)
        kb = gather_blocks(ks_blocks, idx).reshape(B, G, Q_BLOCK, k_sel * SLC_BLOCK, dh)
        vb = gather_blocks(vs_blocks, idx).reshape(B, G, Q_BLOCK, k_sel * SLC_BLOCK, dh)
        key_pos = (idx[..., None] * SLC_BLOCK + jnp.arange(SLC_BLOCK, dtype=jnp.int32)
                   ).reshape(B, G, Q_BLOCK, k_sel * SLC_BLOCK)
        d_s = tq[None, None, :, None] - key_pos
        lg_s = jnp.einsum("bgrqd,bgqkd->bgrqk", qb, kb).astype(jnp.float32) + bias_grouped(rel_bias, d_s)
        p_s = masked_softmax(lg_s, (d_s >= 0)[:, :, None])
        o_s = jnp.einsum("bgrqk,bgqkd->bgrqd", p_s.astype(vb.dtype), vb)

        kwb = lax.dynamic_slice_in_dim(kw_pad, s0, WINDOW + Q_BLOCK, axis=2)
        vwb = lax.dynamic_slice_in_dim(vw_pad, s0, WINDOW + Q_BLOCK, axis=2)
        kpos = s0 - WINDOW + jnp.arange(WINDOW + Q_BLOCK, dtype=jnp.int32)
        d_w = tq[:, None] - kpos[None, :]
        mask_w = (d_w >= 0) & (d_w < WINDOW) & (kpos[None, :] >= 0)
        lg_w = jnp.einsum("bgrqd,bgkd->bgrqk", qb, kwb).astype(jnp.float32) + bias_shared(rel_bias, d_w)
        p_w = masked_softmax(lg_w, mask_w)
        o_w = jnp.einsum("bgrqk,bgkd->bgrqd", p_w.astype(vwb.dtype), vwb)

        o = gb[..., 0:1] * o_c + gb[..., 1:2] * o_s + gb[..., 2:3] * o_w
        return o.astype(h.dtype)

    o = lax.map(query_block, jnp.arange(S // Q_BLOCK, dtype=jnp.int32))
    nsa_out = o.transpose(1, 0, 4, 2, 3, 5).reshape(B, S, NSA_WIDTH)

    z_u = jax.nn.gelu(u)
    z_v = layer_norm(jax.nn.gelu(v), gmlp_ln_g, gmlp_ln_b)
    n_chunks = S // GMLP_CHUNK
    zv = z_v.reshape(B, n_chunks, GMLP_CHUNK, N_GMLP_GROUPS, GMLP_GROUP_DIM)
    causal = jnp.tril(jnp.ones((GMLP_CHUNK, GMLP_CHUNK), dtype=bool))
    w_s = jnp.where(causal, gmlp_w_s, 0.0).astype(zv.dtype)
    sv = jnp.einsum("gts,bnsgd->bntgd", w_s, zv) + gmlp_b_s.T[None, None, :, :, None]
    gm = (z_u.reshape(B, n_chunks, GMLP_CHUNK, N_GMLP_GROUPS, GMLP_GROUP_DIM) * sv).reshape(B, S, GMLP_WIDTH)

    mixed = jnp.concatenate([nsa_out, gm.astype(h.dtype)], axis=-1)
    return jnp.einsum("bse,ed->bsd", mixed, w_out)

def swiglu_ffn(h, w_gate_up, w_down):
    gate, up = jnp.split(jnp.einsum("bsd,df->bsf", h, w_gate_up), 2, axis=-1)
    return jnp.einsum("bsf,fd->bsd", jax.nn.silu(gate) * up, w_down)

def second_inputs(seed: int = 0) -> dict:
    key = jax.random.key(seed)
    ks = jax.random.split(key, 20)
    f32 = jnp.float32
    L = DEPTH

    def nrm(k, shape, scale):
        return jax.random.normal(k, shape, f32) * scale

    def gain(k, shape):
        return 1.0 + 0.05 * jax.random.normal(k, shape, f32)

    return {
        "x": nrm(ks[0], (BATCH, SEQ, D_MODEL), 1.0),
        "rel_bias": nrm(ks[1], (N_BUCKETS, N_NSA_HEADS), 0.5),
        "norm_mix_pre": gain(ks[2], (L, D_MODEL)),
        "norm_mix_post": gain(ks[3], (L, D_MODEL)),
        "norm_ffn_pre": gain(ks[4], (L, D_MODEL)),
        "norm_ffn_post": gain(ks[5], (L, D_MODEL)),
        "w_in": nrm(ks[6], (L, D_MODEL, IN_WIDTH_2), D_MODEL ** -0.5),
        "cmp_pos_k": nrm(ks[7], (L, CMP_BLOCK, HEAD_DIM), 0.1),
        "cmp_w1_k": nrm(ks[8], (L, CMP_BLOCK * HEAD_DIM, CMP_HIDDEN), (CMP_BLOCK * HEAD_DIM) ** -0.5),
        "cmp_w2_k": nrm(ks[9], (L, CMP_HIDDEN, HEAD_DIM), CMP_HIDDEN ** -0.5),
        "cmp_pos_v": nrm(ks[10], (L, CMP_BLOCK, HEAD_DIM), 0.1),
        "cmp_w1_v": nrm(ks[11], (L, CMP_BLOCK * HEAD_DIM, CMP_HIDDEN), (CMP_BLOCK * HEAD_DIM) ** -0.5),
        "cmp_w2_v": nrm(ks[12], (L, CMP_HIDDEN, HEAD_DIM), CMP_HIDDEN ** -0.5),
        "gmlp_ln_g": gain(ks[13], (L, GMLP_WIDTH)),
        "gmlp_ln_b": nrm(ks[14], (L, GMLP_WIDTH), 0.02),
        "gmlp_w_s": nrm(ks[15], (L, N_GMLP_GROUPS, GMLP_CHUNK, GMLP_CHUNK), GMLP_CHUNK ** -0.5),
        "gmlp_b_s": gain(ks[16], (L, N_GMLP_GROUPS, GMLP_CHUNK)),
        "w_out": nrm(ks[17], (L, D_MODEL, D_MODEL), D_MODEL ** -0.5),
        "w_gate_up": nrm(ks[18], (L, D_MODEL, 2 * D_FF), D_MODEL ** -0.5),
        "w_down": nrm(ks[19], (L, D_FF, D_MODEL), D_FF ** -0.5),
    }

def second_block(x, rel_bias, norm_mix_pre, norm_mix_post, norm_ffn_pre, norm_ffn_post, w_in,
              cmp_pos_k, cmp_w1_k, cmp_w2_k, cmp_pos_v, cmp_w1_v, cmp_w2_v,
              gmlp_ln_g, gmlp_ln_b, gmlp_w_s, gmlp_b_s, w_out, w_gate_up, w_down):
    h = x
    for l in range(DEPTH):
        mix = nsa_gmlp_mixer(rms_norm_2(h, norm_mix_pre[l]), w_in[l],
                             cmp_pos_k[l], cmp_w1_k[l], cmp_w2_k[l],
                             cmp_pos_v[l], cmp_w1_v[l], cmp_w2_v[l],
                             gmlp_ln_g[l], gmlp_ln_b[l], gmlp_w_s[l], gmlp_b_s[l],
                             w_out[l], rel_bias)
        h = h + rms_norm_2(mix, norm_mix_post[l])
        ffn = swiglu_ffn(rms_norm_2(h, norm_ffn_pre[l]), w_gate_up[l], w_down[l])
        h = h + rms_norm_2(ffn, norm_ffn_post[l])
    return h


def setup_inputs(seed=0):
    out = dict(first_inputs(seed))
    for name, value in second_inputs(seed + 1).items():
        if name != "x":
            out[name + "_2"] = value
    return out


def reference(
    x, norm_gain, w_in, b_forget, fox_qk_gain, moba_qk_gain, swa_qk_gain, sinks, w_out,
    rel_bias, rel_bias_2, norm_mix_pre_2, norm_mix_post_2, norm_ffn_pre_2, norm_ffn_post_2,
    w_in_2, cmp_pos_k_2, cmp_w1_k_2, cmp_w2_k_2, cmp_pos_v_2, cmp_w1_v_2, cmp_w2_v_2,
    gmlp_ln_g_2, gmlp_ln_b_2, gmlp_w_s_2, gmlp_b_s_2, w_out_2, w_gate_up_2, w_down_2,
):
    x = first_block(
        x, norm_gain, w_in, b_forget, fox_qk_gain, moba_qk_gain, swa_qk_gain, sinks, w_out,
        rel_bias,
    )
    return second_block(
        x, rel_bias_2, norm_mix_pre_2, norm_mix_post_2, norm_ffn_pre_2, norm_ffn_post_2, w_in_2,
        cmp_pos_k_2, cmp_w1_k_2, cmp_w2_k_2, cmp_pos_v_2, cmp_w1_v_2, cmp_w2_v_2, gmlp_ln_g_2,
        gmlp_ln_b_2, gmlp_w_s_2, gmlp_b_s_2, w_out_2, w_gate_up_2, w_down_2,
    )


_drawn_inputs = setup_inputs


def setup_inputs(seed=0):
    import zlib

    import numpy as np

    out = dict(_drawn_inputs(seed))
    spreads = {}
    factors = {'norm_gain': 5.256,
     'b_forget': 5.201,
     'fox_qk_gain': 8.0,
     'moba_qk_gain': 8.0,
     'swa_qk_gain': 8.0,
     'sinks': 64.0,
     'rel_bias': 6.99,
     'cmp_pos_k_2': 64.0,
     'gmlp_ln_b_2': 200.0,
     'rel_bias_2': 39.853,
     'norm_mix_pre_2': 8.0,
     'norm_mix_post_2': 21.85,
     'norm_ffn_pre_2': 8.0,
     'norm_ffn_post_2': 25.487,
     'cmp_w1_k_2': 8.0,
     'cmp_w2_k_2': 8.0,
     'cmp_pos_v_2': 8.0,
     'cmp_w1_v_2': 7.229,
     'cmp_w2_v_2': 4.146,
     'gmlp_ln_g_2': 64.0,
     'gmlp_b_s_2': 53.232}
    for name, (base, spread) in spreads.items():
        noise = np.random.default_rng([zlib.crc32(name.encode()), seed]).standard_normal(out[name].shape)
        drawn = base * np.exp(spread * noise) if base else spread * noise
        out[name] = jnp.asarray(drawn.astype(out[name].dtype))
    for name, factor in factors.items():
        out[name] = (out[name] * factor).astype(out[name].dtype)
    return out
```

```python
from contextlib import ExitStack

import numpy as np

import concourse.bass as bass
from concourse import mybir

F32 = mybir.dt.float32
F32R = mybir.dt.float32r
BF16 = mybir.dt.bfloat16
ALU = mybir.AluOpType
ACT = mybir.ActivationFunctionType
AX = mybir.AxisListType

P = 128
SEQ = 512
D = 1024
NT = SEQ // P
KD = D // P
HD = 64
EPS = 1e-6
LN_EPS = 1e-5
MASK = -1e30
FLOOR = -1e29
QSCALE = HD ** -0.5
FF = 2816
NCMP = 31
RING = 6

FQ, FV, FG = 0, 512, 772
MQ, MV, MG = 1028, 1540, 1796
SQ_, SV, SG_ = 2052, 2564, 2820
WQ, WG = 3076, 3588
CHUNKS1 = [
    [(FQ, 512)],
    [(FV, 260)],
    [(MQ, 512)],
    [(MV, 256), (SV, 256)],
    [(SQ_, 512)],
    [(WQ, 512)],
    [(MG, 256), (SG_, 256)],
    [(WG, 256), (FG, 256)],
]
CHUNKS2 = [[(512, 512)], [(0, 512)], [(1024, 280)], [(1304, 512)], [(1816, 512)]]
W_OUT = [[(0, 512)], [(512, 512)]]
GU_CHUNKS = FF // 256
DOWN_TILES = FF // P

FULL = [[(3, 0, 4)], [(2, 0, 3), (0, 0, 1)], [(1, 0, 2)]]
BAND = [[(1, 0, 2), (2, 1, 2)], [(3, 2, 2), (0, 0, 1)]]
KEYS = [[0], [1, 3], [2]]
KEY_COLS = {0: 0, 1: 512, 3: 896, 2: 1024}
POS = {3: 0, 2: 1, 0: 2, 1: 3}


def rel_bucket_of(dist, max_distance):
    half = 16
    d = np.maximum(dist, 0)
    ratio = np.log(np.maximum(d, half).astype(np.float32) / np.float32(half)).astype(np.float32)
    large = half + (ratio / np.float32(np.log(max_distance / half)) * np.float32(half)).astype(np.int32)
    return np.where(d < half, d, np.minimum(large, 31))


def one_hot(dist, valid, max_distance):
    out = np.zeros((33, len(dist)), np.float32)
    b = rel_bucket_of(dist, max_distance)
    out[b[valid], np.nonzero(valid)[0]] = 1.0
    out[32, ~valid] = MASK
    return out


def constants():
    i = np.arange(P)
    tri = (i[:, None] <= i[None, :]).astype(np.float32)
    d_full = 511 - np.arange(640)
    d_band = 255 - np.arange(384)
    d_cmp = np.arange(1024) - 511
    return {
        "ident": np.eye(P, dtype=np.float32),
        "tri_ones": np.concatenate([tri, np.ones((P, 384), np.float32)], 1),
        "suffix": np.ascontiguousarray(tri.T),
        "causal": np.where(i[None, :] > i[:, None], np.float32(MASK), np.float32(0)),
        "strict": np.where(i[:, None] >= i[None, :], np.float32(MASK), np.float32(0)),
        "hot_full": one_hot(d_full, d_full >= 0, 1024),
        "hot_band": one_hot(d_band, (d_band >= 0) & (d_band < 128), 1024),
        "hot_t5": one_hot(d_full, d_full >= 0, 128),
        "hot_cmp": one_hot(d_cmp, d_cmp >= 0, 128),
    }


def slots_and_groups():
    groups, first = [], {}
    s = 0
    for phase, chunks in (("in1", CHUNKS1), ("out1", W_OUT), ("in2", CHUNKS2), ("out2", W_OUT)):
        for c, cols in enumerate(chunks):
            first[phase, c] = s
            for part in range(2):
                groups.append((phase, c, part, s, sum(w for _, w in cols)))
                s += 4
    for c in range(GU_CHUNKS):
        first["gu", c] = s
        for part in range(2):
            groups.append(("gu", c, part, s, 512))
            s += 4
    for g in range(DOWN_TILES // 2):
        first["down", 2 * g] = s
        first["down", 2 * g + 1] = s + 2
        groups.append(("down", g, 0, s, 512))
        s += 4
    return groups, first, s


def make_timeline(first, n_slots):
    tl = []

    def hi_lo(s):
        if s + 4 < n_slots:
            tl.append(("split", s + 4))

    def mm(phase, c, k, per=1):
        s = first[phase, c] + k * per
        for j in range(per):
            hi_lo(s + j)
        tl.append(("mm", phase, c, k))

    def transposed(phase):
        for t in range(NT):
            if phase != "out2":
                tl.append(("pre", phase, t))
            tl.append(("xt", phase, t, 0))
            tl.append(("xt", phase, t, 1))

    queue = {n: [] for n in range(200)}
    order = []

    def at(tick, *steps):
        queue[tick] += list(steps)

    def softmax_head(tick, name, h, plan, lag_t=1, lag_o=2):
        for g in range(len(plan)):
            at(tick + g, ("S", name, h, g))
            at(tick + g + lag_t, ("T", name, h, g))
            at(tick + g + lag_o, ("O", name, h, g))

    for t in range(NT):
        at(9 + t, ("qn", "fox", t), ("qt", "fox", t))
    at(16, ("logf",))
    for h in range(4):
        at(16 + h, ("C", h))
    for t in range(NT):
        at(25 + t, ("qn", "moba", t), ("qt", "moba", t))
        at(41 + t, ("qt", "sb", t))
        at(49 + t, ("qn", "swa", t), ("qt", "swa", t))
    for h in range(4):
        softmax_head(17 + 3 * h, "fox", h, FULL)
        softmax_head(30 + 3 * h, "moba", h, FULL)
        a = 45 + 3 * h
        for g in range(3):
            at(a + g, ("Z", h, g))
            at(a + g + 4, ("F", h, g))
        at(a + 2, ("sp", h))
        at(a + 7, ("OS", h))
        softmax_head(61 + 2 * h, "swa", h, BAND)
    rank = {"OS": 0, "O": 0, "T": 1, "F": 2, "S": 3, "Z": 3, "sp": 4, "qn": -2, "qt": -1, "logf": -4, "C": -3}

    def flush(tick):
        tl.extend(sorted(queue[tick], key=lambda x: rank[x[0]]))
        queue[tick] = []

    for s in range(4):
        tl.append(("split", s))
    transposed("in1")
    for c in range(len(CHUNKS1)):
        for k in range(KD):
            flush(8 * c + k)
            mm("in1", c, k)
        tl.append(("ev", "in1", c))
    for tick in range(64, 200):
        flush(tick)
    transposed("out1")
    for c in range(2):
        for k in range(KD):
            mm("out1", c, k)
        tl.append(("ev", "out1", c))

    transposed("in2")
    for t in range(NT):
        at(8 + t, ("qt", "cmp", t), ("qt", "slc", t))
        at(16 + t, ("qt", "q", t))
        at(24 + t, ("qt", "win", t))
    at(13, ("blocks",))
    at(15, ("hidden", 0))
    at(20, ("hidden", 1))
    at(21, ("cmpkv",))
    at(24, ("gates",))
    rank.update({"blocks": 5, "hidden": 6, "cmpkv": 7, "gates": -5, "CS": 3, "CT": 1, "CO": 0})
    for i in range(NT):
        at(25 + i, ("CS", i))
        at(26 + i, ("CT", i))
        at(27 + i, ("CO", i))
    for h in range(16):
        softmax_head(29 + 3 * h, "slc" if h < 8 else "win", h % 8, FULL)
    rank.update({"gm_w": 8, "gm_n": 8, "gm": 8})
    at(42, ("gm_w", 0))
    at(43, ("gm_w", 1))
    for t in range(NT):
        at(44 + t, ("gm_n", t))
    for u in range(4):
        at(49 + u, ("gm", u))
    for c in range(len(CHUNKS2)):
        for k in range(KD):
            flush(8 * c + k)
            mm("in2", c, k)
        tl.append(("ev", "in2", c))
    for tick in range(40, 200):
        flush(tick)
    transposed("out2")
    for c in range(2):
        for k in range(KD):
            mm("out2", c, k)
        tl.append(("ev", "out2", c))
    for t in range(NT):
        tl.append(("post", "mix", t))
    transposed("gu")
    for c in range(GU_CHUNKS):
        for k in range(KD):
            mm("gu", c, k)
        tl.append(("ev", "gu", c))
    for kt in range(DOWN_TILES):
        if kt < 2:
            tl.append(("act", kt))
    for kt in range(DOWN_TILES):
        if kt + 2 < DOWN_TILES:
            tl.append(("act", kt + 2))
        mm("down", kt, 0, 2)
    for t in range(NT):
        tl.append(("ev", "down", t))
    for t in range(NT):
        tl.append(("post", "ffn", t))
    return tl


def hybrid_two_block_kernel(nc, a, c, out):
    groups, first, n_slots = slots_and_groups()
    timeline = make_timeline(first, n_slots)

    nth, seen = {}, {}

    def kind(step):
        k = step[0]
        return {"S": "sc", "Z": "sc", "C": "sc", "CS": "sc", "hidden": "sc", "gm": "sc", "cmpkv": "sc",
                "T": "tr", "F": "tr", "CT": "tr", "qt": "tr", "gm_w": "tr",
                "OS": "o", "O": "o", "CO": "o"}.get(k, k)

    for step in timeline:
        nth[step] = seen.get(kind(step), 0)
        seen[kind(step)] = nth[step] + 1

    with ExitStack() as ctx:
        def sem(name):
            return ctx.enter_context(nc.semaphore(name))

        BASE = 16512

        def at(name, kb, shape, dtype=F32):
            return nc.alloc_sbuf_tensor_at(name, [P] + shape, dtype, offset=BASE + int(kb * 1024))

        XT = at("XT", 0, [KD, 2, SEQ], F32R)
        WR = at("WR", 32, [RING, 2, 512], F32R)
        RAW = at("RAW", 56, [2, 4, 512])
        R1 = at("R1", 72, [NT, D])
        R2 = at("R2", 88, [NT, D])
        ident = at("ident_sb", 104, [P])
        identb = at("identb", 104.5, [P], BF16)
        causal = at("causal_sb", 104.75, [P], BF16)
        strict = at("strict_sb", 105, [P], BF16)
        tri = at("tri_sb", 105.25, [512])
        suffix = at("suffix_sb", 107.25, [P])
        gain = [at("gain0", 107.75, [D]), at("gain1", 111.75, [D])]
        sq = at("sq", 115.75, [512])
        st = at("st", 117.75, [576])
        cmp_bias = at("cmp_bias", 120, [NT, 8, 32])
        prob = at("prob", 124, [2, 1280])
        probT = at("probT", 134, [1280])
        V1 = at("V1", 139, [NT, 896])
        qk_nat = at("qk_nat", 153, [NT, 512])
        qkT1 = at("qkT1", 161, [2, 4, SEQ])
        bias_moba = at("bias_moba", 177, [4, 512])
        bias_swa = at("bias_swa", 185, [4, 256])
        fox_c = at("fox_c", 189, [4, 512])
        soft = at("soft", 189, [2, 1280])
        x_again = at("x_again", 161, [NT, D])
        hots = at("hots", 161, [2688])
        rows = at("rows", 199, [1664])
        stage = at("stage", 199, [384])
        V2 = at("V2", 139, [NT, 2, P])
        nat2 = at("nat2", 143, [NT, 512])
        cmp_nat = at("cmp_nat", 151, [NT, 4, P])
        zv = at("zv", 151, [NT, 512])
        hidT = at("hidT", 151, [2, 2, 64])
        hidV = at("hidV", 152, [2, 2, P])
        w1 = at("w1", 159, [16, 256])
        qT2 = at("qT2", 175, [4, SEQ])
        kT2 = at("kT2", 183, [2, 2, SEQ])
        bias_t5 = at("bias_t5", 191, [8, 512])
        cmpT = at("cmpT", 72, [2, 2, SEQ])
        blocks = at("blocks", 80, [2, 16, 64])
        vbd = at("vbd", 111.75, [2, 4, HD])
        w2k = at("w2k", 113.75, [2, P])
        w2v = at("w2v", 114.75, [2, HD])
        kcT = at("kcT", 115.25, [2, 2, 32])
        ws_nat = at("ws_nat", 0, [8, P])
        wsT = at("wsT", 4, [8, P])
        ln_g = at("ln_g", 8, [512])
        ln_b = at("ln_b", 10, [512])
        gated = at("gated", 120, [2, 512])
        actT = at("actT", 124, [DOWN_TILES, SEQ])

        half = st[:, 0:4]
        qk_gain = st[:, 4:10]
        pos = st[:, 10:42]
        gmlp_b = st[:, 42:50]
        b_forget = st[:, 50:54]
        sinks = st[:, 54:58]
        ss = st[:, 58:62]
        rr = st[:, 62:66]
        ms8 = st[:, 66:74]
        rr8 = st[:, 74:82]
        lf = st[:, 82:98]
        lf_a = st[:, 98:114]
        lf_u = st[:, 114:130]
        mx = st[:, 130:146]
        nm = st[:, 146:162]
        sm = st[:, 162:178]
        es = st[:, 178:194]
        ri = st[:, 194:210]
        gates = st[:, 210:306]
        g_tmp = st[:, 306:402]
        cm8 = st[:, 402:410]
        cs8 = st[:, 410:418]
        cf8 = st[:, 418:450]
        tab1 = st[:, 450:458]
        tab2 = st[:, 458:466]
        negmu = st[:, 466:470]

        psum = ctx.enter_context(nc.psum_tensor("psum", [P, 8, 512], F32))
        MM = [psum[:, i, :] for i in range(4)]
        SC = [psum[:, 4, :], psum[:, 5, :]]
        TR = psum[:, 6, :]
        OB = psum[:, 7, :]
        SET = [[psum[:, i, :] for i in range(4)], [psum[:, 4 + i, :] for i in range(4)]]

        rows_d = nc.dram_tensor("rows_scratch", [20, 640], F32, kind="Internal").ap()
        rep_d = nc.dram_tensor("rep_scratch", [20, P, 640], F32, kind="Internal").ap()
        repb_d = nc.dram_tensor("repb_scratch", [4, P, 384], F32, kind="Internal").ap()

        s_x = [sem(f"x_landed{t}") for t in range(NT)]
        s_gain = sem("gain_landed")
        s_const = sem("consts_landed")
        s_tab = sem("tables_landed")
        s_raw = [sem("raw_landed0"), sem("raw_landed1")]
        s_rows = sem("rows_stored")
        s_rep = sem("rows_replicated")
        s_bias1 = sem("bias1_landed")
        s_bias2 = sem("bias2_landed")
        s_xa = sem("x_again_landed")
        s_w1 = sem("w1_landed")
        s_small2 = sem("small2_landed")
        s_gm_in = sem("gmlp_in_landed")
        s_out = sem("out_stored")
        w_hi = sem("w_hi")
        w_lo = sem("w_lo")
        w_used = sem("w_used")
        s_ident = sem("ident_landed")
        ev_act = sem("ev_act")
        ev_dve = sem("ev_dve")
        v_chain = sem("dve_chain")
        a_chain = sem("act_chain")
        p_chain = sem("pool_chain")
        ms_ready = sem("mean_square_ready")
        r_ready = sem("rsqrt_ready")
        pre_done = sem("pre_done")
        xt_in = sem("xt_transposed")
        xt_hi = sem("xt_hi")
        xt_lo = sem("xt_lo")
        qn_done = sem("qn_done")
        sc_in = sem("scores_in_psum")
        sc_out = sem("scores_out_of_psum")
        tr_in = sem("transposes_in_psum")
        tr_out = sem("transposes_out_of_psum")
        o_in = sem("o_in_psum")
        o_out = sem("o_out_of_psum")
        e_done = sem("exp_done")
        lf_pre = sem("logf_abs")
        lf_act = sem("logf_ln")
        lf_done = sem("logf_done")
        sp_abs = sem("sp_abs")
        sp_ln = sem("sp_ln")
        sp_done = sem("sp_done")
        w_sub = sem("sb_weights_sub")
        a_done = sem("sb_weights_exp")
        tab_done = sem("tables_in_psum")
        tab_out = sem("tables_out")
        setup_dve = sem("setup_dve")
        blk_done = sem("blocks_done")
        hid_act = sem("hidden_gelu")
        hid_rep = sem("hidden_replicated")
        gate_e = sem("gate_exp")
        cs_sub = sem("cmp_sub")
        cs_exp = sem("cmp_exp")
        gm_w = sem("gm_weights_ready")
        gm_n = sem("gm_norm_ready")
        act_hi = sem("act_hi")
        act_lo = sem("act_lo")
        gs_done = sem("gate_silu")
        post_done = sem("post_done")

        def group_cols(phase, chunk):
            return {"in1": CHUNKS1, "out1": W_OUT, "in2": CHUNKS2, "out2": W_OUT}[phase][chunk]

        weights = {"in1": a["w_in"], "out1": a["w_out"], "in2": a["w_in_2"], "out2": a["w_out_2"],
                   "gu": a["w_gate_up_2"], "down": a["w_down_2"]}

        def evac_engine(phase, chunk, t):
            if (phase, chunk) in (("in1", 6), ("in1", 7), ("in2", 3), ("in2", 4)):
                return "act"
            if phase in ("out1",):
                return "dve"
            if phase == "down":
                return "act" if t % 2 == 0 else "dve"
            return "act" if t % 2 == 0 else "dve"

        ev_count = {}
        n_act = n_dve = 0
        for step in timeline:
            if step[0] == "ev" and step[1] != "down":
                if step[1] == "gu":
                    n_dve += 1
                else:
                    for t in range(NT):
                        if evac_engine(step[1], step[2], t) == "act":
                            n_act += 1
                        else:
                            n_dve += 1
                ev_count[step] = (n_act, n_dve)

        def wait_evacuated(eng, step):
            eng.wait_ge(ev_act, ev_count[step][0])
            eng.wait_ge(ev_dve, ev_count[step][1])

        HEADS = {"fox": (FULL, 4), "moba": (FULL, 4), "swa": (BAND, 4), "slc": (FULL, 8), "win": (FULL, 8)}

        def prev_head(name, h):
            if h:
                return (name, h - 1)
            return {"fox": None, "moba": ("fox", 3), "swa": ("sb", 3), "slc": ("cmp", 3), "win": ("slc", 7)}[name]

        def last_o(head):
            name, h = head
            if name == "sb":
                return ("OS", h)
            if name == "cmp":
                return ("CO", h)
            return ("O", name, h, len(HEADS[name][0]) - 1)

        def head_index(name, h):
            return {"fox": 0, "moba": 4, "swa": 12, "slc": 0, "win": 8}[name] + h

        def segments(plan, g):
            col = 0
            n = sum(len(x) for x in plan[:g])
            for i, j, m in plan[g]:
                yield i, j, m, col, n
                col += m * P
                n += 1

        def width(plan, g):
            return P * sum(m for _, _, m in plan[g])

        GROUP_AT = [0, 512, 1024]
        KINDS1 = {"fox": 0, "moba": 1, "sb": 2, "swa": 3}

        def q_of(name, h):
            e = 64 * (h % 2)
            if name in KINDS1:
                return qkT1[e:e + 64, KINDS1[name] % 2, h // 2, :]
            return qT2[e:e + 64, h // 2, :]

        def k_of(name, h):
            e = 64 * (h % 2)
            if name in KINDS1:
                return qkT1[e:e + 64, KINDS1[name] % 2, 2 + h // 2, :]
            return kT2[e:e + 64, 0 if name == "slc" else 1, h // 4, :]

        def v_of(name, h, j):
            if name == "swa":
                return V1[:, j, 768 + HD * (h // 2):768 + HD * (h // 2) + HD]
            if name in KINDS1:
                at_ = 256 * KINDS1[name] + HD * h
                return V1[:, j, at_:at_ + HD]
            return V2[:, j, 0 if name == "slc" else 1, HD * (h // 4):HD * (h // 4) + HD]

        def bias_of(name, h, i, m):
            if name == "fox":
                return fox_c[:, h, 0:m * P]
            if name == "moba":
                return bias_moba[:, h, 384 - P * i:512]
            if name == "swa":
                return bias_swa[:, h, 256 - m * P:256]
            return bias_t5[:, h, 384 - P * i:512]

        def q_ready(name):
            return {"slc": ("qt", "q", 3), "win": ("qt", "win", 3)}.get(name, ("qt", name, 3))

        e_index = {}
        for step in timeline:
            if step[0] == "S":
                e_index[step[1:]] = len(e_index) + 1

        def evacuate(eng, phase, ch, t):
            act_ = eng is nc.scalar
            copy = (lambda o, i: eng.activation(o, i, ACT.Copy)) if act_ else (lambda o, i: eng.tensor_copy(o, i))
            m = MM[t]
            if phase == "in1":
                if ch in (0, 2, 4):
                    yield copy(qk_nat[:, t, :], m)
                elif ch == 1:
                    yield copy(V1[:, t, 0:256], m[:, 0:256])
                    yield copy(lf_u[:, 4 * t:4 * t + 4], m[:, 256:260])
                elif ch == 3:
                    yield copy(V1[:, t, 256:768], m)
                elif ch == 5:
                    yield copy(qk_nat[:, t, 0:256], m[:, 0:256])
                    for e in range(2):
                        yield copy(qk_nat[:, t, 256:512].rearrange("p (g e d) -> p g e d", g=2, e=2)[:, :, e, :],
                                   m[:, 256:384].rearrange("p (g d) -> p g d", g=2))
                    yield copy(V1[:, t, 768:896], m[:, 384:512])
                elif ch == 6:
                    yield eng.activation(R1[:, t, 256:768], m, ACT.Silu)
                elif ch == 7:
                    yield eng.activation(R1[:, t, 768:1024], m[:, 0:256], ACT.Silu)
                    yield eng.activation(R1[:, t, 0:256], m[:, 256:512], ACT.Silu)
            elif phase == "in2":
                if ch == 0:
                    for e in range(2):
                        yield copy(cmp_nat[:, t, :, HD * e:HD * e + HD], m[:, 0:256].rearrange("p (g d) -> p g d", g=4))
                        yield copy(nat2[:, t, 0:256].rearrange("p (g e d) -> p g e d", g=2, e=2)[:, :, e, :],
                                   m[:, 256:384].rearrange("p (g d) -> p g d", g=2))
                    yield copy(V2[:, t, 0, :], m[:, 384:512])
                elif ch == 1:
                    yield copy(nat2[:, t, :], m)
                elif ch == 2:
                    for e in range(2):
                        yield copy(nat2[:, t, 0:256].rearrange("p (g e d) -> p g e d", g=2, e=2)[:, :, e, :],
                                   m[:, 0:128].rearrange("p (g d) -> p g d", g=2))
                    yield copy(V2[:, t, 1, :], m[:, 128:256])
                    yield copy(g_tmp.rearrange("p (c q) -> p c q", q=4)[:, :, POS[t]], m[:, 256:280])
                elif ch == 3:
                    yield eng.activation(R1[:, t, 512:1024], m, ACT.Gelu_apprx_tanh)
                elif ch == 4:
                    yield eng.activation(zv[:, t, :], m, ACT.Gelu_apprx_tanh)
            elif phase == "out2":
                yield copy(R1[:, t, 512 * ch:512 * ch + 512], m)

        o_heads = {}
        n_heads = 0
        for step in timeline:
            if step[0] in ("O", "OS", "CO") and (step[0] != "O" or step == last_o((step[1], step[2]))):
                n_heads += 1
            o_heads[step] = n_heads

        o_total1 = o_heads[last_o(("swa", 3))]

        block = ctx.enter_context(nc.Block())

        @block.sync
        def _(sp):
            def bcast(dst, src, n):
                return sp.dma_start(dst, src.rearrange("o n -> o n").broadcast_to([P, n]))

            x_v = a["x"].rearrange("o (t p) d -> p (o t) d", p=P)
            for t in range(NT):
                sp.dma_start(R1[:, t, :], x_v[:, t, :]).then_inc(s_x[t], 16)
                if t == 0:
                    bcast(gain[0][:, :], a["norm_gain"], D).then_inc(s_gain, 16)
                    sp.dma_start(ident[:, :], c["ident"]).then_inc(s_ident, 16)
            raw_count = [0, 0]

            def load_group(g):
                phase, chunk, part, s0, w = groups[g]
                if g >= 2:
                    sp.wait_ge(w_lo, groups[g - 2][3] + 4)
                W = weights[phase]
                dst = RAW[:, g % 2, :, :]
                if phase == "down":
                    src = W[0, 256 * chunk:256 * chunk + 256, :].rearrange("(k p) (h n) -> p k h n", p=P, h=2)
                    sp.dma_start(dst.rearrange("p (k h) n -> p k h n", h=2), src).then_inc(s_raw[g % 2], 16)
                    raw_count[g % 2] += 16
                    return
                kk = W[0, 512 * part:512 * part + 512, :].rearrange("(k p) n -> p k n", p=P)
                cols = group_cols(phase, chunk) if phase != "gu" else [(256 * chunk, 256), (FF + 256 * chunk, 256)]
                col = 0
                for start, n in cols:
                    sp.dma_start(dst[:, :, col:col + n], kk[:, :, start:start + n]).then_inc(s_raw[g % 2], 16)
                    raw_count[g % 2] += 16
                    col += n

            def small_loads():
                sp.dma_start(tab1[0:32, :], a["rel_bias"]).then_inc(s_tab, 16)
                sp.dma_start(tab2[0:32, :], a["rel_bias_2"]).then_inc(s_tab, 16)
                for name, lo, n in (("hot_full", 0, 640), ("hot_band", 640, 384), ("hot_t5", 1024, 640), ("hot_cmp", 1664, 1024)):
                    sp.dma_start(hots[0:33, lo:lo + n], c[name]).then_inc(s_tab, 16)
                sp.dma_start(tri[:, :], c["tri_ones"]).then_inc(s_const, 16)
                sp.dma_start(suffix[:, :], c["suffix"]).then_inc(s_const, 16)
                sp.dma_start(stage[:, 0:128], c["causal"]).then_inc(s_const, 16)
                sp.dma_start(stage[:, 128:256], c["strict"]).then_inc(s_const, 16)
                with nc.allow_non_contiguous_dma(reason="gains as columns: a few hundred words, once"):
                    for n, name in enumerate(("fox_qk_gain", "moba_qk_gain", "swa_qk_gain")):
                        for e in range(2):
                            sp.dma_start(qk_gain[64 * e:64 * e + 64, 2 * n:2 * n + 2],
                                         a[name].rearrange("o j d -> d (o j)")).then_inc(s_const, 16)
                bcast(b_forget, a["b_forget"], 4).then_inc(s_const, 16)
                bcast(sinks, a["sinks"], 4).then_inc(s_const, 16)

            def store_rows():
                sp.wait_ge(tab_out, 5)
                sp.dma_start(rows_d[0:4, 0:640], rows[0:4, 0:640]).then_inc(s_rows, 16)
                sp.dma_start(rows_d[4:8, 0:384], rows[4:8, 640:1024]).then_inc(s_rows, 16)
                sp.dma_start(rows_d[8:16, 0:640], rows[0:8, 1024:1664]).then_inc(s_rows, 16)
                sp.wait_ge(s_rows, 48)
                for lo, n in ((0, 4), (8, 8)):
                    for h in range(lo, lo + n):
                        sp.dma_start(rep_d[h], rows_d[h:h + 1, :].broadcast_to([P, 640])).then_inc(s_rep, 16)
                for h in range(4):
                    sp.dma_start(repb_d[h], rows_d[4 + h:5 + h, 0:384].broadcast_to([P, 384])).then_inc(s_rep, 16)

            def skewed(dst, rep, h, n, pitch):
                return sp.dma_start(dst, bass.AP(rep.tensor, h * P * pitch + P - 1, [[pitch - 1, P], [1, n]]))

            def load_bias1():
                sp.wait_ge(s_rep, 16 * 16)
                for h in range(4):
                    skewed(bias_moba[:, h, :], rep_d, h, 512, 640).then_inc(s_bias1, 16)
                for h in range(4):
                    skewed(bias_swa[:, h, :], repb_d, h, 256, 384).then_inc(s_bias1, 16)

            def load_bias2():
                sp.wait_ge(tr_in, nth["F", 3, 2] + 1)
                sp.wait_ge(sp_done, 4)
                for h in range(8):
                    skewed(bias_t5[:, h, :], rep_d, 8 + h, 512, 640).then_inc(s_bias2, 16)

            def load_x_again():
                sp.wait_ge(sc_in, nth["S", "swa", 3, 1] + 1)
                sp.dma_start(x_again[:, :, :], x_v).then_inc(s_xa, 16)

            def load_w1(which):
                if which == "k":
                    wait_evacuated(sp, ("ev", "out1", 1))
                else:
                    sp.wait_ge(sc_in, nth["hidden", 0] + 1)
                src = a[f"cmp_w1_{which}_2"]
                sp.dma_start(w1[:, :, :], src.rearrange("o (m p) f -> p (o m) f", p=P)).then_inc(s_w1, 16)

            def load_small2():
                for e in range(2):
                    sp.dma_start(w2k[:, :, 64 * e:64 * e + 64],
                                 a["cmp_w2_k_2"].rearrange("o (f p) d -> p (o f) d", p=P)).then_inc(s_small2, 16)
                sp.dma_start(w2v[:, :, :], a["cmp_w2_v_2"].rearrange("o (f p) d -> p (o f) d", p=P)).then_inc(s_small2, 16)
                with nc.allow_non_contiguous_dma(reason="position rows as columns, once"):
                    for n, name in enumerate(("cmp_pos_k_2", "cmp_pos_v_2")):
                        v = a[name].rearrange("o (m e) d -> e d (o m)", e=2)
                        for e in range(2):
                            sp.dma_start(pos[64 * e:64 * e + 64, 16 * n:16 * n + 16], v[e]).then_inc(s_small2, 16)
                    sp.dma_start(gmlp_b, a["gmlp_b_s_2"].rearrange("o g t -> t (o g)")).then_inc(s_small2, 16)

            def load_gmlp():
                sp.wait_ge(w_used, first["in2", 4] + KD)
                sp.dma_start(ws_nat[:, :, :], a["gmlp_w_s_2"].rearrange("o g t s -> t (o g) s")).then_inc(s_gm_in, 16)
                bcast(ln_g[:, :], a["gmlp_ln_g_2"], 512).then_inc(s_gm_in, 16)
                bcast(ln_b[:, :], a["gmlp_ln_b_2"], 512).then_inc(s_gm_in, 16)

            def load_gain(n, name, pre):
                if pre is not None:
                    sp.wait_ge(pre[0], pre[1])
                bcast(gain[n][:, :], a[name], D).then_inc(s_gain, 16)

            before = {}
            index = {}
            for g, (phase, chunk, part, s0, w) in enumerate(groups):
                index[phase, chunk, part] = g
            before[index["in1", 1, 0]] = [small_loads]
            before[index["in1", 1, 1]] = [store_rows]
            before[index["in1", 2, 0]] = [load_bias1]
            before[index["in1", 3, 0]] = [load_small2]
            before[index["out1", 0, 0]] = [lambda: load_gain(0, "norm_mix_pre_2", (pre_done, nth["pre", "in1", 3] + 1))]
            before[index["out1", 1, 0]] = [load_x_again, load_bias2]
            before[index["in2", 1, 0]] = [lambda: load_w1("k")]
            before[index["in2", 3, 0]] = [lambda: load_w1("v"),
                                          lambda: load_gain(0, "norm_ffn_pre_2", (pre_done, nth["pre", "in2", 3] + 1))]
            before[index["out2", 1, 0]] = [load_gmlp, lambda: load_gain(1, "norm_mix_post_2", (o_in, nth["CO", 3] + 1))]
            before[index["gu", 2, 0]] = [lambda: load_gain(1, "norm_ffn_post_2", (post_done, 4))]
            for g in range(len(groups)):
                for f in before.get(g, []):
                    f()
                load_group(g)
            out_v = out.rearrange("o (t p) d -> p (o t) d", p=P)
            for t in range(NT):
                sp.wait_ge(post_done, NT + t + 1)
                sp.dma_start(out_v[:, t, :], R2[:, t, :]).then_inc(s_out, 16)
            sp.wait_ge(s_rows, 48)
            sp.wait_ge(s_rep, 256)
            sp.wait_ge(s_out, 16 * NT)

        @block.tensor
        def _(pe):
            def product(outp, stationary, moving, start, stop):
                for n, (x, y) in enumerate(((0, 0), (0, 1), (1, 0))):
                    last = pe.matmul(outp, stationary(x), moving(y), start=start and n == 0, stop=stop and n == 2)
                return last

            def tables():
                pe.wait_ge(s_tab, 96)
                pe.wait_ge(setup_dve, 1)
                pe.matmul(SC[0][0:8, :], tab1[0:33, :], hots[0:33, 0:512], start=True, stop=True).then_inc(tab_done, 1)
                pe.matmul(SC[1][0:8, 0:128], tab1[0:33, :], hots[0:33, 512:640], start=True, stop=True).then_inc(tab_done, 1)
                pe.wait_ge(tab_out, 1)
                pe.matmul(SC[0][0:8, 0:384], tab1[0:33, :], hots[0:33, 640:1024], start=True, stop=True).then_inc(tab_done, 1)
                pe.wait_ge(tab_out, 2)
                pe.matmul(SC[1][0:8, :], tab2[0:33, :], hots[0:33, 1024:1536], start=True, stop=True).then_inc(tab_done, 1)
                pe.wait_ge(tab_out, 3)
                pe.matmul(SC[0][0:8, 0:128], tab2[0:33, :], hots[0:33, 1536:1664], start=True, stop=True).then_inc(tab_done, 1)
                for b, bank in enumerate((TR, OB)):
                    for i in range(2):
                        for n in range(NCMP):
                            v = 1664 + P * (2 * b + i) - 16 * n + 480
                            col = (i * 32 + n) * 8
                            last = pe.matmul(bank[:, col:col + 8], hots[0:33, v:v + P], tab2[0:33, :], start=True, stop=True)
                    last.then_inc(tab_done, 1)

            def wait_tr(step):
                if nth[step]:
                    pe.wait_ge(tr_out, nth[step])
                else:
                    pe.wait_ge(tab_out, 6)

            def wait_sc(step):
                if nth[step] >= 2:
                    pe.wait_ge(sc_out, nth[step] - 1)

            tables_at = ("split", first["in1", 1] + 4)
            for step in timeline:
                what = step[0]
                if step == tables_at:
                    tables()
                if what == "xt":
                    _, phase, t, hf = step
                    n = nth[step]
                    bank = MM[n % 4]
                    if n % 8 == 0:
                        if n:
                            wait_evacuated(pe, {"out1": ("ev", "in1", 7), "in2": ("ev", "out1", 1),
                                                "out2": ("ev", "in2", 4), "gu": ("ev", "out2", 1)}[phase])
                        else:
                            pe.wait_ge(s_ident, 16)
                    if n >= 4:
                        pe.wait_ge(xt_lo, n - 3)
                    if phase != "out2":
                        pe.wait_ge(pre_done, nth["pre", phase, t] + 1)
                        src = prob[:, t % 2, 0:D]
                    else:
                        if t == 0 and hf == 0:
                            pe.wait_ge(o_out, o_heads[last_o(("win", 7))])
                            pe.wait_ge(sc_out, nth["gm", 3] + 1)
                        src = R1[:, t, :]
                    for q in range(4):
                        k = 4 * hf + q
                        last = pe.transpose(bank[:, P * q:P * q + P], src[:, P * k:P * k + P], ident[:, :])
                    last.then_inc(xt_in, 1)
                elif what == "mm":
                    _, phase, ch, k = step
                    s = first[phase, ch] + k
                    if phase == "down":
                        s = first[phase, ch]
                        pe.wait_ge(w_lo, s + 2)
                        pe.wait_ge(act_lo, ch + 1)
                        if ch == 0:
                            pe.wait_ge(ev_dve, ev_count["ev", "gu", GU_CHUNKS - 1][1])
                            pe.wait_ge(ev_act, ev_count["ev", "gu", GU_CHUNKS - 1][0])
                        for hf in range(2):
                            for t in range(NT):
                                last = product(SET[hf][t], lambda x, t=t: XT[:, ch % 8, x, P * t:P * t + P],
                                               lambda y, hf=hf: WR[:, (s + hf) % RING, y, :],
                                               ch == 0, ch == DOWN_TILES - 1)
                            last.then_inc(w_used, 1)
                        continue
                    pe.wait_ge(w_lo, s + 1)
                    if k == 0:
                        if ch == 0:
                            pe.wait_ge(xt_lo, nth["xt", phase, 3, 1] + 1)
                        if phase == "gu":
                            if ch == 1:
                                pe.wait_ge(tr_out, seen["tr"])
                                pe.wait_ge(sc_out, seen["sc"])
                                pe.wait_ge(o_out, n_heads)
                            if ch >= 2:
                                wait_evacuated(pe, ("ev", phase, ch - 2))
                        elif ch:
                            prev = ("ev", phase, ch - 1)
                    for t in range(NT):
                        if k == 0 and ch and phase != "gu":
                            who = evac_engine(phase, ch - 1, t)
                            done = ev_count[prev][0 if who == "act" else 1]
                            mine = [u for u in range(NT) if evac_engine(phase, ch - 1, u) == who]
                            pe.wait_ge(ev_act if who == "act" else ev_dve, done - len(mine) + mine.index(t) + 1)
                        if phase == "gu":
                            last = product(SET[ch % 2][t], lambda x, t=t: WR[:, s % RING, x, P * t:P * t + P],
                                           lambda y: XT[:, k, y, :], k == 0, k == KD - 1)
                        else:
                            w = sum(n for _, n in group_cols(phase, ch))
                            last = product(MM[t][:, 0:w], lambda x, t=t: XT[:, k, x, P * t:P * t + P],
                                           lambda y: WR[:, s % RING, y, 0:w], k == 0, k == KD - 1)
                    last.then_inc(w_used, 1)
                elif what == "qt":
                    _, name, t = step
                    wait_tr(step)
                    tok = slice(P * t, P * t + P)
                    if name in KINDS1:
                        if name == "sb":
                            wait_evacuated(pe, ("ev", "in1", 4))
                        else:
                            pe.wait_ge(qn_done, nth["qn", name, t] + 1)
                        srcs = [qk_nat[:, t, P * q:P * q + P] for q in range(4)]
                    elif name == "cmp":
                        wait_evacuated(pe, ("ev", "in2", 0))
                        srcs = [cmp_nat[:, t, q, :] for q in range(4)]
                    elif name == "q":
                        wait_evacuated(pe, ("ev", "in2", 1))
                        srcs = [nat2[:, t, P * q:P * q + P] for q in range(4)]
                    else:
                        wait_evacuated(pe, ("ev", "in2", 0 if name == "slc" else 2))
                        srcs = [nat2[:, t, P * q:P * q + P] for q in range(2)]
                    for q, src in enumerate(srcs):
                        last = pe.transpose(TR[:, P * q:P * q + P], src, ident[:, :])
                    last.then_inc(tr_in, 1)
                elif what == "C":
                    h = step[1]
                    wait_sc(step)
                    if h == 0:
                        pe.wait_ge(lf_done, 1)
                        pe.wait_ge(tab_out, 5)
                    for kb in range(NT):
                        last = pe.matmul(SC[nth[step] % 2][:, P * kb:SEQ], lf[:, 4 * kb + h:4 * kb + h + 1].broadcast_to([P, P]),
                                         tri[:, 0:SEQ - P * kb], start=kb == 0, stop=True, skip_group_check=True)
                    last.then_inc(sc_in, 1)
                elif what == "S":
                    _, name, h, g = step
                    plan = HEADS[name][0]
                    wait_sc(step)
                    if h == 0 and g == 0:
                        pe.wait_ge(tr_out, nth[q_ready(name)] + 1)
                        if name == "fox":
                            pe.wait_ge(setup_dve, 3)
                    bank = SC[nth[step] % 2]
                    for i, j, m, col, n in segments(plan, g):
                        last = pe.matmul(bank[:, col:col + m * P], q_of(name, h)[:, P * i:P * i + P],
                                         k_of(name, h)[:, P * j:P * (j + m)], start=True, stop=True)
                        if name == "fox":
                            d = col + (m - 1) * P
                            last = pe.matmul(bank[:, d:d + P], identb[:, :], causal[:, :], start=False, stop=True, skip_group_check=True)
                    last.then_inc(sc_in, 1)
                elif what == "T":
                    _, name, h, g = step
                    plan = HEADS[name][0]
                    wait_tr(step)
                    pe.wait_ge(e_done, e_index[name, h, g])
                    buf = prob[:, head_index(name, h) % 2, GROUP_AT[g]:GROUP_AT[g] + width(plan, g)]
                    for q in range(width(plan, g) // P):
                        last = pe.transpose(TR[:, P * q:P * q + P], buf[:, P * q:P * q + P], ident[:, :])
                    last.then_inc(tr_in, 1)
                elif what == "O":
                    _, name, h, g = step
                    plan = HEADS[name][0]
                    pe.wait_ge(tr_out, nth["T", name, h, g] + 1)
                    if g == 0:
                        if name == "fox" and h == 0:
                            wait_evacuated(pe, ("ev", "in1", 1))
                            pe.wait_ge(tab_out, 7)
                        elif o_heads[step]:
                            pe.wait_ge(o_out, o_heads[step])
                        if name == "moba" and h == 0:
                            wait_evacuated(pe, ("ev", "in1", 3))
                        if name == "swa" and h == 0:
                            wait_evacuated(pe, ("ev", "in1", 5))
                        if name == "slc" and h == 0:
                            wait_evacuated(pe, ("ev", "in2", 0))
                        if name == "win" and h == 0:
                            wait_evacuated(pe, ("ev", "in2", 2))
                    for i, j, m, col, n in segments(plan, g):
                        for b in range(m):
                            at_ = GROUP_AT[g] + col + b * P
                            last = pe.matmul(OB[:, HD * n:HD * n + HD], probT[:, at_:at_ + P], v_of(name, h, j + b),
                                             start=b == 0, stop=b == m - 1)
                    last.then_inc(o_in, 1)
                elif what == "Z":
                    _, h, g = step
                    wait_sc(step)
                    if h == 0 and g == 0:
                        pe.wait_ge(tr_out, nth["qt", "sb", 3] + 1)
                    bank = SC[nth[step] % 2]
                    for j in KEYS[g]:
                        col = KEY_COLS[j] - GROUP_AT[g]
                        w = SEQ - P * j
                        pe.matmul(bank[:, col:col + w], k_of("sb", h)[:, P * j:P * j + P], q_of("sb", h)[:, P * j:SEQ],
                                  start=True, stop=True)
                        last = pe.matmul(bank[:, col:col + P], identb[:, :], strict[:, :], start=False, stop=True, skip_group_check=True)
                    last.then_inc(sc_in, 1)
                elif what == "F":
                    _, h, g = step
                    wait_tr(step)
                    pe.wait_ge(sp_done, h + 1)
                    for j in KEYS[g]:
                        col = KEY_COLS[j] - GROUP_AT[g]
                        for jj in range(j, NT):
                            w = SEQ - P * jj
                            off = P * (jj - j)
                            last = pe.matmul(TR[:, col + off:col + off + w], suffix[:, :] if jj == j else tri[:, P:2 * P],
                                             soft[:, h % 2, KEY_COLS[jj]:KEY_COLS[jj] + w], start=jj == j, stop=True,
                                             skip_group_check=True)
                    last.then_inc(tr_in, 1)
                elif what == "OS":
                    h = step[1]
                    pe.wait_ge(a_done, 3 * h + 3)
                    pe.wait_ge(o_out, o_heads[step] - 1)
                    if h == 0:
                        wait_evacuated(pe, ("ev", "in1", 3))
                    for i in range(NT):
                        for j in range(i + 1):
                            at_ = KEY_COLS[j] + P * (i - j)
                            last = pe.matmul(OB[:, HD * i:HD * i + HD], probT[:, at_:at_ + P], v_of("sb", h, j), start=j == 0, stop=j == i)
                    last.then_inc(o_in, 1)
                elif what == "hidden":
                    kv = step[1]
                    wait_sc(step)
                    pe.wait_ge(s_w1, 16 * (kv + 1))
                    pe.wait_ge(blk_done, 1)
                    for f in range(2):
                        for m in range(16):
                            last = pe.matmul(SC[nth[step] % 2][:, 64 * f:64 * f + 64], w1[:, m, P * f:P * f + P],
                                             blocks[:, kv, m, :], start=m == 0, stop=m == 15)
                    last.then_inc(sc_in, 1)
                elif what == "cmpkv":
                    wait_sc(step)
                    pe.wait_ge(hid_rep, 1)
                    pe.wait_ge(hid_act, 2)
                    pe.wait_ge(s_small2, 16 * 8)
                    bank = SC[nth[step] % 2]
                    for f in range(2):
                        pe.matmul(bank[:, 0:64], w2k[:, f, :], hidT[:, 0, f, :], start=f == 0, stop=f == 1)
                    for g in range(2):
                        for f in range(2):
                            last = pe.matmul(bank[:, 64 + 64 * g:128 + 64 * g], hidV[:, f, g, :], w2v[:, f, :], start=f == 0, stop=f == 1)
                    last.then_inc(sc_in, 1)
                elif what == "CS":
                    i = step[1]
                    wait_sc(step)
                    if i == 0:
                        pe.wait_ge(sc_out, nth["cmpkv",] + 1)
                        pe.wait_ge(tr_out, nth["qt", "q", 3] + 1)
                    for pair in range(4):
                        last = pe.matmul(SC[nth[step] % 2][:, 64 * pair:64 * pair + 64], qT2[:, pair, P * i:P * i + P],
                                         kcT[:, pair // 2, :, :].rearrange("p e n -> p (e n)"), start=True, stop=True)
                    last.then_inc(sc_in, 1)
                elif what == "CT":
                    i = step[1]
                    wait_tr(step)
                    pe.wait_ge(cs_exp, i + 1)
                    for g in range(2):
                        last = pe.transpose(TR[:, P * g:P * g + P], prob[:, i % 2, P * g:P * g + P], ident[:, :])
                    last.then_inc(tr_in, 1)
                elif what == "CO":
                    i = step[1]
                    pe.wait_ge(tr_out, nth["CT", i] + 1)
                    pe.wait_ge(o_out, o_heads[step] - 1)
                    for g in range(2):
                        last = pe.matmul(OB[:, 256 * g:256 * g + 256], probT[:, P * g:P * g + P],
                                         vbd[:, g, :, :].rearrange("p r d -> p (r d)"), start=True, stop=True)
                    last.then_inc(o_in, 1)
                elif what == "gm_w":
                    u = step[1]
                    wait_tr(step)
                    pe.wait_ge(s_gm_in, 48)
                    for q in range(4):
                        last = pe.transpose(TR[:, P * q:P * q + P], ws_nat[:, 4 * u + q, :], ident[:, :])
                    last.then_inc(tr_in, 1)
                elif what == "gm":
                    u = step[1]
                    wait_sc(step)
                    pe.wait_ge(gm_n, 4)
                    pe.wait_ge(tr_out, nth["gm_w", 1] + 1)
                    for q in range(2):
                        g = 2 * u + q
                        last = pe.matmul(SC[nth[step] % 2][:, 256 * q:256 * q + 256], wsT[:, g, :],
                                         zv[:, :, HD * g:HD * g + HD], start=True, stop=True)
                    last.then_inc(sc_in, 1)

        @block.scalar
        def _(act):
            link_n = [0]

            def link(ins):
                link_n[0] += 1
                ins.then_inc(a_chain, 1)
                act.wait_ge(a_chain, link_n[0])

            raw_seen = [0, 0]
            group_of = {}
            for g, (phase, chunk, part, s0, w) in enumerate(groups):
                n = 1 if phase == "down" else (2 if phase == "gu" else len(group_cols(phase, chunk)))
                raw_seen[g % 2] += 16 * n
                for q in range(4):
                    group_of[s0 + q] = (g, q, w, raw_seen[g % 2])

            for step in timeline:
                what = step[0]
                if what == "split":
                    s = step[1]
                    g, q, w, landed = group_of[s]
                    act.wait_ge(s_raw[g % 2], landed)
                    if s >= RING:
                        act.wait_ge(w_used, s - RING + 1)
                    act.activation(WR[:, s % RING, 0, 0:w], RAW[:, g % 2, q, 0:w], ACT.Copy).then_inc(w_hi, 1)
                elif what == "xt":
                    _, phase, t, hf = step
                    n = nth[step]
                    act.wait_ge(xt_in, n + 1)
                    if n % 8 == 0 and n:
                        prev = {"out1": ("in1", 7), "in2": ("out1", 1), "out2": ("in2", 4), "gu": ("out2", 1)}[phase]
                        act.wait_ge(w_used, first[prev] + KD)
                        if phase == "out2":
                            act.wait_ge(sc_out, nth["gm", 3] + 1)
                            act.wait_ge(sc_in, nth["gm", 3] + 1)
                    act.activation(XT[:, 4 * hf:4 * hf + 4, 0, P * t:P * t + P],
                                   MM[n % 4].rearrange("p (q n) -> p q n", q=4), ACT.Copy).then_inc(xt_hi, 1)
                elif what == "ev":
                    _, phase, ch = step
                    if phase == "down":
                        t = ch
                        act.wait_ge(w_used, n_slots)
                        act.activation(R1[:, t, 0:512], SET[0][t], ACT.Copy).then_inc(ev_act, 1)
                        continue
                    act.wait_ge(w_used, first[phase, ch] + KD)
                    if phase == "gu":
                        for m in range(2):
                            if ch:
                                act.wait_ge(ev_dve, ev_count["ev", "gu", ch - 1][1])
                            act.activation(gated[:, m, :], SET[ch % 2][m], ACT.Silu).then_inc(gs_done, 1)
                        continue
                    if (phase, ch) == ("in2", 0):
                        act.wait_ge(xt_lo, nth["xt", "in2", 3, 1] + 1)
                    if (phase, ch) == ("in1", 4):
                        act.wait_ge(tr_in, nth["qt", "moba", 3] + 1)
                    if (phase, ch) == ("in1", 2):
                        act.wait_ge(tr_in, nth["qt", "fox", 3] + 1)
                    if (phase, ch) == ("in1", 5):
                        act.wait_ge(tr_in, nth["qt", "sb", 3] + 1)
                    if (phase, ch) == ("in1", 6):
                        act.wait_ge(pre_done, 4)
                    if (phase, ch) == ("in2", 1):
                        act.wait_ge(tr_in, nth["qt", "slc", 3] + 1)
                    if (phase, ch) == ("in2", 2):
                        act.wait_ge(tr_in, nth["qt", "q", 3] + 1)
                    if (phase, ch) == ("in2", 3):
                        act.wait_ge(sc_in, nth["hidden", 1] + 1)
                    if (phase, ch) == ("in2", 4):
                        act.wait_ge(sc_out, nth["cmpkv",] + 1)
                    if (phase, ch) == ("out2", 0):
                        act.wait_ge(xt_in, nth["xt", "out2", 3, 1] + 1)
                    for t in range(NT):
                        if evac_engine(phase, ch, t) != "act":
                            continue
                        for ins in evacuate(act, phase, ch, t):
                            last = ins
                        last.then_inc(ev_act, 1)
                elif what == "logf":
                    act.wait_ge(lf_pre, 1)
                    link(act.activation(lf_a, lf_a, ACT.Exp))
                    act.activation(lf_a, lf_a, ACT.Ln, bias=1.0).then_inc(lf_act, 1)
                elif what == "S":
                    _, name, h, g = step
                    plan = HEADS[name][0]
                    act.wait_ge(sc_out, nth[step] + 1)
                    hi = head_index(name, h)
                    buf = prob[:, hi % 2, GROUP_AT[g]:GROUP_AT[g] + width(plan, g)]
                    sl = 4 * (hi % 4)
                    for i, j, m, col, n in segments(plan, g):
                        last = act.activation(buf[:, col:col + m * P], buf[:, col:col + m * P], ACT.Exp,
                                              bias=nm[:, sl + n:sl + n + 1], accum_out=sm[:, sl + n:sl + n + 1])
                        if name == "swa":
                            last = act.activation(es[:, sl + n:sl + n + 1], nm[:, sl + n:sl + n + 1], ACT.Exp, bias=sinks[:, h:h + 1])
                    last.then_inc(e_done, 1)
                elif what == "sp":
                    h = step[1]
                    act.wait_ge(sp_abs, h + 1)
                    link(act.activation(soft[:, h % 2, :], soft[:, h % 2, :], ACT.Exp))
                    act.activation(soft[:, h % 2, :], soft[:, h % 2, :], ACT.Ln, bias=1.0).then_inc(sp_ln, 1)
                elif what == "F":
                    _, h, g = step
                    act.wait_ge(tr_out, nth[step] + 1)
                    if g == 0:
                        act.wait_ge(o_in, nth[last_o(("sb", h - 1) if h else ("moba", 3))] + 1)
                    lo = GROUP_AT[g]
                    w = sum(SEQ - P * j for j in KEYS[g])
                    act.activation(probT[:, lo:lo + w], prob[:, h % 2, lo:lo + w], ACT.Exp).then_inc(a_done, 1)
                elif what == "hidden":
                    kv = step[1]
                    act.wait_ge(sc_in, nth[step] + 1)
                    if kv == 0:
                        act.wait_ge(tr_in, nth["qt", "cmp", 3] + 1)
                    act.activation(hidT[:, kv, :, :], SC[nth[step] % 2][:, 0:128].rearrange("p (f n) -> p f n", f=2),
                                   ACT.Gelu_apprx_tanh).then_inc(hid_act, 1)
                elif what == "gates":
                    wait_evacuated(act, ("ev", "in2", 2))
                    act.activation(g_tmp, g_tmp, ACT.Exp, scale=-1.0).then_inc(gate_e, 1)
                elif what == "CS":
                    i = step[1]
                    act.wait_ge(cs_sub, i + 1)
                    act.activation(prob[:, i % 2, 0:256], prob[:, i % 2, 0:256], ACT.Exp).then_inc(cs_exp, 1)
                elif what == "act":
                    kt = step[1]
                    act.wait_ge(ev_dve, ev_count["ev", "gu", kt // 2][1])
                    if kt == 0:
                        act.wait_ge(w_used, first["gu", GU_CHUNKS - 1] + KD)
                    if kt >= 8:
                        act.wait_ge(w_used, first["down", kt - 8] + 2)
                    act.activation(XT[:, kt % 8, 0, :], actT[:, kt, :], ACT.Copy).then_inc(act_hi, 1)

        @block.vector
        def _(dve):
            link_n = [0]

            def link(ins):
                link_n[0] += 1
                ins.then_inc(v_chain, 1)
                dve.wait_ge(v_chain, link_n[0])

            dve.memset(half, -0.5)
            dve.memset(tab1[32:33, :], 1.0)
            dve.memset(tab2[32:33, :], 1.0).then_inc(setup_dve, 1)
            dve.memset(cmp_bias[:, :, :, :], MASK).then_inc(setup_dve, 1)

            def setup():
                dve.wait_ge(s_const, 16 * 12)
                dve.wait_ge(s_ident, 16)
                dve.tensor_copy(identb[:, :], ident[:, :])
                dve.tensor_copy(causal[:, :], stage[:, 0:128])
                dve.tensor_copy(strict[:, :], stage[:, 128:256])
                for n in range(3):
                    last = dve.tensor_scalar(qk_gain[:, 2 * n:2 * n + 1], qk_gain[:, 2 * n:2 * n + 1], QSCALE, None, ALU.mult)
                last.then_inc(setup_dve, 1)
                dve.wait_ge(setup_dve, 3)
                dve.wait_ge(tab_done, 1)
                dve.tensor_copy(rows[0:8, 0:512], SC[0][0:8, :]).then_inc(tab_out, 1)
                dve.wait_ge(tab_done, 2)
                dve.tensor_copy(rows[0:8, 512:640], SC[1][0:8, 0:128]).then_inc(tab_out, 1)
                dve.wait_ge(tab_done, 3)
                dve.tensor_copy(rows[0:8, 640:1024], SC[0][0:8, 0:384]).then_inc(tab_out, 1)
                dve.wait_ge(tab_done, 4)
                dve.tensor_copy(rows[0:8, 1024:1536], SC[1][0:8, :]).then_inc(tab_out, 1)
                dve.wait_ge(tab_done, 5)
                dve.tensor_copy(rows[0:8, 1536:1664], SC[0][0:8, 0:128]).then_inc(tab_out, 1)
                for b, bank in enumerate((TR, OB)):
                    dve.wait_ge(tab_done, 6 + b)
                    for i in range(2):
                        last = dve.tensor_copy(cmp_bias[:, 2 * b + i, :, 0:NCMP].rearrange("p h n -> p n h"),
                                               bank[:, 256 * i:256 * i + 8 * NCMP].rearrange("p (n h) -> p n h", h=8))
                    last.then_inc(tab_out, 1)

            n_ms = 0
            setup_at = ("split", first["in1", 1] + 4)
            for step in timeline:
                what = step[0]
                if step == setup_at:
                    setup()
                if what == "pre":
                    _, phase, t = step
                    n = nth[step]
                    hn = prob[:, t % 2, 0:D]
                    if t >= 2:
                        dve.wait_ge(xt_in, nth["xt", phase, t - 2, 1] + 1)
                    elif phase == "out1":
                        dve.wait_ge(tr_in, nth["T", "swa", 3, 1] + 1)
                    elif phase == "in2":
                        dve.wait_ge(xt_in, nth["xt", "out1", 2 + t, 1] + 1)
                    elif phase == "gu":
                        dve.wait_ge(tr_in, nth["T", "win", 7, 2] + 1)
                    if phase == "out1":
                        if t == 0:
                            wait_evacuated(dve, ("ev", "in1", 7))
                            dve.wait_ge(o_out, o_total1)
                        dve.tensor_tensor(hn, R2[:, t, :], R1[:, t, :], ALU.mult).then_inc(pre_done, 1)
                        continue
                    src = {"in1": R1, "in2": R2, "gu": R2}[phase]
                    if phase == "in1":
                        dve.wait_ge(s_x[t], 16)
                    elif phase == "in2":
                        wait_evacuated(dve, ("ev", "out1", 1))
                    else:
                        dve.wait_ge(post_done, t + 1)
                    link(dve.tensor_tensor_reduce(hn, src[:, t, :], src[:, t, :], 1.0, 0.0, ALU.mult, ALU.add, ss[:, t:t + 1]))
                    dve.tensor_scalar(ss[:, t:t + 1], ss[:, t:t + 1], 1.0 / D, EPS, ALU.mult, ALU.add).then_inc(ms_ready, 1)
                    n_ms += 1
                    dve.wait_ge(r_ready, n_ms)
                    if t == 0:
                        dve.wait_ge(s_gain, {"in1": 16, "in2": 32, "gu": 64}[phase])
                    dve.scalar_tensor_tensor(out=hn, in0=src[:, t, :], scalar=rr[:, t:t + 1], in1=gain[0][:, :],
                                             op0=ALU.mult, op1=ALU.mult).then_inc(pre_done, 1)
                elif what == "xt":
                    _, phase, t, hf = step
                    n = nth[step]
                    dve.wait_ge(xt_hi, n + 1)
                    hi_part = XT[:, 4 * hf:4 * hf + 4, 0, P * t:P * t + P]
                    dve.tensor_tensor(XT[:, 4 * hf:4 * hf + 4, 1, P * t:P * t + P],
                                      MM[n % 4].rearrange("p (q n) -> p q n", q=4), hi_part.bitcast(F32),
                                      ALU.subtract).then_inc(xt_lo, 1)
                elif what == "ev":
                    _, phase, ch = step
                    if phase == "down":
                        t = ch
                        dve.wait_ge(w_used, n_slots)
                        dve.tensor_copy(R1[:, t, 512:1024], SET[1][t]).then_inc(ev_dve, 1)
                        continue
                    if phase == "gu":
                        for m in range(2):
                            dve.wait_ge(gs_done, 2 * ch + m + 1)
                            if ch == 0:
                                dve.wait_ge(tr_in, seen["tr"])
                            last = dve.tensor_tensor(actT[:, 2 * ch + m, :], SET[ch % 2][2 + m], gated[:, m, :], ALU.mult)
                        last.then_inc(ev_dve, 1)
                        continue
                    dve.wait_ge(w_used, first[phase, ch] + KD)
                    if (phase, ch) == ("in1", 2):
                        dve.wait_ge(tr_in, nth["qt", "fox", 3] + 1)
                    if (phase, ch) == ("in1", 4):
                        dve.wait_ge(tr_in, nth["qt", "moba", 3] + 1)
                    if (phase, ch) == ("in1", 5):
                        dve.wait_ge(tr_in, nth["qt", "sb", 3] + 1)
                    if (phase, ch) == ("in2", 1):
                        dve.wait_ge(tr_in, nth["qt", "slc", 3] + 1)
                    if (phase, ch) == ("in2", 2):
                        dve.wait_ge(tr_in, nth["qt", "q", 3] + 1)
                    if (phase, ch) == ("out2", 0):
                        dve.wait_ge(xt_in, nth["xt", "out2", 3, 1] + 1)
                    for t in range(NT):
                        if evac_engine(phase, ch, t) != "dve":
                            continue
                        if phase == "out1":
                            dve.wait_ge(s_xa, 16)
                            cols = slice(512 * ch, 512 * ch + 512)
                            dve.tensor_tensor(R2[:, t, cols], MM[t], x_again[:, t, cols], ALU.add).then_inc(ev_dve, 1)
                            continue
                        for ins in evacuate(dve, phase, ch, t):
                            last = ins
                        last.then_inc(ev_dve, 1)
                elif what == "qn":
                    _, name, t = step
                    wait_evacuated(dve, ("ev", "in1", {"fox": 0, "moba": 2, "swa": 5}[name]))
                    link(dve.tensor_tensor(sq[:, :], qk_nat[:, t, :], qk_nat[:, t, :], ALU.mult))
                    link(dve.tensor_reduce(ms8, sq[:, :].rearrange("p (h d) -> p h d", d=HD), AX.X, ALU.add))
                    dve.tensor_scalar(ms8, ms8, 1.0 / HD, EPS, ALU.mult, ALU.add).then_inc(ms_ready, 1)
                    n_ms += 1
                    dve.wait_ge(r_ready, n_ms)
                    v = qk_nat[:, t, :].rearrange("p (h d) -> p h d", d=HD)
                    dve.tensor_tensor(v, v, rr8.unsqueeze(2).broadcast_to([P, 8, HD]), ALU.mult).then_inc(qn_done, 1)
                elif what == "qt":
                    _, name, t = step
                    dve.wait_ge(tr_in, nth[step] + 1)
                    tok = slice(P * t, P * t + P)
                    if name in KINDS1:
                        kd = KINDS1[name]
                        if t == 0 and name == "sb":
                            dve.wait_ge(sc_in, nth["S", "fox", 3, 2] + 1)
                        if t == 0 and name == "swa":
                            dve.wait_ge(sc_in, nth["S", "moba", 3, 2] + 1)
                        for part in range(2):
                            dst = qkT1[:, kd % 2, 2 * part:2 * part + 2, tok]
                            src = TR[:, 256 * part:256 * part + 256].rearrange("p (q n) -> p q n", q=2)
                            if name == "sb":
                                last = dve.tensor_scalar(dst, src, QSCALE if part == 0 else 1.0, None, ALU.mult)
                            else:
                                gcol = 2 * {"fox": 0, "moba": 1, "swa": 2}[name] + part
                                last = dve.tensor_scalar(dst, src, qk_gain[:, gcol:gcol + 1], None, ALU.mult)
                    elif name == "q":
                        last = dve.tensor_scalar(qT2[:, :, tok], TR.rearrange("p (q n) -> p q n", q=4), QSCALE, None, ALU.mult)
                    elif name == "cmp":
                        if t == 0:
                            dve.wait_ge(pre_done, nth["pre", "out1", 3] + 1)
                        src = TR.rearrange("p (v g n) -> p v g n", v=2, g=2)
                        for v in range(2):
                            dve.tensor_copy(cmpT[0:64, v, :, tok], src[0:64, v])
                            lo = 1 if t == 0 else 0
                            last = dve.tensor_copy(cmpT[64:128, v, :, P * t - 1 + lo:P * t + P - 1], src[64:128, v, :, lo:P])
                    else:
                        last = dve.tensor_copy(kT2[:, 0 if name == "slc" else 1, :, tok], TR[:, 0:256].rearrange("p (g n) -> p g n", g=2))
                    last.then_inc(tr_out, 1)
                elif what == "logf":
                    wait_evacuated(dve, ("ev", "in1", 1))
                    link(dve.tensor_tensor(lf_u.rearrange("p (t h) -> p t h", h=4), lf_u.rearrange("p (t h) -> p t h", h=4),
                                           b_forget.unsqueeze(1).broadcast_to([P, 4, 4]), ALU.add))
                    dve.scalar_tensor_tensor(out=lf_a, in0=lf_u, scalar=-1.0, in1=lf_u, op0=ALU.mult, op1=ALU.min).then_inc(lf_pre, 1)
                    dve.wait_ge(lf_pre, 1)
                    link(dve.tensor_scalar(lf_u, lf_u, -1.0, 0.0, ALU.mult, ALU.max))
                    dve.wait_ge(lf_act, 1)
                    dve.tensor_tensor(lf, lf_u, lf_a, ALU.add).then_inc(lf_done, 1)
                elif what == "C":
                    h = step[1]
                    dve.wait_ge(sc_in, nth[step] + 1)
                    dve.tensor_copy(fox_c[:, h, :], SC[nth[step] % 2]).then_inc(sc_out, 1)
                elif what == "S":
                    _, name, h, g = step
                    plan = HEADS[name][0]
                    hi = head_index(name, h)
                    buf = prob[:, hi % 2, GROUP_AT[g]:GROUP_AT[g] + width(plan, g)]
                    sl = 4 * (hi % 4)
                    dve.wait_ge(sc_in, nth[step] + 1)
                    if name == "swa" and h < 2:
                        if g == 0:
                            dve.wait_ge(a_done, 3 * (2 + h) + 3)
                    elif name == "slc" and h < 2:
                        dve.wait_ge(tr_in, nth["CT", 2 + h] + 1)
                    elif name == "fox" and h < 2:
                        dve.wait_ge(xt_in, 8)
                        if h == 0 and g == 0:
                            dve.wait_ge(sc_out, nth["C", 0] + 1)
                    elif name in ("moba", "win") and h < 2:
                        dve.wait_ge(tr_in, nth["T", "fox" if name == "moba" else "slc", HEADS["fox" if name == "moba" else "slc"][1] - 2 + h, g] + 1)
                    else:
                        dve.wait_ge(tr_in, nth["T", name, h - 2, g] + 1)
                    if h == 0 and g == 0 and name in ("moba", "swa"):
                        dve.wait_ge(s_bias1, 128)
                    if h == 0 and g == 0 and name == "slc":
                        dve.wait_ge(s_bias2, 128)
                    if name == "fox" and g == 0:
                        dve.wait_ge(sc_out, nth["C", h] + 1)
                    first_n = None
                    for i, j, m, col, n in segments(plan, g):
                        first_n = n if first_n is None else first_n
                        last = dve.tensor_tensor_reduce(buf[:, col:col + m * P], SC[nth[step] % 2][:, col:col + m * P],
                                                        bias_of(name, h, i, m), 1.0, -3e38, ALU.add, ALU.max,
                                                        mx[:, sl + n:sl + n + 1])
                    link(last)
                    ns = slice(sl + first_n, sl + n + 1)
                    if name == "swa":
                        dve.tensor_scalar(nm[:, ns], mx[:, ns], sinks[:, h:h + 1], -1.0, ALU.max, ALU.mult).then_inc(sc_out, 1)
                    else:
                        dve.tensor_scalar(nm[:, ns], mx[:, ns], -1.0, None, ALU.mult).then_inc(sc_out, 1)
                elif what == "T":
                    _, name, h, g = step
                    w = width(HEADS[name][0], g)
                    dve.wait_ge(tr_in, nth[step] + 1)
                    prev = prev_head(name, h)
                    if prev is not None:
                        same = prev[0] in HEADS and HEADS[prev[0]][0] is HEADS[name][0]
                        dve.wait_ge(o_in, nth[("O", *prev, g) if same else last_o(prev)] + 1)
                    dve.tensor_copy(probT[:, GROUP_AT[g]:GROUP_AT[g] + w], TR[:, 0:w]).then_inc(tr_out, 1)
                elif what == "O":
                    _, name, h, g = step
                    plan = HEADS[name][0]
                    if step != last_o((name, h)):
                        continue
                    sl = 4 * (head_index(name, h) % 4)
                    dve.wait_ge(o_in, nth[step] + 1)
                    if name == "swa":
                        link(dve.tensor_tensor(sm[:, sl:sl + 4], sm[:, sl:sl + 4], es[:, sl:sl + 4], ALU.add))
                    link(dve.reciprocal(ri[:, sl:sl + 4], sm[:, sl:sl + 4]))
                    if name in ("slc", "win"):
                        gc = 4 * (3 * h + (1 if name == "slc" else 2))
                        link(dve.tensor_tensor(ri[:, sl:sl + 4], ri[:, sl:sl + 4], gates[:, gc:gc + 4], ALU.mult))
                    for gg in range(len(plan)):
                        for i, j, m, col, n in segments(plan, gg):
                            src = OB[:, HD * n:HD * n + HD]
                            f = ri[:, sl + n:sl + n + 1]
                            if name in ("slc", "win"):
                                dst = R1[:, i, HD * h:HD * h + HD]
                                last = dve.scalar_tensor_tensor(out=dst, in0=src, scalar=f, in1=dst, op0=ALU.mult, op1=ALU.add)
                            else:
                                lo = 256 * KINDS1[name] + HD * h
                                last = dve.tensor_scalar(R2[:, i, lo:lo + HD], src, f, None, ALU.mult)
                    last.then_inc(o_out, 1)
                elif what == "Z":
                    _, h, g = step
                    lo = GROUP_AT[g]
                    w = sum(SEQ - P * j for j in KEYS[g])
                    dve.wait_ge(sc_in, nth[step] + 1)
                    if g == 0:
                        if h < 2:
                            dve.wait_ge(tr_in, nth["T", "moba", 2 + h, 2] + 1)
                        else:
                            dve.wait_ge(a_done, 3 * (h - 2) + 3)
                    dve.tensor_copy(prob[:, h % 2, lo:lo + w], SC[nth[step] % 2][:, 0:w]).then_inc(sc_out, 1)
                elif what == "sp":
                    h = step[1]
                    dve.wait_ge(sc_out, nth["Z", h, 2] + 1)
                    if h >= 2:
                        dve.wait_ge(tr_in, nth["F", h - 2, 2] + 1)
                    dve.scalar_tensor_tensor(out=soft[:, h % 2, :], in0=prob[:, h % 2, :], scalar=-1.0, in1=prob[:, h % 2, :],
                                             op0=ALU.mult, op1=ALU.min).then_inc(sp_abs, 1)
                    dve.wait_ge(sp_ln, h + 1)
                    dve.scalar_tensor_tensor(out=soft[:, h % 2, :], in0=prob[:, h % 2, :], scalar=0.0, in1=soft[:, h % 2, :],
                                             op0=ALU.max, op1=ALU.add).then_inc(sp_done, 1)
                elif what == "F":
                    _, h, g = step
                    lo = GROUP_AT[g]
                    w = sum(SEQ - P * j for j in KEYS[g])
                    dve.wait_ge(tr_in, nth[step] + 1)
                    dve.tensor_tensor(prob[:, h % 2, lo:lo + w], prob[:, h % 2, lo:lo + w], TR[:, 0:w], ALU.subtract).then_inc(tr_out, 1)
                elif what == "OS":
                    h = step[1]
                    dve.wait_ge(o_in, nth[step] + 1)
                    lo = 512 + HD * h
                    dve.tensor_copy(R2[:, :, lo:lo + HD], OB[:, 0:256].rearrange("p (i d) -> p i d", i=4)).then_inc(o_out, 1)
                elif what == "blocks":
                    dve.wait_ge(tr_out, nth["qt", "cmp", 3] + 1)
                    dve.wait_ge(s_small2, 16 * 8)
                    for v in range(2):
                        for g in range(2):
                            dve.memset(blocks[:, v, :, 32 * g + NCMP:32 * g + 32], 0.0)
                            src = cmpT[:, v, g, 0:480 + 32].rearrange("p (i u) -> p i u", u=16)
                            for hb in range(2):
                                s_ = src[:, hb:hb + NCMP, :].rearrange("p i (m e) -> p m i e", e=2)[:, :, :, 0]
                                dst = blocks[:, v, 8 * hb:8 * hb + 8, 32 * g:32 * g + NCMP]
                                pp = pos[:, 16 * v + 8 * hb:16 * v + 8 * hb + 8].unsqueeze(2).broadcast_to([P, 8, NCMP])
                                last = dve.tensor_tensor(dst, s_, pp, ALU.add)
                    last.then_inc(blk_done, 1)
                elif what == "hidden":
                    kv = step[1]
                    dve.wait_ge(hid_act, kv + 1)
                    dve.sem_inc(sc_out, 1)
                    if kv == 1:
                        for f in range(2):
                            for g in range(2):
                                last = dve.tensor_copy(hidV[:, f, g, :].rearrange("p (r i) -> p r i", r=4),
                                                       hidT[:, 1, f, 32 * g:32 * g + 32].unsqueeze(1).broadcast_to([P, 4, 32]))
                        last.then_inc(hid_rep, 1)
                elif what == "cmpkv":
                    dve.wait_ge(sc_in, nth[step] + 1)
                    bank = SC[nth[step] % 2]
                    dve.memset(kcT[:, :, :, :], 0.0)
                    link(dve.memset(vbd[:, :, :, :], 0.0))
                    for e in range(2):
                        dve.tensor_copy(kcT[64 * e:64 * e + 64, :, e, :], bank[64 * e:64 * e + 64, 0:64].rearrange("p (g n) -> p g n", g=2))
                    for r in range(4):
                        last = dve.tensor_copy(vbd[32 * r:32 * r + 32, :, r, :], bank[32 * r:32 * r + 32, 64:192].rearrange("p (g d) -> p g d", g=2))
                    last.then_inc(sc_out, 1)
                elif what == "gates":
                    wait_evacuated(dve, ("ev", "in2", 2))
                    dve.wait_ge(gate_e, 1)
                    link(dve.tensor_scalar(g_tmp, g_tmp, 1.0, None, ALU.add))
                    link(dve.reciprocal(gates, g_tmp))
                elif what == "CS":
                    i = step[1]
                    p3 = prob[:, i % 2, 0:256].rearrange("p (h n) -> p h n", h=8)
                    dve.wait_ge(sc_in, nth[step] + 1)
                    if i >= 2:
                        dve.wait_ge(tr_in, nth["CT", i - 2] + 1)
                    else:
                        dve.wait_ge(xt_in, nth["xt", "in2", 3, 1] + 1)
                    dve.tensor_tensor(p3, SC[nth[step] % 2][:, 0:256].rearrange("p (h n) -> p h n", h=8),
                                      cmp_bias[:, i, :, :], ALU.add).then_inc(sc_out, 1)
                    dve.wait_ge(sc_out, nth[step] + 1)
                    link(dve.tensor_reduce(cm8, p3, AX.X, ALU.max))
                    link(dve.tensor_scalar(cm8, cm8, FLOOR, None, ALU.max))
                    dve.tensor_tensor(p3, p3, cm8.unsqueeze(2).broadcast_to([P, 8, 32]), ALU.subtract).then_inc(cs_sub, 1)
                    dve.wait_ge(cs_exp, i + 1)
                    link(dve.tensor_reduce(cs8, p3, AX.X, ALU.add))
                    link(dve.tensor_scalar(cs8, cs8, 1e-30, None, ALU.max))
                    link(dve.reciprocal(cs8, cs8))
                    gv = gates.rearrange("p (h b q) -> p h b q", h=8, b=3)[:, :, 0, POS[i]]
                    link(dve.tensor_tensor(cf8[:, 8 * i:8 * i + 8], cs8, gv, ALU.mult))
                elif what == "CT":
                    i = step[1]
                    dve.wait_ge(tr_in, nth[step] + 1)
                    if i:
                        dve.wait_ge(o_in, nth["CO", i - 1] + 1)
                    else:
                        dve.wait_ge(o_in, nth[last_o(("swa", 3))] + 1)
                    dve.tensor_copy(probT[:, 0:256], TR[:, 0:256]).then_inc(tr_out, 1)
                elif what == "CO":
                    i = step[1]
                    dve.wait_ge(o_in, nth[step] + 1)
                    if i == 0:
                        dve.wait_ge(sc_in, nth["hidden", 1] + 1)
                    dve.tensor_tensor(R1[:, i, 0:512].rearrange("p (h d) -> p h d", h=8), OB.rearrange("p (h d) -> p h d", h=8),
                                      cf8[:, 8 * i:8 * i + 8].unsqueeze(2).broadcast_to([P, 8, HD]), ALU.mult).then_inc(o_out, 1)
                elif what == "gm_w":
                    u = step[1]
                    dve.wait_ge(tr_in, nth[step] + 1)
                    dve.tensor_tensor(wsT[:, 4 * u:4 * u + 4, :], TR.rearrange("p (q n) -> p q n", q=4),
                                      tri[:, 0:P].unsqueeze(1).broadcast_to([P, 4, P]), ALU.mult).then_inc(tr_out, 1)
                elif what == "gm_n":
                    t = step[1]
                    wait_evacuated(dve, ("ev", "in2", 4))
                    z = zv[:, t, :]
                    link(dve.tensor_reduce(negmu[:, t:t + 1], z, AX.X, ALU.add))
                    link(dve.tensor_scalar(negmu[:, t:t + 1], negmu[:, t:t + 1], 1.0 / 512, None, ALU.mult))
                    link(dve.tensor_scalar(z, z, negmu[:, t:t + 1], None, ALU.subtract))
                    link(dve.tensor_tensor_reduce(sq[:, :], z, z, 1.0, 0.0, ALU.mult, ALU.add, ss[:, t:t + 1]))
                    dve.tensor_scalar(ss[:, t:t + 1], ss[:, t:t + 1], 1.0 / 512, LN_EPS, ALU.mult, ALU.add).then_inc(ms_ready, 1)
                    n_ms += 1
                    dve.wait_ge(r_ready, n_ms)
                    dve.wait_ge(s_gm_in, 48)
                    link(dve.scalar_tensor_tensor(out=z, in0=z, scalar=rr[:, t:t + 1], in1=ln_g[:, :], op0=ALU.mult, op1=ALU.mult))
                    dve.tensor_tensor(z, z, ln_b[:, :], ALU.add).then_inc(gm_n, 1)
                elif what == "gm":
                    u = step[1]
                    dve.wait_ge(sc_in, nth[step] + 1)
                    for q in range(2):
                        g = 2 * u + q
                        dst = R1[:, :, 512 + HD * g:512 + HD * g + HD]
                        last = dve.scalar_tensor_tensor(out=dst, in0=SC[nth[step] % 2][:, 256 * q:256 * q + 256].rearrange("p (n d) -> p n d", n=4),
                                                        scalar=gmlp_b[:, g:g + 1], in1=dst, op0=ALU.add, op1=ALU.mult)
                    last.then_inc(sc_out, 1)
                elif what == "act":
                    kt = step[1]
                    dve.wait_ge(act_hi, kt + 1)
                    dve.tensor_tensor(XT[:, kt % 8, 1, :], actT[:, kt, :], XT[:, kt % 8, 0, :].bitcast(F32), ALU.subtract).then_inc(act_lo, 1)
                elif what == "post":
                    _, name, t = step
                    n = nth[step]
                    hn = prob[:, t % 2, 0:D] if name == "mix" else actT[:, 2 * (t % 2):2 * (t % 2) + 2, :].rearrange("p a n -> p (a n)")
                    if name == "mix":
                        wait_evacuated(dve, ("ev", "out2", 1))
                        dve.wait_ge(tr_in, seen["tr"])
                    else:
                        dve.wait_ge(ev_act, n_act + t + 1)
                        dve.wait_ge(ev_dve, n_dve + t + 1)
                    if t == 0:
                        dve.wait_ge(s_gain, 64 if name == "mix" else 80)
                    link(dve.tensor_tensor_reduce(hn, R1[:, t, :], R1[:, t, :], 1.0, 0.0, ALU.mult, ALU.add, ss[:, t:t + 1]))
                    dve.tensor_scalar(ss[:, t:t + 1], ss[:, t:t + 1], 1.0 / D, EPS, ALU.mult, ALU.add).then_inc(ms_ready, 1)
                    n_ms += 1
                    dve.wait_ge(r_ready, n_ms)
                    link(dve.scalar_tensor_tensor(out=hn, in0=R1[:, t, :], scalar=rr[:, t:t + 1], in1=gain[1][:, :],
                                                  op0=ALU.mult, op1=ALU.mult))
                    dve.tensor_tensor(R2[:, t, :], R2[:, t, :], hn, ALU.add).then_inc(post_done, 1)

        @block.gpsimd
        def _(pool):
            n_ms = 0
            group_of = {}
            for g, (phase, chunk, part, s0, w) in enumerate(groups):
                for q in range(4):
                    group_of[s0 + q] = (g, q, w)
            for step in timeline:
                what = step[0]
                if what == "split":
                    s = step[1]
                    g, q, w = group_of[s]
                    pool.wait_ge(w_hi, s + 1)
                    pool.tensor_tensor(WR[:, s % RING, 1, 0:w], RAW[:, g % 2, q, 0:w], WR[:, s % RING, 0, 0:w].bitcast(F32),
                                       ALU.subtract).then_inc(w_lo, 1)
                    continue
                if what == "pre" and step[1] in ("in1", "in2", "gu"):
                    src, dst, n = ss[:, step[2]:step[2] + 1], rr[:, step[2]:step[2] + 1], 1
                elif what == "post":
                    src, dst, n = ss[:, step[2]:step[2] + 1], rr[:, step[2]:step[2] + 1], 1
                elif what == "qn":
                    src, dst, n = ms8, rr8, 8
                elif what == "gm_n":
                    src, dst, n = ss[:, step[1]:step[1] + 1], rr[:, step[1]:step[1] + 1], 1
                else:
                    continue
                n_ms += 1
                pool.wait_ge(ms_ready, n_ms)
                pool.tensor_tensor(dst, src, half[:, 0:1].broadcast_to([P, n]) if n > 1 else half[:, 0:1], ALU.pow).then_inc(r_ready, 1)


_INS = [
    "x", "norm_gain", "w_in", "b_forget", "fox_qk_gain", "moba_qk_gain", "swa_qk_gain", "sinks", "w_out",
    "rel_bias", "rel_bias_2", "norm_mix_pre_2", "norm_mix_post_2", "norm_ffn_pre_2", "norm_ffn_post_2",
    "w_in_2", "cmp_pos_k_2", "cmp_w1_k_2", "cmp_w2_k_2", "cmp_pos_v_2", "cmp_w1_v_2", "cmp_w2_v_2",
    "gmlp_ln_g_2", "gmlp_ln_b_2", "gmlp_w_s_2", "gmlp_b_s_2", "w_out_2", "w_gate_up_2", "w_down_2",
]


def kernel(**inputs):
    import concourse.bacc as _bacc
    from concourse.bass_utils import run_bass_kernel_spmd as _run

    nc = _bacc.Bacc("TRN2", target_bir_lowering=False, num_devices=1)
    arrays, args, consts = {}, {}, {}
    for name in _INS:
        v = np.ascontiguousarray(inputs[name])
        arrays[f"in_{name}_dram"] = v
        args[name] = nc.dram_tensor(f"in_{name}_dram", v.shape, mybir.dt.from_np(v.dtype), kind="ExternalInput").ap()
    for name, v in constants().items():
        arrays[f"const_{name}_dram"] = v
        consts[name] = nc.dram_tensor(f"const_{name}_dram", v.shape, mybir.dt.from_np(v.dtype), kind="ExternalInput").ap()
    out = nc.dram_tensor("out_0_dram", (1, SEQ, D), F32, kind="ExternalOutput").ap()
    hybrid_two_block_kernel(nc, args, consts, out)
    r = _run(nc, [arrays], core_ids=[0])
    return r.results[0]["out_0_dram"]
```

```python
from contextlib import ExitStack

import numpy as np

import concourse.bass as bass
from concourse import mybir

F32 = mybir.dt.float32
F32R = mybir.dt.float32r
BF16 = mybir.dt.bfloat16
ALU = mybir.AluOpType
ACT = mybir.ActivationFunctionType
AX = mybir.AxisListType

P = 128
SEQ = 512
D = 1024
NT = SEQ // P
KD = D // P
HD = 64
EPS = 1e-6
LN_EPS = 1e-5
MASK = -1e30
FLOOR = -1e29
QSCALE = HD ** -0.5
FF = 2816
NCMP = 31
RING = 6

FQ, FV, FG = 0, 512, 772
MQ, MV, MG = 1028, 1540, 1796
SQ_, SV, SG_ = 2052, 2564, 2820
WQ, WG = 3076, 3588
CHUNKS1 = [
    [(FQ, 512)],
    [(FV, 260)],
    [(MQ, 512)],
    [(MV, 256), (SV, 256)],
    [(SQ_, 512)],
    [(WQ, 512)],
    [(FG, 256), (MG, 256)],
    [(SG_, 256), (WG, 256)],
]
CHUNKS2 = [[(512, 512)], [(0, 512)], [(1024, 280)], [(1304, 512)], [(1816, 512)]]
W_OUT = [[(0, 512)], [(512, 512)]]
GU_CHUNKS = FF // 256
DOWN_TILES = FF // P

HALVES = {"out2": (1, 0)}

FULL = [[(3, 0, 4)], [(2, 0, 3), (0, 0, 1)], [(1, 0, 2)]]
BAND = [[(1, 0, 2), (2, 1, 2)], [(3, 2, 2), (0, 0, 1)]]
KEYS = [[0], [1, 3], [2]]
KEY_COLS = {0: 0, 1: 512, 3: 896, 2: 1024}
POS = {3: 0, 2: 1, 0: 2, 1: 3}


def rel_bucket_of(dist, max_distance):
    half = 16
    d = np.maximum(dist, 0)
    ratio = np.log(np.maximum(d, half).astype(np.float32) / np.float32(half)).astype(np.float32)
    large = half + (ratio / np.float32(np.log(max_distance / half)) * np.float32(half)).astype(np.int32)
    return np.where(d < half, d, np.minimum(large, 31))


def one_hot(dist, valid, max_distance):
    out = np.zeros((33, len(dist)), np.float32)
    b = rel_bucket_of(dist, max_distance)
    out[b[valid], np.nonzero(valid)[0]] = 1.0
    out[32, ~valid] = MASK
    return out


def constants():
    i = np.arange(P)
    tri = (i[:, None] <= i[None, :]).astype(np.float32)
    d_full = 511 - np.arange(640)
    d_band = 255 - np.arange(384)
    d_cmp = np.arange(1024) - 511
    return {
        "ident": np.eye(P, dtype=np.float32),
        "tri_ones": np.concatenate([tri, np.ones((P, 384), np.float32)], 1),
        "suffix": np.ascontiguousarray(tri.T),
        "causal": np.where(i[None, :] > i[:, None], np.float32(MASK), np.float32(0)),
        "strict": np.where(i[:, None] >= i[None, :], np.float32(MASK), np.float32(0)),
        "hot_full": one_hot(d_full, d_full >= 0, 1024),
        "hot_band": one_hot(d_band, (d_band >= 0) & (d_band < 128), 1024),
        "hot_t5": one_hot(d_full, d_full >= 0, 128),
        "hot_cmp": one_hot(d_cmp, d_cmp >= 0, 128),
    }


def slots_and_groups():
    groups, first = [], {}
    s = 0
    for phase, chunks in (("in1", CHUNKS1), ("out1", W_OUT), ("in2", CHUNKS2), ("out2", W_OUT)):
        for c, cols in enumerate(chunks):
            first[phase, c] = s
            for part in range(2):
                groups.append((phase, c, part, s, sum(w for _, w in cols)))
                s += 4
    for c in range(GU_CHUNKS):
        first["gu", c] = s
        for part in range(2):
            groups.append(("gu", c, part, s, 512))
            s += 4
    for g in range(DOWN_TILES // 2):
        first["down", 2 * g] = s
        first["down", 2 * g + 1] = s + 2
        groups.append(("down", g, 0, s, 512))
        s += 4
    return groups, first, s


def halves(phase):
    return HALVES.get(phase, (0, 1))


def k_tile(phase, n):
    return 4 * halves(phase)[n // 4] + n % 4


def make_timeline(first, n_slots):
    tl = []

    def hi_lo(s):
        if s + 4 < n_slots:
            tl.append(("split", s + 4))

    def mm(phase, c, n, per=1):
        for j in range(per):
            hi_lo(first[phase, c] + n * per + j)
        tl.append(("mm", phase, c, n))

    queue = {n: [] for n in range(200)}
    order = []

    def at(tick, *steps):
        queue[tick] += list(steps)

    def softmax_head(tick, name, h, plan, lag_t=2, lag_o=4):
        for g in range(len(plan)):
            at(tick + g, ("S", name, h, g))
            at(tick + g + lag_t, ("T", name, h, g))
            at(tick + g + lag_o, ("O", name, h, g))

    for name, tick in (("fox", 8), ("moba", 24), ("swa", 48)):
        for t in range(NT):
            at(tick + t, ("qa", name, t))
            at(tick + t + 1, ("qb", name, t))
            at(tick + t + 2, ("qt", name, t))
    at(16, ("logf",))
    for h in range(4):
        at(17 + h, ("C", h))
    for t in range(NT):
        at(40 + t, ("qt", "sb", t))
    for h in range(4):
        softmax_head(18 + 3 * h, "fox", h, FULL)
        softmax_head(30 + 3 * h, "moba", h, FULL)
        a = 46 + 3 * h
        for g in range(3):
            at(a + g, ("Z", h, g))
            at(a + g + 4, ("F", h, g))
        at(a + 2, ("sp", h))
        at(a + 3, ("sp_b", h))
        at(a + 7, ("OS", h))
        softmax_head(60 + 2 * h, "swa", h, BAND)
    rank = {"OS": 0, "O": 0, "T": 1, "F": 2, "S": 3, "Z": 3, "sp": 4, "sp_b": 1.5, "qb": -3, "qa": -2, "qt": 4.5, "logf": -4, "C": -3}

    def flush(tick, *product):
        steps = sorted(queue[tick], key=lambda x: rank[x[0]])
        tl.extend(x for x in steps if rank[x[0]] <= 1)
        if product:
            mm(*product)
        tl.extend(x for x in steps if rank[x[0]] > 1)
        queue[tick] = []

    def out_product(phase, after, begun):
        hf = halves(phase)[1]
        for c in range(2):
            for n in range(KD):
                if c == 0 and n == begun:
                    if after:
                        tl.extend(("gx", phase, t, hf) for t in range(2))
                    tl.append(("xt", phase, 0, hf))
                if c or n >= begun:
                    mm(phase, c, n)
                if c == 0 and n in (2, 3):
                    for t in ((1, 2), (3,))[n - 2]:
                        if after and t < 3:
                            tl.append(("gx", phase, t + 1, hf))
                        tl.append(("xt", phase, t, hf))
                if c == 1 and after:
                    if n == 3:
                        tl.extend(("gx", after, t, 0) for t in range(NT))
                    for t in {4: (0,), 5: (1, 2), 6: (3,)}.get(n, ()):
                        tl.append(("xt", after, t, 0))
            if phase == "out1" or c == 0:
                tl.append(("ev", phase, c))
            if phase == "out2" and c == 0:
                tl.extend(("sqa", t) for t in range(NT))

    tl.append(("gx", "in1", 0, 0))
    tl.append(("gx", "in1", 0, 1))
    for t in range(NT):
        for hf in range(2):
            if t + 1 < NT:
                tl.append(("gx", "in1", t + 1, hf))
            tl.append(("xt", "in1", t, hf))
        if t == 0:
            for s in range(4):
                tl.append(("split", s))
        if t == 1:
            tl.append(("rows",))
        tl.append(("sq", "in1", t))
    tl.append(("ms", "in1", 0))
    tl.append(("rows_out",))
    for c in range(len(CHUNKS1)):
        for k in range(KD):
            flush(8 * c + k, "in1", c, k)
            if 8 * c + k in (58, 59, 60, 61):
                tl.append(("gx", "out1", 8 * c + k - 58, 0))
        tl.append(("ev", "in1", c))
    begun = 2
    for tick in range(64, 80):
        if 67 <= tick < 67 + begun:
            flush(tick, "out1", 0, tick - 67)
        else:
            flush(tick)
        if tick in (64, 65):
            for t in (2 * (tick - 64), 2 * (tick - 64) + 1):
                tl.append(("xt", "out1", t, 0))
    out_product("out1", "in2", begun)
    tl.append(("windows",))

    for t in range(NT):
        at(8 + t, ("qt", "cmp", t), ("qt", "slc", t))
        at(16 + t, ("qt", "q", t))
        at(24 + t, ("qt", "win", t))
    at(13, ("blocks",))
    at(15, ("hidden", 0))
    at(20, ("hidden", 1))
    at(21, ("cmpkv",))
    at(24, ("gates",))
    rank.update({"blocks": 5, "hidden": 6, "cmpkv": 7, "gates": -5, "CS": 3, "CT": 1, "CO": 0})
    for i in range(NT):
        at(25 + i, ("CS", i))
        at(26 + i, ("CT", i))
        at(27 + i, ("CO", i))
    for h in range(16):
        softmax_head(29 + 3 * h, "slc" if h < 8 else "win", h % 8, FULL)
    rank.update({"gm_w": 8, "gm_b": 8, "gm_a": 9, "gm": 10})
    at(42, ("gm_w", 0))
    at(43, ("gm_w", 1))
    for t in range(NT):
        at(44 + t, ("gm_a", t))
        at(45 + t, ("gm_b", t))
    for u in range(4):
        at(49 + u, ("gm", u))
    for c in range(len(CHUNKS2)):
        for k in range(KD):
            if c == 0 and k == 0:
                tl.extend([("gx", "in2", 0, 1), ("gx", "in2", 1, 1)])
            flush(8 * c + k, "in2", c, k)
            if c == 0 and k < 3:
                for t in ((0,), (1,), (2, 3))[k]:
                    tl.append(("xt", "in2", t, 1))
                    if t < 2:
                        tl.append(("gx", "in2", t + 2, 1))
                if k == 2:
                    for t in range(NT):
                        tl.append(("sq", "in2", t))
                    tl.append(("ms", "in2", 0))
                    tl.append(("cmp_bias",))
        tl.append(("ev", "in2", c))
    begun = 0
    for tick in range(40, 200):
        if tick >= 64 and tick % 8 == 0 and begun < 2 and queue[tick]:
            flush(tick, "out2", 0, begun)
            begun += 1
        else:
            flush(tick)
        if 55 <= tick < 55 + NT:
            tl.append(("xt", "out2", tick - 55, 1))
    out_product("out2", None, begun)
    mix = [[("sq", "mix", t), ("ms", "mix", t)] for t in range(NT)]
    post = [[("post", "mix", t)] for t in range(NT)]
    sq_gu = [[("sq", "gu", t), ("ms", "gu", t)] for t in range(NT)]
    gx_gu = [[("gx", "gu", t, 0), ("gx", "gu", t, 1)] for t in range(NT)]
    for steps in (mix[0], mix[1], post[0], mix[2], mix[3], post[1], sq_gu[0], post[2], sq_gu[1], gx_gu[0], post[3], sq_gu[2]):
        tl.extend(steps)
    for t in range(NT):
        for hf in range(2):
            if t + 1 < NT:
                tl.append(gx_gu[t + 1][hf])
            tl.append(("xt", "gu", t, hf))
        if t == 0:
            tl.extend(sq_gu[3])
    for c in range(GU_CHUNKS):
        for k in range(KD):
            mm("gu", c, k)
        tl.append(("ev", "gu", c))
    for kt in range(2):
        tl.append(("act", kt))
    for kt in range(DOWN_TILES):
        if kt + 2 < DOWN_TILES:
            tl.append(("act", kt + 2))
        mm("down", kt, 0, 2)
    ffn = [[("sq", "ffn", t), ("ms", "ffn", t)] for t in range(NT)]
    post = [[("post", "ffn", t)] for t in range(NT)]
    for steps in (ffn[0], ffn[1], post[0], ffn[2], post[1], ffn[3], post[2], post[3]):
        tl.extend(steps)
    return tl


def hybrid_two_block_kernel(nc, a, c, out):
    groups, first, n_slots = slots_and_groups()
    timeline = make_timeline(first, n_slots)

    nth, seen = {}, {}

    def kind(step):
        k = step[0]
        return {"S": "sc", "Z": "sc", "C": "sc", "CS": "sc", "hidden": "sc", "gm": "sc", "cmpkv": "sc",
                "T": "tr", "F": "tr", "CT": "tr", "qt": "tr", "gm_w": "tr",
                "OS": "o", "O": "o", "CO": "o", "qa": "ms", "gm_a": "ms"}.get(k, k)

    def by_pool(step):
        return step[1] == "in1" and step[3] == 1

    for step in timeline:
        k_ = "gx_pool" if step[0] == "gx" and by_pool(step) else kind(step)
        nth[step] = seen.get(k_, 0)
        seen[k_] = nth[step] + 1

    with ExitStack() as ctx:
        def sem(name):
            return ctx.enter_context(nc.semaphore(name))

        BASE = 16512

        def at(name, kb, shape, dtype=F32):
            return nc.alloc_sbuf_tensor_at(name, [P] + shape, dtype, offset=BASE + int(kb * 1024))

        XT = at("XT", 0, [KD, 2, SEQ], F32R)
        WR = at("WR", 32, [RING, 2, 512], F32R)
        RAW = at("RAW", 56, [2, 4, 512])
        R1 = at("R1", 72, [NT, D])
        R2 = at("R2", 88, [NT, D])
        ident = at("ident_sb", 104, [P])
        identb = at("identb", 104.5, [P], BF16)
        causal = at("causal_sb", 104.75, [P], BF16)
        strict = at("strict_sb", 105, [P], BF16)
        tri = at("tri_sb", 105.25, [512])
        suffix = at("suffix_sb", 107.25, [P])
        gain = [at("gain0", 107.75, [D]), at("gain1", 111.75, [D])]
        sq = at("sq", 115.75, [512])
        st = at("st", 117.75, [560])
        cmp_bias = at("cmp_bias", 120, [NT, 8, 32])
        prob = at("prob", 124, [2, 1280])
        squares = at("squares", 124, [NT, 640])[:, :, 0:512]
        probT = at("probT", 134, [1280])
        V1 = at("V1", 139, [NT, 896])
        qk_nat = at("qk_nat", 153, [NT, 512])
        qkT1 = at("qkT1", 161, [2, 4, SEQ])
        bias_moba = at("bias_moba", 177, [4, 512])
        bias_swa = at("bias_swa", 185, [4, 256])
        fox_c = at("fox_c", 189, [4, 512])
        soft = at("soft", 189, [2, 1280])
        x_again = at("x_again", 161, [NT, D])
        hots = at("hots", 161, [1664])
        hot_cmp = at("hot_cmp", 179, [1024])
        rows = at("rows", 199, [1664])
        stage = at("stage", 197.5, [384])
        V2 = at("V2", 139, [NT, 2, P])
        hot_parts = at("hot_parts", 183, [1024], F32R)
        tab_parts = at("tab_parts", 117.75 + 560 / 256, [16], F32R)
        nat2 = at("nat2", 143, [NT, 512])
        cmp_nat = at("cmp_nat", 151, [NT, 4, P])
        zv = at("zv", 151, [NT, 512])
        hidT = at("hidT", 151, [2, 2, 64])
        hidV = at("hidV", 152, [2, 2, P])
        w1 = at("w1", 159, [16, 256])
        qT2 = at("qT2", 175, [4, SEQ])
        kT2 = at("kT2", 183, [2, 2, SEQ])
        bias_t5 = at("bias_t5", 191, [8, 512])
        cmpT = at("cmpT", 72, [2, 2, SEQ])
        blocks = at("blocks", 80, [2, 16, 64])
        vbd = at("vbd", 111.75, [2, 4, HD])
        w2k = at("w2k", 113.75, [2, P])
        w2v = at("w2v", 114.75, [2, HD])
        kcT = at("kcT", 115.25, [2, 2, 32])
        ws_nat = at("ws_nat", 0, [8, P])
        wsT = at("wsT", 4, [8, P])
        ln_g = at("ln_g", 8, [512])
        ln_b = at("ln_b", 10, [512])
        gated = at("gated", 120, [2, 512])
        actT = at("actT", 124, [DOWN_TILES, SEQ])

        half = st[:, 0:4]
        qk_gain = st[:, 4:10]
        pos = st[:, 10:42]
        gmlp_b = st[:, 42:50]
        b_forget = st[:, 50:54]
        sinks = st[:, 54:58]
        ss = st[:, 58:62]
        rr = st[:, 62:66]
        ms8 = st[:, 66:74]
        rr8 = st[:, 74:82]
        lf = st[:, 82:98]
        lf_a = st[:, 98:114]
        lf_u = st[:, 114:130]
        mx = st[:, 130:146]
        nm = st[:, 146:162]
        sm = st[:, 162:178]
        es = st[:, 178:194]
        ri = st[:, 194:210]
        gates = st[:, 210:306]
        g_tmp = st[:, 306:402]
        cm8 = st[:, 402:410]
        cs8 = st[:, 410:418]
        cf8 = st[:, 418:450]
        tab1 = st[:, 450:458]
        tab2 = st[:, 458:466]
        negmu = st[:, 466:470]
        ss_a = st[:, 470:474]

        psum = ctx.enter_context(nc.psum_tensor("psum", [P, 8, 512], F32))
        MM = [psum[:, i, :] for i in range(4)]
        SC = [psum[:, 4, :], psum[:, 5, :]]
        TR = psum[:, 6, :]
        OB = psum[:, 7, :]
        XB = [psum[:, 4 + i, :] for i in range(4)]
        WINDOWS = psum[:, 6:8, :].rearrange("p b n -> p (b n)")
        SET = [[psum[:, i, :] for i in range(4)], [psum[:, 4 + i, :] for i in range(4)]]

        rows_d = nc.dram_tensor("rows_scratch", [20, 640], F32, kind="Internal").ap()
        rep_d = nc.dram_tensor("rep_scratch", [20, P, 640], F32, kind="Internal").ap()
        repb_d = nc.dram_tensor("repb_scratch", [4, P, 384], F32, kind="Internal").ap()

        s_x = [sem(f"x_landed{t}") for t in range(NT)]
        s_gain = sem("gain_landed")
        s_const = sem("consts_landed")
        s_tab = sem("tables_landed")
        s_raw = [sem("raw_landed0"), sem("raw_landed1")]
        s_rows = sem("rows_stored")
        s_rep = sem("rows_replicated")
        s_bias1 = sem("bias1_landed")
        s_bias2 = sem("bias2_landed")
        s_xa = sem("x_again_landed")
        s_w1 = sem("w1_landed")
        s_small2 = sem("small2_landed")
        s_gm_in = sem("gmlp_in_landed")
        s_out = sem("out_stored")
        w_hi = sem("w_hi")
        w_lo = sem("w_lo")
        w_used = sem("w_used")
        s_ident = sem("ident_landed")
        ev_act = sem("ev_act")
        ev_dve = sem("ev_dve")
        v_chain = sem("dve_chain")
        a_chain = sem("act_chain")
        p_chain = sem("pool_chain")
        ms_ready = sem("mean_square_ready")
        r_ready = sem("rsqrt_ready")
        sq_done = sem("squares_summed")
        sqa_done = sem("first_squares_summed")
        gx_done = sem("rows_times_gain")
        gx_pool = sem("rows_times_gain_by_pool")
        hot_r = sem("cmp_hots_copied")
        post_dve = sem("post_by_dve")
        post_lo = sem("post_scaled")
        post_pool = sem("post_by_pool")
        xt_in = sem("xt_transposed")
        xt_hi = sem("xt_hi")
        xt_lo = sem("xt_lo")
        qn_done = sem("qk_normed")
        s_cmp = sem("cmp_hots_landed")
        cmp_in = sem("cmp_bias_in_psum")
        cmp_out = sem("cmp_bias_ready")
        sc_in = sem("scores_in_psum")
        sc_out = sem("scores_out_of_psum")
        tr_in = sem("transposes_in_psum")
        tr_out = sem("transposes_out_of_psum")
        o_in = sem("o_in_psum")
        o_out = sem("o_out_of_psum")
        e_done = sem("exp_done")
        lf_pre = sem("logf_abs")
        lf_act = sem("logf_ln")
        lf_done = sem("logf_done")
        sp_abs = sem("sp_abs")
        sp_ln = sem("sp_ln")
        sp_done = sem("sp_done")
        w_sub = sem("sb_weights_sub")
        a_done = sem("sb_weights_exp")
        tab_done = sem("tables_in_psum")
        tab_out = sem("tables_out")
        setup_dve = sem("setup_dve")
        blk_done = sem("blocks_done")
        hid_act = sem("hidden_gelu")
        hid_rep = sem("hidden_replicated")
        gate_e = sem("gate_exp")
        cs_sub = sem("cmp_sub")
        cs_exp = sem("cmp_exp")
        gm_w = sem("gm_weights_ready")
        gm_n = sem("gm_norm_ready")
        act_hi = sem("act_hi")
        act_lo = sem("act_lo")
        gs_done = sem("gate_silu")

        def group_cols(phase, chunk):
            return {"in1": CHUNKS1, "out1": W_OUT, "in2": CHUNKS2, "out2": W_OUT}[phase][chunk]

        weights = {"in1": a["w_in"], "out1": a["w_out"], "in2": a["w_in_2"], "out2": a["w_out_2"],
                   "gu": a["w_gate_up_2"], "down": a["w_down_2"]}

        def evac_engine(phase, chunk, t):
            if (phase, chunk) in (("in1", 6), ("in1", 7), ("in2", 3), ("in2", 4)):
                return "act"
            if phase == "out1":
                return "dve"
            return "act" if t % 2 == 0 else "dve"

        ev_count = {}
        n_act = n_dve = 0
        for step in timeline:
            if step[0] == "ev":
                if step[1] == "gu":
                    n_dve += 1
                else:
                    for t in range(NT):
                        if evac_engine(step[1], step[2], t) == "act":
                            n_act += 1
                        else:
                            n_dve += 1
                ev_count[step] = (n_act, n_dve)

        def wait_evacuated(eng, step):
            eng.wait_ge(ev_act, ev_count[step][0])
            eng.wait_ge(ev_dve, ev_count[step][1])

        HEADS = {"fox": (FULL, 4), "moba": (FULL, 4), "swa": (BAND, 4), "slc": (FULL, 8), "win": (FULL, 8)}

        def prev_head(name, h):
            if h:
                return (name, h - 1)
            return {"fox": None, "moba": ("fox", 3), "swa": ("sb", 3), "slc": ("cmp", 3), "win": ("slc", 7)}[name]

        def last_o(head):
            name, h = head
            if name == "sb":
                return ("OS", h)
            if name == "cmp":
                return ("CO", h)
            return ("O", name, h, len(HEADS[name][0]) - 1)

        def head_index(name, h):
            return {"fox": 0, "moba": 4, "swa": 12, "slc": 0, "win": 8}[name] + h

        def segments(plan, g):
            col = 0
            n = sum(len(x) for x in plan[:g])
            for i, j, m in plan[g]:
                yield i, j, m, col, n
                col += m * P
                n += 1

        def width(plan, g):
            return P * sum(m for _, _, m in plan[g])

        GROUP_AT = [0, 512, 1024]
        KINDS1 = {"fox": 0, "moba": 1, "sb": 2, "swa": 3}

        def q_of(name, h):
            e = 64 * (h % 2)
            if name in KINDS1:
                return qkT1[e:e + 64, KINDS1[name] % 2, h // 2, :]
            return qT2[e:e + 64, h // 2, :]

        def k_of(name, h):
            e = 64 * (h % 2)
            if name in KINDS1:
                return qkT1[e:e + 64, KINDS1[name] % 2, 2 + h // 2, :]
            return kT2[e:e + 64, 0 if name == "slc" else 1, h // 4, :]

        def v_of(name, h, j):
            if name in ("slc", "win"):
                return V2[:, j, 0 if name == "slc" else 1, :], h // 4
            if name == "swa":
                return V1[:, j, 768:896], h // 2
            lo = 256 * KINDS1[name] + P * (h // 2)
            return V1[:, j, lo:lo + P], h % 2

        def bias_of(name, h, i, m):
            if name == "fox":
                return fox_c[:, h, 0:m * P]
            if name == "moba":
                return bias_moba[:, h, 384 - P * i:512]
            if name == "swa":
                return bias_swa[:, h, 256 - m * P:256]
            return bias_t5[:, h, 384 - P * i:512]

        def q_ready(name):
            return {"slc": ("qt", "q", 3), "win": ("qt", "win", 3)}.get(name, ("qt", name, 3))

        e_index = {}
        for step in timeline:
            if step[0] == "S":
                e_index[step[1:]] = len(e_index) + 1

        def evacuate(eng, phase, ch, t):
            act_ = eng is nc.scalar

            def copy(o, i):
                if phase == "out2":
                    return eng.activation(o, i, ACT.Copy) if act_ else eng.tensor_copy(o, i)
                r = rr[:, t:t + 1]
                return eng.activation(o, i, ACT.Copy, scale=r) if act_ else eng.tensor_scalar(o, i, r, None, ALU.mult)

            m = MM[t]
            if phase == "in1":
                if ch in (0, 2, 4):
                    yield copy(qk_nat[:, t, :], m)
                elif ch == 1:
                    yield copy(V1[:, t, 0:256], m[:, 0:256])
                    yield copy(lf_u[:, 4 * t:4 * t + 4], m[:, 256:260])
                elif ch == 3:
                    yield copy(V1[:, t, 256:768], m)
                elif ch == 5:
                    yield copy(qk_nat[:, t, 0:256], m[:, 0:256])
                    for e in range(2):
                        yield copy(qk_nat[:, t, 256:512].rearrange("p (g e d) -> p g e d", g=2, e=2)[:, :, e, :],
                                   m[:, 256:384].rearrange("p (g d) -> p g d", g=2))
                    yield copy(V1[:, t, 768:896], m[:, 384:512])
                elif ch == 6:
                    yield eng.activation(R1[:, t, 0:512], m, ACT.Silu, scale=rr[:, t:t + 1])
                elif ch == 7:
                    yield eng.activation(R1[:, t, 512:1024], m, ACT.Silu, scale=rr[:, t:t + 1])
            elif phase == "in2":
                if ch == 0:
                    for e in range(2):
                        yield copy(cmp_nat[:, t, :, HD * e:HD * e + HD], m[:, 0:256].rearrange("p (g d) -> p g d", g=4))
                        yield copy(nat2[:, t, 0:256].rearrange("p (g e d) -> p g e d", g=2, e=2)[:, :, e, :],
                                   m[:, 256:384].rearrange("p (g d) -> p g d", g=2))
                    yield copy(V2[:, t, 0, :], m[:, 384:512])
                elif ch == 1:
                    yield copy(nat2[:, t, :], m)
                elif ch == 2:
                    for e in range(2):
                        yield copy(nat2[:, t, 0:256].rearrange("p (g e d) -> p g e d", g=2, e=2)[:, :, e, :],
                                   m[:, 0:128].rearrange("p (g d) -> p g d", g=2))
                    yield copy(V2[:, t, 1, :], m[:, 128:256])
                    yield copy(g_tmp.rearrange("p (c q) -> p c q", q=4)[:, :, POS[t]], m[:, 256:280])
                elif ch == 3:
                    yield eng.activation(R1[:, t, 512:1024], m, ACT.Gelu_apprx_tanh, scale=rr[:, t:t + 1])
                elif ch == 4:
                    yield eng.activation(zv[:, t, :], m, ACT.Gelu_apprx_tanh, scale=rr[:, t:t + 1])
            elif phase == "out2":
                yield copy(R1[:, t, 512 * ch:512 * ch + 512], m)

        def xt_bank(step):
            _, phase, t, hf = step
            if (phase, hf) in (("in1", 0), ("in1", 1), ("out1", 0), ("out2", 1)):
                return ("mm", (2 * t + hf) % 4 if phase == "in1" else t)
            return ("xb", (2 * t + hf) % 4 if phase == "gu" else (t % 2 if phase == "in2" else t))

        xt_before, by_bank = {}, {}
        for step in timeline:
            if step[0] == "xt":
                xt_before[step] = by_bank.get(xt_bank(step))
                by_bank[xt_bank(step)] = step

        def wait_rows(eng, phase, hf, count):
            eng.wait_ge(count, nth["xt", phase, 3, hf] + 1)

        o_heads = {}
        n_heads = 0
        for step in timeline:
            if step[0] in ("O", "OS", "CO") and (step[0] != "O" or step == last_o((step[1], step[2]))):
                n_heads += 1
            o_heads[step] = n_heads

        o_total1 = o_heads[last_o(("swa", 3))]

        block = ctx.enter_context(nc.Block())

        @block.sync
        def _(sp):
            def bcast(dst, src, n):
                return sp.dma_start(dst, src.rearrange("o n -> o n").broadcast_to([P, n]))

            x_v = a["x"].rearrange("o (t p) d -> p (o t) d", p=P)
            raw_count = [0, 0]

            def load_group(g):
                phase, chunk, n_part, s0, w = groups[g]
                part = n_part if phase == "down" else halves(phase)[n_part]
                if g >= 2:
                    sp.wait_ge(w_lo, groups[g - 2][3] + 4)
                W = weights[phase]
                dst = RAW[:, g % 2, :, :]
                if phase == "down":
                    src = W[0, 256 * chunk:256 * chunk + 256, :].rearrange("(k p) (h n) -> p k h n", p=P, h=2)
                    sp.dma_start(dst.rearrange("p (k h) n -> p k h n", h=2), src).then_inc(s_raw[g % 2], 16)
                    raw_count[g % 2] += 16
                    return
                kk = W[0, 512 * part:512 * part + 512, :].rearrange("(k p) n -> p k n", p=P)
                cols = group_cols(phase, chunk) if phase != "gu" else [(256 * chunk, 256), (FF + 256 * chunk, 256)]
                col = 0
                for start, n in cols:
                    sp.dma_start(dst[:, :, col:col + n], kk[:, :, start:start + n]).then_inc(s_raw[g % 2], 16)
                    raw_count[g % 2] += 16
                    col += n

            def load_tables():
                sp.dma_start(tab1[0:32, :], a["rel_bias"]).then_inc(s_tab, 16)
                sp.dma_start(tab2[0:32, :], a["rel_bias_2"]).then_inc(s_tab, 16)
                for name, lo, n in (("hot_full", 0, 640), ("hot_band", 640, 384), ("hot_t5", 1024, 640)):
                    sp.dma_start(hots[0:33, lo:lo + n], c[name]).then_inc(s_tab, 16)

            def small_loads():
                sp.dma_start(tri[:, :], c["tri_ones"]).then_inc(s_const, 16)
                sp.dma_start(suffix[:, :], c["suffix"]).then_inc(s_const, 16)
                sp.dma_start(stage[:, 0:128], c["causal"]).then_inc(s_const, 16)
                sp.dma_start(stage[:, 128:256], c["strict"]).then_inc(s_const, 16)
                with nc.allow_non_contiguous_dma(reason="gains as columns: a few hundred words, once"):
                    for n, name in enumerate(("fox_qk_gain", "moba_qk_gain", "swa_qk_gain")):
                        for e in range(2):
                            sp.dma_start(qk_gain[64 * e:64 * e + 64, 2 * n:2 * n + 2],
                                         a[name].rearrange("o j d -> d (o j)")).then_inc(s_const, 16)
                bcast(b_forget, a["b_forget"], 4).then_inc(s_const, 16)
                bcast(sinks, a["sinks"], 4).then_inc(s_const, 16)

            def store_rows():
                sp.wait_ge(tab_out, 4)
                sp.dma_start(rows_d[0:4, 0:640], rows[0:4, 0:640]).then_inc(s_rows, 16)
                sp.dma_start(rows_d[4:8, 0:384], rows[4:8, 640:1024]).then_inc(s_rows, 16)
                sp.dma_start(rows_d[8:16, 0:640], rows[0:8, 1024:1664]).then_inc(s_rows, 16)

            def replicate_rows():
                sp.wait_ge(s_rows, 48)
                for lo, n in ((0, 4), (8, 8)):
                    for h in range(lo, lo + n):
                        sp.dma_start(rep_d[h], rows_d[h:h + 1, :].broadcast_to([P, 640])).then_inc(s_rep, 16)
                for h in range(4):
                    sp.dma_start(repb_d[h], rows_d[4 + h:5 + h, 0:384].broadcast_to([P, 384])).then_inc(s_rep, 16)

            def skewed(dst, rep, h, n, pitch):
                return sp.dma_start(dst, bass.AP(rep.tensor, h * P * pitch + P - 1, [[pitch - 1, P], [1, n]]))

            def load_bias1():
                sp.wait_ge(s_rep, 16 * 16)
                for h in range(4):
                    skewed(bias_moba[:, h, :], rep_d, h, 512, 640).then_inc(s_bias1, 16)
                for h in range(4):
                    skewed(bias_swa[:, h, :], repb_d, h, 256, 384).then_inc(s_bias1, 16)

            def load_bias2():
                sp.wait_ge(tr_in, nth["F", 3, 2] + 1)
                sp.wait_ge(sp_done, 4)
                for h in range(8):
                    skewed(bias_t5[:, h, :], rep_d, 8 + h, 512, 640).then_inc(s_bias2, 16)

            def load_hot_cmp():
                sp.wait_ge(sc_out, nth["S", "moba", 3, 2] + 1)
                sp.dma_start(hot_cmp[0:33, :], c["hot_cmp"]).then_inc(s_cmp, 16)

            def load_x_again():
                sp.wait_ge(sc_in, nth["S", "swa", 3, 1] + 1)
                sp.dma_start(x_again[:, :, :], x_v).then_inc(s_xa, 16)

            def load_w1(which):
                if which == "k":
                    wait_evacuated(sp, ("ev", "out1", 1))
                else:
                    sp.wait_ge(sc_in, nth["hidden", 0] + 1)
                src = a[f"cmp_w1_{which}_2"]
                sp.dma_start(w1[:, :, :], src.rearrange("o (m p) f -> p (o m) f", p=P)).then_inc(s_w1, 16)

            def load_small2():
                for e in range(2):
                    sp.dma_start(w2k[:, :, 64 * e:64 * e + 64],
                                 a["cmp_w2_k_2"].rearrange("o (f p) d -> p (o f) d", p=P)).then_inc(s_small2, 16)
                sp.dma_start(w2v[:, :, :], a["cmp_w2_v_2"].rearrange("o (f p) d -> p (o f) d", p=P)).then_inc(s_small2, 16)
                with nc.allow_non_contiguous_dma(reason="position rows as columns, once"):
                    for n, name in enumerate(("cmp_pos_k_2", "cmp_pos_v_2")):
                        v = a[name].rearrange("o (m e) d -> e d (o m)", e=2)
                        for e in range(2):
                            sp.dma_start(pos[64 * e:64 * e + 64, 16 * n:16 * n + 16], v[e]).then_inc(s_small2, 16)
                    sp.dma_start(gmlp_b, a["gmlp_b_s_2"].rearrange("o g t -> t (o g)")).then_inc(s_small2, 16)

            def load_gmlp():
                sp.wait_ge(w_used, first["in2", 4] + KD)
                sp.dma_start(ws_nat[:, :, :], a["gmlp_w_s_2"].rearrange("o g t s -> t (o g) s")).then_inc(s_gm_in, 16)
                bcast(ln_g[:, :], a["gmlp_ln_g_2"], 512).then_inc(s_gm_in, 16)
                bcast(ln_b[:, :], a["gmlp_ln_b_2"], 512).then_inc(s_gm_in, 16)

            def load_gain(n, name, pre):
                if pre is not None:
                    sp.wait_ge(pre[0], pre[1])
                bcast(gain[n][:, :], a[name], D).then_inc(s_gain, 16)

            index = {(phase, chunk, part): g for g, (phase, chunk, part, _, _) in enumerate(groups)}
            before = {
                index["in1", 1, 0]: [small_loads],
                index["in1", 1, 1]: [store_rows],
                index["in1", 2, 0]: [replicate_rows],
                index["in1", 2, 1]: [load_bias1],
                index["in1", 4, 0]: [load_small2],
                index["out1", 0, 0]: [lambda: load_gain(0, "norm_mix_pre_2", (gx_pool, NT)),
                                      load_hot_cmp],
                index["out1", 1, 0]: [load_x_again, load_bias2],
                index["in2", 1, 0]: [lambda: load_w1("k")],
                index["in2", 3, 0]: [lambda: load_w1("v"),
                                     lambda: load_gain(0, "norm_ffn_pre_2", (gx_done, nth["gx", "in2", 3, 1] + 1))],
                index["out2", 1, 0]: [load_gmlp, lambda: load_gain(1, "norm_mix_post_2", (o_in, nth["CO", 3] + 1))],
                index["gu", 2, 0]: [lambda: load_gain(1, "norm_ffn_post_2", (post_dve, NT))],
            }
            sp.dma_start(R1[:, 0, :], x_v[:, 0, :]).then_inc(s_x[0], 16)
            bcast(gain[0][:, :], a["norm_gain"], D).then_inc(s_gain, 16)
            sp.dma_start(ident[:, :], c["ident"]).then_inc(s_ident, 16)
            load_tables()
            for t in range(1, NT):
                sp.dma_start(R1[:, t, :], x_v[:, t, :]).then_inc(s_x[t], 16)
            for g in range(len(groups)):
                for f in before.get(g, []):
                    f()
                load_group(g)
            out_v = out.rearrange("o (t p) d -> p (o t) d", p=P)
            for t in range(NT):
                sp.wait_ge(post_dve, NT + t + 1)
                sp.wait_ge(post_pool, NT + t + 1)
                sp.dma_start(out_v[:, t, :], R2[:, t, :]).then_inc(s_out, 16)
            sp.wait_ge(s_rows, 48)
            sp.wait_ge(s_rep, 256)
            sp.wait_ge(s_out, 16 * NT)

        @block.tensor
        def _(pe):
            def product(outp, stationary, moving, start, stop):
                for n, (x, y) in enumerate(((0, 0), (0, 1), (1, 0))):
                    last = pe.matmul(outp, stationary(x), moving(y), start=start and n == 0, stop=stop and n == 2)
                return last

            def distance_rows():
                pe.wait_ge(s_tab, 80)
                pe.wait_ge(setup_dve, 1)
                for n, (bank, table) in enumerate(((SC[0], tab1), (SC[1], tab1), (TR, tab2), (OB, tab2))):
                    lo, hi = (0, 512, 1024, 1536, 1664)[n:n + 2]
                    pe.matmul(bank[0:8, 0:hi - lo], table[0:33, :], hots[0:33, lo:hi], start=True, stop=True).then_inc(tab_done, 1)

            def wait_tr(step):
                if nth[step]:
                    pe.wait_ge(tr_out, nth[step])
                else:
                    pe.wait_ge(tab_out, 3)

            def wait_sc(step):
                if nth[step] >= 2:
                    pe.wait_ge(sc_out, nth[step] - 1)

            for step in timeline:
                what = step[0]
                if what == "rows":
                    distance_rows()
                elif what == "windows":
                    pe.wait_ge(hot_r, 1)
                    pe.wait_ge(tr_out, nth["T", "swa", 3, 1] + 1)
                    pe.wait_ge(o_out, o_total1)
                    pe.wait_ge(xt_lo, nth["xt", "out1", 3, 1] + 1)
                    for u in range(55):
                        at_ = 864 - 16 * u
                        last = pe.matmul(WINDOWS[:, 16 * u:16 * u + 16], hot_parts[0:33, at_:at_ + P], tab_parts[0:33, :],
                                         start=True, stop=True)
                    last.then_inc(cmp_in, 1)
                elif what == "xt":
                    _, phase, t, hf = step
                    kind_, i = xt_bank(step)
                    bank = MM[i] if kind_ == "mm" else XB[i]
                    if xt_before[step]:
                        pe.wait_ge(xt_lo, nth[xt_before[step]] + 1)
                    if t == 0:
                        if phase == "in1":
                            pe.wait_ge(s_ident, 16)
                        elif (phase, hf) == ("out1", 0):
                            wait_evacuated(pe, ("ev", "in1", 7))
                        elif (phase, hf) == ("out2", 1):
                            wait_evacuated(pe, ("ev", "in2", 4))
                            pe.wait_ge(sc_out, nth["gm", 3] + 1)
                        elif (phase, hf) == ("out1", 1):
                            pe.wait_ge(tr_out, nth["T", "swa", 3, 1] + 1)
                            pe.wait_ge(sc_out, nth["S", "swa", 3, 1] + 1)
                            pe.wait_ge(o_out, o_total1)
                        elif (phase, hf) == ("out2", 0):
                            pe.wait_ge(tr_out, seen["tr"])
                            pe.wait_ge(sc_out, seen["sc"])
                            pe.wait_ge(o_out, n_heads)
                    if phase == "out2":
                        src = R1[:, t, :]
                    else:
                        pe.wait_ge(gx_pool if by_pool(step) else gx_done, nth["gx", phase, t, hf] + 1)
                        src = {"in1": R2, "out1": R2, "in2": R1, "gu": R1}[phase][:, t, :]
                    for q in range(4):
                        k = 4 * hf + q
                        last = pe.transpose(bank[:, P * q:P * q + P], src[:, P * k:P * k + P], ident[:, :])
                    last.then_inc(xt_in, 1)
                elif what == "mm":
                    _, phase, ch, n = step
                    s = first[phase, ch] + n
                    if phase == "down":
                        s = first[phase, ch]
                        pe.wait_ge(w_lo, s + 2)
                        pe.wait_ge(act_lo, ch + 1)
                        if ch == 0:
                            wait_evacuated(pe, ("ev", "gu", GU_CHUNKS - 1))
                        order = [(hf, t) for hf in range(2) for t in range(NT)]
                        if ch == DOWN_TILES - 1:
                            order = [(hf, t) for t in range(NT) for hf in range(2)]
                        for hf, t in order:
                            last = product(SET[hf][t], lambda x, t=t: XT[:, ch % 8, x, P * t:P * t + P],
                                           lambda y, hf=hf: WR[:, (s + hf) % RING, y, :],
                                           ch == 0, ch == DOWN_TILES - 1)
                            if (t == NT - 1) if ch < DOWN_TILES - 1 else (hf == 1):
                                last.then_inc(w_used, 1)
                        continue
                    k = k_tile(phase, n)
                    pe.wait_ge(w_lo, s + 1)
                    if ch == 0 and n % 4 == 0:
                        wait_rows(pe, phase, 1 if phase == "in1" else halves(phase)[n // 4], xt_lo)
                    if phase == "gu" and n == 0:
                        if ch == 0:
                            pe.wait_ge(post_dve, NT)
                        if ch >= 2:
                            wait_evacuated(pe, ("ev", phase, ch - 2))
                    prev = ("ev", phase, ch - 1) if ch else {"in2": ("ev", "out1", 1)}.get(phase)
                    for t in range(NT):
                        if n == 0 and prev and phase != "gu":
                            who = evac_engine(prev[1], prev[2], t)
                            done = ev_count[prev][0 if who == "act" else 1]
                            mine = [u for u in range(NT) if evac_engine(prev[1], prev[2], u) == who]
                            pe.wait_ge(ev_act if who == "act" else ev_dve, done - len(mine) + mine.index(t) + 1)
                        if phase == "gu":
                            last = product(SET[ch % 2][t], lambda x, t=t: WR[:, s % RING, x, P * t:P * t + P],
                                           lambda y: XT[:, k, y, :], n == 0, n == KD - 1)
                        else:
                            w = sum(n_ for _, n_ in group_cols(phase, ch))
                            last = product(MM[t][:, 0:w], lambda x, t=t: XT[:, k, x, P * t:P * t + P],
                                           lambda y: WR[:, s % RING, y, 0:w], n == 0, n == KD - 1)
                    last.then_inc(w_used, 1)
                elif what == "qt":
                    _, name, t = step
                    wait_tr(step)
                    tok = slice(P * t, P * t + P)
                    if name in KINDS1:
                        if name == "sb":
                            wait_evacuated(pe, ("ev", "in1", 4))
                        else:
                            pe.wait_ge(qn_done, nth["qb", name, t] + 1)
                        srcs = [qk_nat[:, t, P * q:P * q + P] for q in range(4)]
                    elif name == "cmp":
                        wait_evacuated(pe, ("ev", "in2", 0))
                        pe.wait_ge(cmp_out, 1)
                        srcs = [cmp_nat[:, t, q, :] for q in range(4)]
                    elif name == "q":
                        wait_evacuated(pe, ("ev", "in2", 1))
                        srcs = [nat2[:, t, P * q:P * q + P] for q in range(4)]
                    else:
                        wait_evacuated(pe, ("ev", "in2", 0 if name == "slc" else 2))
                        srcs = [nat2[:, t, P * q:P * q + P] for q in range(2)]
                    for q, src in enumerate(srcs):
                        last = pe.transpose(TR[:, P * q:P * q + P], src, ident[:, :])
                    last.then_inc(tr_in, 1)
                elif what == "C":
                    h = step[1]
                    wait_sc(step)
                    if h == 0:
                        pe.wait_ge(lf_done, 1)
                        pe.wait_ge(tab_out, 2)
                    for kb in range(NT):
                        last = pe.matmul(SC[nth[step] % 2][:, P * kb:SEQ], lf[:, 4 * kb + h:4 * kb + h + 1].broadcast_to([P, P]),
                                         tri[:, 0:SEQ - P * kb], start=kb == 0, stop=True, skip_group_check=True)
                    last.then_inc(sc_in, 1)
                elif what == "S":
                    _, name, h, g = step
                    plan = HEADS[name][0]
                    wait_sc(step)
                    if h == 0 and g == 0:
                        pe.wait_ge(tr_out, nth[q_ready(name)] + 1)
                        if name == "fox":
                            pe.wait_ge(setup_dve, 3)
                    bank = SC[nth[step] % 2]
                    for i, j, m, col, n in segments(plan, g):
                        last = pe.matmul(bank[:, col:col + m * P], q_of(name, h)[:, P * i:P * i + P],
                                         k_of(name, h)[:, P * j:P * (j + m)], start=True, stop=True)
                        if name == "fox":
                            d = col + (m - 1) * P
                            last = pe.matmul(bank[:, d:d + P], identb[:, :], causal[:, :], start=False, stop=True, skip_group_check=True)
                    last.then_inc(sc_in, 1)
                elif what == "T":
                    _, name, h, g = step
                    plan = HEADS[name][0]
                    wait_tr(step)
                    pe.wait_ge(e_done, e_index[name, h, g])
                    buf = prob[:, head_index(name, h) % 2, GROUP_AT[g]:GROUP_AT[g] + width(plan, g)]
                    for q in range(width(plan, g) // P):
                        last = pe.transpose(TR[:, P * q:P * q + P], buf[:, P * q:P * q + P], ident[:, :])
                    last.then_inc(tr_in, 1)
                elif what == "O":
                    _, name, h, g = step
                    plan = HEADS[name][0]
                    pe.wait_ge(tr_out, nth["T", name, h, g] + 1)
                    if g == 0:
                        if name == "fox" and h == 0:
                            wait_evacuated(pe, ("ev", "in1", 1))
                            pe.wait_ge(tab_out, 4)
                        elif o_heads[step]:
                            pe.wait_ge(o_out, o_heads[step])
                        if name == "moba" and h == 0:
                            wait_evacuated(pe, ("ev", "in1", 3))
                        if name == "swa" and h == 0:
                            wait_evacuated(pe, ("ev", "in1", 5))
                        if name == "slc" and h == 0:
                            wait_evacuated(pe, ("ev", "in2", 0))
                        if name == "win" and h == 0:
                            wait_evacuated(pe, ("ev", "in2", 2))
                    for i, j, m, col, n in segments(plan, g):
                        for b in range(m):
                            at_ = GROUP_AT[g] + col + b * P
                            last = pe.matmul(OB[:, P * n:P * n + P], probT[:, at_:at_ + P], v_of(name, h, j + b)[0],
                                             start=b == 0, stop=b == m - 1)
                    last.then_inc(o_in, 1)
                elif what == "Z":
                    _, h, g = step
                    wait_sc(step)
                    if h == 0 and g == 0:
                        pe.wait_ge(tr_out, nth["qt", "sb", 3] + 1)
                    bank = SC[nth[step] % 2]
                    for j in KEYS[g]:
                        col = KEY_COLS[j] - GROUP_AT[g]
                        w = SEQ - P * j
                        pe.matmul(bank[:, col:col + w], k_of("sb", h)[:, P * j:P * j + P], q_of("sb", h)[:, P * j:SEQ],
                                  start=True, stop=True)
                        last = pe.matmul(bank[:, col:col + P], identb[:, :], strict[:, :], start=False, stop=True, skip_group_check=True)
                    last.then_inc(sc_in, 1)
                elif what == "F":
                    _, h, g = step
                    wait_tr(step)
                    pe.wait_ge(sp_done, h + 1)
                    for j in KEYS[g]:
                        col = KEY_COLS[j] - GROUP_AT[g]
                        for jj in range(j, NT):
                            w = SEQ - P * jj
                            off = P * (jj - j)
                            last = pe.matmul(TR[:, col + off:col + off + w], suffix[:, :] if jj == j else tri[:, P:2 * P],
                                             soft[:, h % 2, KEY_COLS[jj]:KEY_COLS[jj] + w], start=jj == j, stop=True,
                                             skip_group_check=True)
                    last.then_inc(tr_in, 1)
                elif what == "OS":
                    h = step[1]
                    pe.wait_ge(a_done, 3 * h + 3)
                    pe.wait_ge(o_out, o_heads[step] - 1)
                    if h == 0:
                        wait_evacuated(pe, ("ev", "in1", 3))
                    for i in range(NT):
                        for j in range(i + 1):
                            at_ = KEY_COLS[j] + P * (i - j)
                            last = pe.matmul(OB[:, P * i:P * i + P], probT[:, at_:at_ + P], v_of("sb", h, j)[0],
                                             start=j == 0, stop=j == i)
                    last.then_inc(o_in, 1)
                elif what == "hidden":
                    kv = step[1]
                    wait_sc(step)
                    pe.wait_ge(s_w1, 16 * (kv + 1))
                    pe.wait_ge(blk_done, 1)
                    for f in range(2):
                        for m in range(16):
                            last = pe.matmul(SC[nth[step] % 2][:, 64 * f:64 * f + 64], w1[:, m, P * f:P * f + P],
                                             blocks[:, kv, m, :], start=m == 0, stop=m == 15)
                    last.then_inc(sc_in, 1)
                elif what == "cmpkv":
                    wait_sc(step)
                    pe.wait_ge(hid_rep, 1)
                    pe.wait_ge(hid_act, 2)
                    pe.wait_ge(s_small2, 16 * 8)
                    bank = SC[nth[step] % 2]
                    for f in range(2):
                        pe.matmul(bank[:, 0:64], w2k[:, f, :], hidT[:, 0, f, :], start=f == 0, stop=f == 1)
                    for g in range(2):
                        for f in range(2):
                            last = pe.matmul(bank[:, 64 + 64 * g:128 + 64 * g], hidV[:, f, g, :], w2v[:, f, :], start=f == 0, stop=f == 1)
                    last.then_inc(sc_in, 1)
                elif what == "CS":
                    i = step[1]
                    wait_sc(step)
                    if i == 0:
                        pe.wait_ge(sc_out, nth["cmpkv",] + 1)
                        pe.wait_ge(tr_out, nth["qt", "q", 3] + 1)
                    for pair in range(4):
                        last = pe.matmul(SC[nth[step] % 2][:, 64 * pair:64 * pair + 64], qT2[:, pair, P * i:P * i + P],
                                         kcT[:, pair // 2, :, :].rearrange("p e n -> p (e n)"), start=True, stop=True)
                    last.then_inc(sc_in, 1)
                elif what == "CT":
                    i = step[1]
                    wait_tr(step)
                    pe.wait_ge(cs_exp, i + 1)
                    for g in range(2):
                        last = pe.transpose(TR[:, P * g:P * g + P], prob[:, i % 2, P * g:P * g + P], ident[:, :])
                    last.then_inc(tr_in, 1)
                elif what == "CO":
                    i = step[1]
                    pe.wait_ge(tr_out, nth["CT", i] + 1)
                    pe.wait_ge(o_out, o_heads[step] - 1)
                    for g in range(2):
                        last = pe.matmul(OB[:, 256 * g:256 * g + 256], probT[:, P * g:P * g + P],
                                         vbd[:, g, :, :].rearrange("p r d -> p (r d)"), start=True, stop=True)
                    last.then_inc(o_in, 1)
                elif what == "gm_w":
                    u = step[1]
                    wait_tr(step)
                    pe.wait_ge(s_gm_in, 48)
                    for q in range(4):
                        last = pe.transpose(TR[:, P * q:P * q + P], ws_nat[:, 4 * u + q, :], ident[:, :])
                    last.then_inc(tr_in, 1)
                elif what == "gm":
                    u = step[1]
                    wait_sc(step)
                    pe.wait_ge(gm_n, NT)
                    pe.wait_ge(tr_out, nth["gm_w", 1] + 1)
                    for q in range(2):
                        g = 2 * u + q
                        last = pe.matmul(SC[nth[step] % 2][:, 256 * q:256 * q + 256], wsT[:, g, :],
                                         zv[:, :, HD * g:HD * g + HD], start=True, stop=True)
                    last.then_inc(sc_in, 1)

        @block.scalar
        def _(act):
            link_n = [0]

            def link(ins):
                link_n[0] += 1
                ins.then_inc(a_chain, 1)
                act.wait_ge(a_chain, link_n[0])

            raw_seen = [0, 0]
            group_of = {}
            for g, (phase, chunk, part, s0, w) in enumerate(groups):
                n = 1 if phase == "down" else (2 if phase == "gu" else len(group_cols(phase, chunk)))
                raw_seen[g % 2] += 16 * n
                for q in range(4):
                    group_of[s0 + q] = (g, q, w, raw_seen[g % 2])

            for step in timeline:
                what = step[0]
                if what == "split":
                    s = step[1]
                    g, q, w, landed = group_of[s]
                    act.wait_ge(s_raw[g % 2], landed)
                    if s >= RING:
                        act.wait_ge(w_used, s - RING + 1)
                    act.activation(WR[:, s % RING, 0, 0:w], RAW[:, g % 2, q, 0:w], ACT.Copy).then_inc(w_hi, 1)
                elif what == "xt":
                    _, phase, t, hf = step
                    act.wait_ge(xt_in, nth[step] + 1)
                    if t == 0 and phase != "in1":
                        p0, c0 = {"out1": ("in1", 7), "in2": ("out1", 1), "out2": ("in2", 4), "gu": ("out2", 1)}[phase]
                        act.wait_ge(w_used, first[p0, c0] + 4 * (halves(p0).index(hf) + 1))
                        if (phase, hf) == ("out2", 0):
                            act.wait_ge(sc_in, nth["gm", 3] + 1)
                            act.wait_ge(gm_n, NT)
                    kind_, i = xt_bank(step)
                    act.activation(XT[:, 4 * hf:4 * hf + 4, 0, P * t:P * t + P],
                                   (MM[i] if kind_ == "mm" else XB[i]).rearrange("p (q n) -> p q n", q=4), ACT.Copy).then_inc(xt_hi, 1)
                elif what == "sqa":
                    t = step[1]
                    if t == 0:
                        wait_evacuated(act, ("ev", "out2", 0))
                        act.wait_ge(tr_in, seen["tr"])
                    act.activation(squares[:, t, :], R1[:, t, 0:512], ACT.Square, accum_out=ss_a[:, t:t + 1]).then_inc(sqa_done, 1)
                elif what == "sq":
                    _, name, t = step
                    junk = prob[:, t % 2, 0:D]
                    if name in ("in1", "in2", "gu") and t >= 2:
                        act.wait_ge(sq_done, nth[step] - 1)
                    if name == "ffn" and t:
                        act.wait_ge(sq_done, nth[step])
                    if name == "in1":
                        act.wait_ge(s_x[t], 16)
                        act.activation(junk, R1[:, t, :], ACT.Square, accum_out=ss[:, t:t + 1]).then_inc(sq_done, 1)
                    elif name == "in2":
                        if t == 0:
                            act.wait_ge(tr_in, nth["T", "swa", 3, 1] + 1)
                            wait_evacuated(act, ("ev", "out1", 1))
                        act.activation(junk, R2[:, t, :], ACT.Square, accum_out=ss[:, t:t + 1]).then_inc(sq_done, 1)
                    elif name == "mix":
                        if t == 0:
                            act.wait_ge(w_used, first["out2", 1] + KD)
                            act.wait_ge(sqa_done, NT)
                        act.activation(squares[:, t, :], MM[t], ACT.Square, accum_out=ss[:, t:t + 1]).then_inc(sq_done, 1)
                    elif name == "gu":
                        if t == 0:
                            act.wait_ge(sq_done, nth["sq", "mix", 3] + 1)
                        act.wait_ge(post_dve, t + 1)
                        act.wait_ge(post_pool, t + 1)
                        act.activation(junk, R2[:, t, :], ACT.Square, accum_out=ss[:, t:t + 1]).then_inc(sq_done, 1)
                    else:
                        act.wait_ge(w_used, first["down", DOWN_TILES - 1] + min(t + 1, 4))
                        act.activation(gated[:, 0, :], SET[0][t], ACT.Square, accum_out=ss_a[:, t:t + 1])
                        act.activation(gated[:, 1, :], SET[1][t], ACT.Square, accum_out=ss[:, t:t + 1]).then_inc(sq_done, 1)
                elif what == "ev":
                    _, phase, ch = step
                    act.wait_ge(w_used, first[phase, ch] + KD)
                    if phase == "gu":
                        for m in range(2):
                            if ch:
                                act.wait_ge(ev_dve, ev_count["ev", "gu", ch - 1][1])
                            act.activation(gated[:, m, :], SET[ch % 2][m], ACT.Silu).then_inc(gs_done, 1)
                        continue
                    if (phase, ch) in (("in1", 0), ("in2", 0)):
                        act.wait_ge(r_ready, nth["ms", phase, 0] + 1)
                    if (phase, ch) == ("in1", 4):
                        act.wait_ge(tr_in, nth["qt", "moba", 3] + 1)
                    if (phase, ch) == ("in1", 2):
                        act.wait_ge(tr_in, nth["qt", "fox", 3] + 1)
                    if (phase, ch) == ("in1", 5):
                        act.wait_ge(tr_in, nth["qt", "sb", 3] + 1)
                    if (phase, ch) == ("in1", 6):
                        act.wait_ge(gx_done, nth["gx", "in1", 3, 0] + 1)
                        act.wait_ge(gx_pool, NT)
                    if (phase, ch) == ("in2", 1):
                        act.wait_ge(tr_in, nth["qt", "slc", 3] + 1)
                    if (phase, ch) == ("in2", 2):
                        act.wait_ge(tr_in, nth["qt", "q", 3] + 1)
                    if (phase, ch) == ("in2", 3):
                        act.wait_ge(sc_in, nth["hidden", 1] + 1)
                    if (phase, ch) == ("in2", 4):
                        act.wait_ge(sc_out, nth["cmpkv",] + 1)
                    if (phase, ch) == ("out2", 0):
                        act.wait_ge(xt_in, nth["xt", "out2", 3, 0] + 1)
                    for t in range(NT):
                        if evac_engine(phase, ch, t) != "act":
                            continue
                        for ins in evacuate(act, phase, ch, t):
                            last = ins
                        last.then_inc(ev_act, 1)
                elif what == "logf":
                    act.wait_ge(lf_pre, 1)
                    link(act.activation(lf_a, lf_a, ACT.Exp))
                    act.activation(lf_a, lf_a, ACT.Ln, bias=1.0).then_inc(lf_act, 1)
                elif what == "S":
                    _, name, h, g = step
                    plan = HEADS[name][0]
                    act.wait_ge(sc_out, nth[step] + 1)
                    hi = head_index(name, h)
                    buf = prob[:, hi % 2, GROUP_AT[g]:GROUP_AT[g] + width(plan, g)]
                    sl = 4 * (hi % 4)
                    for i, j, m, col, n in segments(plan, g):
                        last = act.activation(buf[:, col:col + m * P], buf[:, col:col + m * P], ACT.Exp,
                                              bias=nm[:, sl + n:sl + n + 1], accum_out=sm[:, sl + n:sl + n + 1])
                        if name == "swa":
                            last = act.activation(es[:, sl + n:sl + n + 1], nm[:, sl + n:sl + n + 1], ACT.Exp, bias=sinks[:, h:h + 1])
                    last.then_inc(e_done, 1)
                elif what == "sp":
                    h = step[1]
                    act.wait_ge(sp_abs, h + 1)
                    link(act.activation(soft[:, h % 2, :], soft[:, h % 2, :], ACT.Exp))
                    act.activation(soft[:, h % 2, :], soft[:, h % 2, :], ACT.Ln, bias=1.0).then_inc(sp_ln, 1)
                elif what == "F":
                    _, h, g = step
                    act.wait_ge(tr_out, nth[step] + 1)
                    if g == 0:
                        act.wait_ge(o_in, nth[last_o(("sb", h - 1) if h else ("moba", 3))] + 1)
                    lo = GROUP_AT[g]
                    w = sum(SEQ - P * j for j in KEYS[g])
                    act.activation(probT[:, lo:lo + w], prob[:, h % 2, lo:lo + w], ACT.Exp).then_inc(a_done, 1)
                elif what == "T":
                    _, name, h, g = step
                    w = width(HEADS[name][0], g)
                    act.wait_ge(tr_in, nth[step] + 1)
                    prev = prev_head(name, h)
                    if prev is not None:
                        same = prev[0] in HEADS and HEADS[prev[0]][0] is HEADS[name][0]
                        act.wait_ge(o_in, nth[("O", *prev, g) if same else last_o(prev)] + 1)
                    act.activation(probT[:, GROUP_AT[g]:GROUP_AT[g] + w], TR[:, 0:w], ACT.Copy).then_inc(tr_out, 1)
                elif what == "hidden":
                    kv = step[1]
                    act.wait_ge(sc_in, nth[step] + 1)
                    if kv == 0:
                        act.wait_ge(tr_in, nth["qt", "cmp", 3] + 1)
                    act.activation(hidT[:, kv, :, :], SC[nth[step] % 2][:, 0:128].rearrange("p (f n) -> p f n", f=2),
                                   ACT.Gelu_apprx_tanh).then_inc(hid_act, 1)
                elif what == "gates":
                    wait_evacuated(act, ("ev", "in2", 2))
                    act.activation(g_tmp, g_tmp, ACT.Exp, scale=-1.0).then_inc(gate_e, 1)
                elif what == "CS":
                    i = step[1]
                    act.wait_ge(cs_sub, i + 1)
                    act.activation(prob[:, i % 2, 0:256], prob[:, i % 2, 0:256], ACT.Exp).then_inc(cs_exp, 1)
                elif what == "act":
                    kt = step[1]
                    act.wait_ge(ev_dve, ev_count["ev", "gu", kt // 2][1])
                    if kt == 0:
                        act.wait_ge(w_used, first["gu", GU_CHUNKS - 1] + KD)
                    if kt >= 8:
                        act.wait_ge(w_used, first["down", kt - 8] + 2)
                    act.activation(XT[:, kt % 8, 0, :], actT[:, kt, :], ACT.Copy).then_inc(act_hi, 1)

        @block.vector
        def _(dve):
            link_n = [0]

            def link(ins):
                link_n[0] += 1
                ins.then_inc(v_chain, 1)
                dve.wait_ge(v_chain, link_n[0])

            dve.memset(half, -0.5)
            dve.memset(tab1[32:33, :], 1.0)
            dve.memset(tab2[32:33, :], 1.0).then_inc(setup_dve, 1)
            dve.sem_inc(setup_dve, 1)

            def setup():
                dve.wait_ge(s_const, 16 * 12)
                dve.wait_ge(s_ident, 16)
                dve.tensor_copy(identb[:, :], ident[:, :])
                dve.tensor_copy(causal[:, :], stage[:, 0:128])
                dve.tensor_copy(strict[:, :], stage[:, 128:256])
                for n in range(3):
                    last = dve.tensor_scalar(qk_gain[:, 2 * n:2 * n + 1], qk_gain[:, 2 * n:2 * n + 1], QSCALE, None, ALU.mult)
                last.then_inc(setup_dve, 1)
                dve.wait_ge(setup_dve, 3)

            for step in timeline:
                what = step[0]
                if what == "rows_out":
                    for n, bank in enumerate((SC[0], SC[1], TR, OB)):
                        lo, hi = (0, 512, 1024, 1536, 1664)[n:n + 2]
                        dve.wait_ge(tab_done, n + 1)
                        dve.tensor_copy(rows[0:8, lo:hi], bank[0:8, 0:hi - lo]).then_inc(tab_out, 1)
                if step == ("ev", "in1", 0):
                    setup()
                if step == ("gx", "in2", 0, 0):
                    dve.wait_ge(s_cmp, 16)
                    dve.wait_ge(sc_in, nth["S", "swa", 3, 1] + 1)
                    dve.tensor_copy(hot_parts[0:33, :], hot_cmp[0:33, :])
                    link(dve.tensor_copy(tab_parts[0:33, 0:8], tab2[0:33, :]))
                    dve.tensor_tensor(tab_parts[0:33, 8:16], tab2[0:33, :], tab_parts[0:33, 0:8].bitcast(F32),
                                      ALU.subtract).then_inc(hot_r, 1)
                if what == "gx" and not by_pool(step):
                    _, phase, t, hf = step
                    cols = slice(512 * hf, 512 * hf + 512)
                    if phase == "in1":
                        dve.wait_ge(s_x[t], 16)
                        if t == 0:
                            dve.wait_ge(s_gain, 16)
                        ins = dve.tensor_tensor(R2[:, t, cols], R1[:, t, cols], gain[0][:, cols], ALU.mult)
                    elif phase == "out1":
                        if t == 0:
                            wait_evacuated(dve, ("ev", "in1", 6 + hf))
                            last_head = ("O", "moba", 3, 2) if hf == 0 else ("O", "swa", 3, 1)
                            dve.wait_ge(o_out, o_heads[last_head])
                        ins = dve.tensor_tensor(R2[:, t, cols], R2[:, t, cols], R1[:, t, cols], ALU.mult)
                    elif phase == "in2":
                        if t == 0:
                            wait_evacuated(dve, ("ev", "out1", hf))
                            dve.wait_ge(s_gain, 32)
                        ins = dve.tensor_tensor(R1[:, t, cols], R2[:, t, cols], gain[0][:, cols], ALU.mult)
                    else:
                        if hf == 0:
                            dve.wait_ge(r_ready, nth["ms", "gu", t] + 1)
                        if t == 0:
                            dve.wait_ge(s_gain, 64)
                        ins = dve.scalar_tensor_tensor(out=R1[:, t, cols], in0=R2[:, t, cols], scalar=rr[:, t:t + 1],
                                                       in1=gain[0][:, cols], op0=ALU.mult, op1=ALU.mult)
                    ins.then_inc(gx_done, 1)
                elif what == "ms":
                    _, name, t = step
                    if name in ("in1", "in2"):
                        dve.wait_ge(sq_done, nth["sq", name, 3] + 1)
                        dve.tensor_scalar(ss, ss, 1.0 / D, EPS, ALU.mult, ALU.add).then_inc(ms_ready, 1)
                    else:
                        dve.wait_ge(sq_done, nth["sq", name, t] + 1)
                        if name != "gu":
                            link(dve.tensor_tensor(ss[:, t:t + 1], ss[:, t:t + 1], ss_a[:, t:t + 1], ALU.add))
                        dve.tensor_scalar(ss[:, t:t + 1], ss[:, t:t + 1], 1.0 / D, EPS, ALU.mult, ALU.add).then_inc(ms_ready, 1)
                elif what == "cmp_bias":
                    dve.wait_ge(cmp_in, 1)
                    link(dve.memset(cmp_bias[:, :, :, :], MASK))
                    for i in range(NT):
                        at_ = 16 * (24 - 8 * i)
                        w = WINDOWS[:, at_:at_ + 16 * NCMP].rearrange("p (n x h) -> p n x h", x=2, h=8)
                        dst = cmp_bias[:, i, :, 0:NCMP].rearrange("p h n -> p n h")
                        link(dve.tensor_copy(dst, w[:, :, 1, :]))
                        last = dve.tensor_tensor(dst, dst, w[:, :, 0, :], ALU.add)
                    last.then_inc(cmp_out, 1)
                elif what == "xt":
                    _, phase, t, hf = step
                    kind_, i = xt_bank(step)
                    dve.wait_ge(xt_hi, nth[step] + 1)
                    hi_part = XT[:, 4 * hf:4 * hf + 4, 0, P * t:P * t + P]
                    dve.tensor_tensor(XT[:, 4 * hf:4 * hf + 4, 1, P * t:P * t + P],
                                      (MM[i] if kind_ == "mm" else XB[i]).rearrange("p (q n) -> p q n", q=4), hi_part.bitcast(F32),
                                      ALU.subtract).then_inc(xt_lo, 1)
                elif what == "ev":
                    _, phase, ch = step
                    if phase == "gu":
                        for m in range(2):
                            dve.wait_ge(gs_done, 2 * ch + m + 1)
                            if ch == 0:
                                dve.wait_ge(tr_in, seen["tr"])
                            last = dve.tensor_tensor(actT[:, 2 * ch + m, :], SET[ch % 2][2 + m], gated[:, m, :], ALU.mult)
                        last.then_inc(ev_dve, 1)
                        continue
                    dve.wait_ge(w_used, first[phase, ch] + KD)
                    if (phase, ch) == ("in1", 2):
                        dve.wait_ge(tr_in, nth["qt", "fox", 3] + 1)
                    if (phase, ch) == ("in1", 4):
                        dve.wait_ge(tr_in, nth["qt", "moba", 3] + 1)
                    if (phase, ch) == ("in1", 5):
                        dve.wait_ge(tr_in, nth["qt", "sb", 3] + 1)
                    if (phase, ch) == ("in2", 1):
                        dve.wait_ge(tr_in, nth["qt", "slc", 3] + 1)
                    if (phase, ch) == ("in2", 2):
                        dve.wait_ge(tr_in, nth["qt", "q", 3] + 1)
                    if (phase, ch) == ("out2", 0):
                        dve.wait_ge(xt_in, nth["xt", "out2", 3, 0] + 1)
                    if (phase, ch) in (("in1", 0), ("in2", 0)):
                        dve.wait_ge(r_ready, nth["ms", phase, 0] + 1)
                    for t in range(NT):
                        if evac_engine(phase, ch, t) != "dve":
                            continue
                        if phase == "out1":
                            dve.wait_ge(s_xa, 16)
                            cols = slice(512 * ch, 512 * ch + 512)
                            dve.tensor_tensor(R2[:, t, cols], MM[t], x_again[:, t, cols], ALU.add).then_inc(ev_dve, 1)
                            continue
                        for ins in evacuate(dve, phase, ch, t):
                            last = ins
                        last.then_inc(ev_dve, 1)
                elif what == "qa":
                    _, name, t = step
                    wait_evacuated(dve, ("ev", "in1", {"fox": 0, "moba": 2, "swa": 5}[name]))
                    link(dve.tensor_tensor(sq[:, :], qk_nat[:, t, :], qk_nat[:, t, :], ALU.mult))
                    link(dve.tensor_reduce(ms8, sq[:, :].rearrange("p (h d) -> p h d", d=HD), AX.X, ALU.add))
                    dve.tensor_scalar(ms8, ms8, 1.0 / HD, EPS, ALU.mult, ALU.add).then_inc(ms_ready, 1)
                elif what == "qb":
                    _, name, t = step
                    dve.wait_ge(r_ready, nth["qa", name, t] + 1)
                    v = qk_nat[:, t, :].rearrange("p (h d) -> p h d", d=HD)
                    dve.tensor_tensor(v, v, rr8.unsqueeze(2).broadcast_to([P, 8, HD]), ALU.mult).then_inc(qn_done, 1)
                elif what == "qt":
                    _, name, t = step
                    dve.wait_ge(tr_in, nth[step] + 1)
                    tok = slice(P * t, P * t + P)
                    if name in KINDS1:
                        kd = KINDS1[name]
                        if t == 0 and name == "sb":
                            dve.wait_ge(sc_in, nth["S", "fox", 3, 2] + 1)
                        if t == 0 and name == "swa":
                            dve.wait_ge(sc_in, nth["S", "moba", 3, 2] + 1)
                        for part in range(2):
                            dst = qkT1[:, kd % 2, 2 * part:2 * part + 2, tok]
                            src = TR[:, 256 * part:256 * part + 256].rearrange("p (q n) -> p q n", q=2)
                            if name == "sb":
                                last = dve.tensor_scalar(dst, src, QSCALE if part == 0 else 1.0, None, ALU.mult)
                            else:
                                gcol = 2 * {"fox": 0, "moba": 1, "swa": 2}[name] + part
                                last = dve.tensor_scalar(dst, src, qk_gain[:, gcol:gcol + 1], None, ALU.mult)
                    elif name == "q":
                        last = dve.tensor_scalar(qT2[:, :, tok], TR.rearrange("p (q n) -> p q n", q=4), QSCALE, None, ALU.mult)
                    elif name == "cmp":
                        if t == 0:
                            dve.wait_ge(xt_in, nth["xt", "in2", 3, 1] + 1)
                        src = TR.rearrange("p (v g n) -> p v g n", v=2, g=2)
                        for v in range(2):
                            dve.tensor_copy(cmpT[0:64, v, :, tok], src[0:64, v])
                            lo = 1 if t == 0 else 0
                            last = dve.tensor_copy(cmpT[64:128, v, :, P * t - 1 + lo:P * t + P - 1], src[64:128, v, :, lo:P])
                    else:
                        last = dve.tensor_copy(kT2[:, 0 if name == "slc" else 1, :, tok], TR[:, 0:256].rearrange("p (g n) -> p g n", g=2))
                    last.then_inc(tr_out, 1)
                elif what == "logf":
                    wait_evacuated(dve, ("ev", "in1", 1))
                    link(dve.tensor_tensor(lf_u.rearrange("p (t h) -> p t h", h=4), lf_u.rearrange("p (t h) -> p t h", h=4),
                                           b_forget.unsqueeze(1).broadcast_to([P, 4, 4]), ALU.add))
                    dve.scalar_tensor_tensor(out=lf_a, in0=lf_u, scalar=-1.0, in1=lf_u, op0=ALU.mult, op1=ALU.min).then_inc(lf_pre, 1)
                    dve.wait_ge(lf_pre, 1)
                    link(dve.tensor_scalar(lf_u, lf_u, -1.0, 0.0, ALU.mult, ALU.max))
                    dve.wait_ge(lf_act, 1)
                    dve.tensor_tensor(lf, lf_u, lf_a, ALU.add).then_inc(lf_done, 1)
                elif what == "C":
                    h = step[1]
                    dve.wait_ge(sc_in, nth[step] + 1)
                    dve.tensor_copy(fox_c[:, h, :], SC[nth[step] % 2]).then_inc(sc_out, 1)
                elif what == "S":
                    _, name, h, g = step
                    plan = HEADS[name][0]
                    hi = head_index(name, h)
                    buf = prob[:, hi % 2, GROUP_AT[g]:GROUP_AT[g] + width(plan, g)]
                    sl = 4 * (hi % 4)
                    dve.wait_ge(sc_in, nth[step] + 1)
                    if name == "swa" and h < 2:
                        if g == 0:
                            dve.wait_ge(a_done, 3 * (2 + h) + 3)
                    elif name == "slc" and h < 2:
                        dve.wait_ge(tr_in, nth["CT", 2 + h] + 1)
                    elif name == "fox" and h < 2:
                        dve.wait_ge(sq_done, 4)
                        if h == 0 and g == 0:
                            dve.wait_ge(sc_out, nth["C", 0] + 1)
                    elif name in ("moba", "win") and h < 2:
                        dve.wait_ge(tr_in, nth["T", "fox" if name == "moba" else "slc", HEADS["fox" if name == "moba" else "slc"][1] - 2 + h, g] + 1)
                    else:
                        dve.wait_ge(tr_in, nth["T", name, h - 2, g] + 1)
                    if h == 0 and g == 0 and name in ("moba", "swa"):
                        dve.wait_ge(s_bias1, 128)
                    if h == 0 and g == 0 and name == "slc":
                        dve.wait_ge(s_bias2, 128)
                    if name == "fox" and g == 0:
                        dve.wait_ge(sc_out, nth["C", h] + 1)
                    first_n = None
                    for i, j, m, col, n in segments(plan, g):
                        first_n = n if first_n is None else first_n
                        last = dve.tensor_tensor_reduce(buf[:, col:col + m * P], SC[nth[step] % 2][:, col:col + m * P],
                                                        bias_of(name, h, i, m), 1.0, -3e38, ALU.add, ALU.max,
                                                        mx[:, sl + n:sl + n + 1])
                    link(last)
                    ns = slice(sl + first_n, sl + n + 1)
                    if name == "swa":
                        dve.tensor_scalar(nm[:, ns], mx[:, ns], sinks[:, h:h + 1], -1.0, ALU.max, ALU.mult).then_inc(sc_out, 1)
                    else:
                        dve.tensor_scalar(nm[:, ns], mx[:, ns], -1.0, None, ALU.mult).then_inc(sc_out, 1)
                elif what == "O":
                    _, name, h, g = step
                    plan = HEADS[name][0]
                    if step != last_o((name, h)):
                        continue
                    sl = 4 * (head_index(name, h) % 4)
                    dve.wait_ge(o_in, nth[step] + 1)
                    if name == "swa":
                        link(dve.tensor_tensor(sm[:, sl:sl + 4], sm[:, sl:sl + 4], es[:, sl:sl + 4], ALU.add))
                    link(dve.reciprocal(ri[:, sl:sl + 4], sm[:, sl:sl + 4]))
                    if name in ("slc", "win"):
                        gc = 4 * (3 * h + (1 if name == "slc" else 2))
                        link(dve.tensor_tensor(ri[:, sl:sl + 4], ri[:, sl:sl + 4], gates[:, gc:gc + 4], ALU.mult))
                    for gg in range(len(plan)):
                        for i, j, m, col, n in segments(plan, gg):
                            at_ = P * n + HD * v_of(name, h, 0)[1]
                            src = OB[:, at_:at_ + HD]
                            f = ri[:, sl + n:sl + n + 1]
                            if name in ("slc", "win"):
                                dst = R1[:, i, HD * h:HD * h + HD]
                                last = dve.scalar_tensor_tensor(out=dst, in0=src, scalar=f, in1=dst, op0=ALU.mult, op1=ALU.add)
                            else:
                                lo = 256 * KINDS1[name] + HD * h
                                last = dve.tensor_scalar(R2[:, i, lo:lo + HD], src, f, None, ALU.mult)
                    last.then_inc(o_out, 1)
                elif what == "Z":
                    _, h, g = step
                    lo = GROUP_AT[g]
                    w = sum(SEQ - P * j for j in KEYS[g])
                    dve.wait_ge(sc_in, nth[step] + 1)
                    if g == 0:
                        if h < 2:
                            dve.wait_ge(tr_in, nth["T", "moba", 2 + h, 2] + 1)
                        else:
                            dve.wait_ge(a_done, 3 * (h - 2) + 3)
                    dve.tensor_copy(prob[:, h % 2, lo:lo + w], SC[nth[step] % 2][:, 0:w]).then_inc(sc_out, 1)
                elif what == "sp":
                    h = step[1]
                    dve.wait_ge(sc_out, nth["Z", h, 2] + 1)
                    if h >= 2:
                        dve.wait_ge(tr_in, nth["F", h - 2, 2] + 1)
                    dve.scalar_tensor_tensor(out=soft[:, h % 2, :], in0=prob[:, h % 2, :], scalar=-1.0, in1=prob[:, h % 2, :],
                                             op0=ALU.mult, op1=ALU.min).then_inc(sp_abs, 1)
                elif what == "sp_b":
                    h = step[1]
                    dve.wait_ge(sp_ln, h + 1)
                    dve.scalar_tensor_tensor(out=soft[:, h % 2, :], in0=prob[:, h % 2, :], scalar=0.0, in1=soft[:, h % 2, :],
                                             op0=ALU.max, op1=ALU.add).then_inc(sp_done, 1)
                elif what == "F":
                    _, h, g = step
                    lo = GROUP_AT[g]
                    w = sum(SEQ - P * j for j in KEYS[g])
                    dve.wait_ge(tr_in, nth[step] + 1)
                    dve.tensor_tensor(prob[:, h % 2, lo:lo + w], prob[:, h % 2, lo:lo + w], TR[:, 0:w], ALU.subtract).then_inc(tr_out, 1)
                elif what == "OS":
                    h = step[1]
                    dve.wait_ge(o_in, nth[step] + 1)
                    lo = 512 + HD * h
                    e = HD * (h % 2)
                    dve.tensor_copy(R2[:, :, lo:lo + HD], OB.rearrange("p (i d) -> p i d", i=4)[:, :, e:e + HD]).then_inc(o_out, 1)
                elif what == "blocks":
                    dve.wait_ge(tr_out, nth["qt", "cmp", 3] + 1)
                    dve.wait_ge(s_small2, 16 * 8)
                    for v in range(2):
                        for g in range(2):
                            dve.memset(blocks[:, v, :, 32 * g + NCMP:32 * g + 32], 0.0)
                            src = cmpT[:, v, g, 0:480 + 32].rearrange("p (i u) -> p i u", u=16)
                            for hb in range(2):
                                s_ = src[:, hb:hb + NCMP, :].rearrange("p i (m e) -> p m i e", e=2)[:, :, :, 0]
                                dst = blocks[:, v, 8 * hb:8 * hb + 8, 32 * g:32 * g + NCMP]
                                pp = pos[:, 16 * v + 8 * hb:16 * v + 8 * hb + 8].unsqueeze(2).broadcast_to([P, 8, NCMP])
                                last = dve.tensor_tensor(dst, s_, pp, ALU.add)
                    last.then_inc(blk_done, 1)
                elif what == "hidden":
                    kv = step[1]
                    dve.wait_ge(hid_act, kv + 1)
                    dve.sem_inc(sc_out, 1)
                    if kv == 1:
                        for f in range(2):
                            for g in range(2):
                                last = dve.tensor_copy(hidV[:, f, g, :].rearrange("p (r i) -> p r i", r=4),
                                                       hidT[:, 1, f, 32 * g:32 * g + 32].unsqueeze(1).broadcast_to([P, 4, 32]))
                        last.then_inc(hid_rep, 1)
                elif what == "cmpkv":
                    dve.wait_ge(sc_in, nth[step] + 1)
                    bank = SC[nth[step] % 2]
                    dve.memset(kcT[:, :, :, :], 0.0)
                    link(dve.memset(vbd[:, :, :, :], 0.0))
                    for e in range(2):
                        dve.tensor_copy(kcT[64 * e:64 * e + 64, :, e, :], bank[64 * e:64 * e + 64, 0:64].rearrange("p (g n) -> p g n", g=2))
                    for r in range(4):
                        last = dve.tensor_copy(vbd[32 * r:32 * r + 32, :, r, :], bank[32 * r:32 * r + 32, 64:192].rearrange("p (g d) -> p g d", g=2))
                    last.then_inc(sc_out, 1)
                elif what == "gates":
                    wait_evacuated(dve, ("ev", "in2", 2))
                    dve.wait_ge(gate_e, 1)
                    link(dve.tensor_scalar(g_tmp, g_tmp, 1.0, None, ALU.add))
                    link(dve.reciprocal(gates, g_tmp))
                elif what == "CS":
                    i = step[1]
                    p3 = prob[:, i % 2, 0:256].rearrange("p (h n) -> p h n", h=8)
                    dve.wait_ge(sc_in, nth[step] + 1)
                    if i >= 2:
                        dve.wait_ge(tr_in, nth["CT", i - 2] + 1)
                    else:
                        dve.wait_ge(sq_done, nth["sq", "in2", 3] + 1)
                    dve.tensor_tensor(p3, SC[nth[step] % 2][:, 0:256].rearrange("p (h n) -> p h n", h=8),
                                      cmp_bias[:, i, :, :], ALU.add).then_inc(sc_out, 1)
                    dve.wait_ge(sc_out, nth[step] + 1)
                    link(dve.tensor_reduce(cm8, p3, AX.X, ALU.max))
                    link(dve.tensor_scalar(cm8, cm8, FLOOR, None, ALU.max))
                    dve.tensor_tensor(p3, p3, cm8.unsqueeze(2).broadcast_to([P, 8, 32]), ALU.subtract).then_inc(cs_sub, 1)
                    dve.wait_ge(cs_exp, i + 1)
                    link(dve.tensor_reduce(cs8, p3, AX.X, ALU.add))
                    link(dve.tensor_scalar(cs8, cs8, 1e-30, None, ALU.max))
                    link(dve.reciprocal(cs8, cs8))
                    gv = gates.rearrange("p (h b q) -> p h b q", h=8, b=3)[:, :, 0, POS[i]]
                    link(dve.tensor_tensor(cf8[:, 8 * i:8 * i + 8], cs8, gv, ALU.mult))
                elif what == "CT":
                    i = step[1]
                    dve.wait_ge(tr_in, nth[step] + 1)
                    dve.wait_ge(o_in, nth["CO", i - 1] + 1 if i else nth[last_o(("swa", 3))] + 1)
                    dve.tensor_copy(probT[:, 0:256], TR[:, 0:256]).then_inc(tr_out, 1)
                elif what == "CO":
                    i = step[1]
                    dve.wait_ge(o_in, nth[step] + 1)
                    if i == 0:
                        dve.wait_ge(sc_in, nth["hidden", 1] + 1)
                    dve.tensor_tensor(R1[:, i, 0:512].rearrange("p (h d) -> p h d", h=8), OB.rearrange("p (h d) -> p h d", h=8),
                                      cf8[:, 8 * i:8 * i + 8].unsqueeze(2).broadcast_to([P, 8, HD]), ALU.mult).then_inc(o_out, 1)
                elif what == "gm_w":
                    u = step[1]
                    dve.wait_ge(tr_in, nth[step] + 1)
                    dve.tensor_tensor(wsT[:, 4 * u:4 * u + 4, :], TR.rearrange("p (q n) -> p q n", q=4),
                                      tri[:, 0:P].unsqueeze(1).broadcast_to([P, 4, P]), ALU.mult).then_inc(tr_out, 1)
                elif what == "gm_a":
                    t = step[1]
                    wait_evacuated(dve, ("ev", "in2", 4))
                    z = zv[:, t, :]
                    link(dve.tensor_reduce(negmu[:, t:t + 1], z, AX.X, ALU.add))
                    link(dve.tensor_scalar(negmu[:, t:t + 1], negmu[:, t:t + 1], 1.0 / 512, None, ALU.mult))
                    link(dve.tensor_scalar(z, z, negmu[:, t:t + 1], None, ALU.subtract))
                    link(dve.tensor_tensor_reduce(sq[:, :], z, z, 1.0, 0.0, ALU.mult, ALU.add, ss[:, t:t + 1]))
                    dve.tensor_scalar(ss[:, t:t + 1], ss[:, t:t + 1], 1.0 / 512, LN_EPS, ALU.mult, ALU.add).then_inc(ms_ready, 1)
                elif what == "gm_b":
                    t = step[1]
                    z = zv[:, t, :]
                    dve.wait_ge(r_ready, nth["gm_a", t] + 1)
                    dve.wait_ge(s_gm_in, 48)
                    link(dve.scalar_tensor_tensor(out=z, in0=z, scalar=rr[:, t:t + 1], in1=ln_g[:, :], op0=ALU.mult, op1=ALU.mult))
                    dve.tensor_tensor(z, z, ln_b[:, :], ALU.add).then_inc(gm_n, 1)
                elif what == "gm":
                    u = step[1]
                    dve.wait_ge(sc_in, nth[step] + 1)
                    for q in range(2):
                        g = 2 * u + q
                        dst = R1[:, :, 512 + HD * g:512 + HD * g + HD]
                        last = dve.scalar_tensor_tensor(out=dst, in0=SC[nth[step] % 2][:, 256 * q:256 * q + 256].rearrange("p (n d) -> p n d", n=4),
                                                        scalar=gmlp_b[:, g:g + 1], in1=dst, op0=ALU.add, op1=ALU.mult)
                    last.then_inc(sc_out, 1)
                elif what == "act":
                    kt = step[1]
                    dve.wait_ge(act_hi, kt + 1)
                    dve.tensor_tensor(XT[:, kt % 8, 1, :], actT[:, kt, :], XT[:, kt % 8, 0, :].bitcast(F32), ALU.subtract).then_inc(act_lo, 1)
                elif what == "post":
                    _, name, t = step
                    lo_half, hi_half = (R1[:, t, 0:512], MM[t]) if name == "mix" else (SET[0][t], SET[1][t])
                    if t == 0:
                        if name == "mix":
                            wait_evacuated(dve, ("ev", "out2", 0))
                        dve.wait_ge(s_gain, 64 if name == "mix" else 80)
                    dve.wait_ge(r_ready, nth["ms", name, t] + 1)
                    dve.scalar_tensor_tensor(out=R1[:, t, 0:512], in0=lo_half, scalar=rr[:, t:t + 1], in1=gain[1][:, 0:512],
                                             op0=ALU.mult, op1=ALU.mult).then_inc(post_lo, 1)
                    link(dve.scalar_tensor_tensor(out=R1[:, t, 512:D], in0=hi_half, scalar=rr[:, t:t + 1], in1=gain[1][:, 512:D],
                                                  op0=ALU.mult, op1=ALU.mult))
                    dve.tensor_tensor(R2[:, t, 512:D], R2[:, t, 512:D], R1[:, t, 512:D], ALU.add).then_inc(post_dve, 1)

        @block.gpsimd
        def _(pool):
            group_of = {}
            for g, (phase, chunk, part, s0, w) in enumerate(groups):
                for q in range(4):
                    group_of[s0 + q] = (g, q, w)
            for step in timeline:
                what = step[0]
                if what == "split":
                    s = step[1]
                    g, q, w = group_of[s]
                    pool.wait_ge(w_hi, s + 1)
                    pool.tensor_tensor(WR[:, s % RING, 1, 0:w], RAW[:, g % 2, q, 0:w], WR[:, s % RING, 0, 0:w].bitcast(F32),
                                       ALU.subtract).then_inc(w_lo, 1)
                    continue
                if what == "gx":
                    if by_pool(step):
                        _, phase, t, hf = step
                        pool.wait_ge(s_x[t], 16)
                        pool.wait_ge(s_gain, 16)
                        pool.tensor_tensor(R2[:, t, 512:D], R1[:, t, 512:D], gain[0][:, 512:D], ALU.mult).then_inc(gx_pool, 1)
                    continue
                if what == "post":
                    t = step[2]
                    pool.wait_ge(post_lo, nth[step] + 1)
                    pool.tensor_tensor(R2[:, t, 0:512], R2[:, t, 0:512], R1[:, t, 0:512], ALU.add).then_inc(post_pool, 1)
                    continue
                if what == "ms" and step[1] in ("in1", "in2"):
                    src, dst, n = ss, rr, NT
                elif what == "ms":
                    src, dst, n = ss[:, step[2]:step[2] + 1], rr[:, step[2]:step[2] + 1], 1
                elif what == "gm_a":
                    src, dst, n = ss[:, step[1]:step[1] + 1], rr[:, step[1]:step[1] + 1], 1
                elif what == "qa":
                    src, dst, n = ms8, rr8, 8
                else:
                    continue
                pool.wait_ge(ms_ready, nth[step] + 1)
                pool.tensor_tensor(dst, src, half[:, 0:1].broadcast_to([P, n]) if n > 1 else half[:, 0:1], ALU.pow).then_inc(r_ready, 1)


_INS = [
    "x", "norm_gain", "w_in", "b_forget", "fox_qk_gain", "moba_qk_gain", "swa_qk_gain", "sinks", "w_out",
    "rel_bias", "rel_bias_2", "norm_mix_pre_2", "norm_mix_post_2", "norm_ffn_pre_2", "norm_ffn_post_2",
    "w_in_2", "cmp_pos_k_2", "cmp_w1_k_2", "cmp_w2_k_2", "cmp_pos_v_2", "cmp_w1_v_2", "cmp_w2_v_2",
    "gmlp_ln_g_2", "gmlp_ln_b_2", "gmlp_w_s_2", "gmlp_b_s_2", "w_out_2", "w_gate_up_2", "w_down_2",
]


def kernel(**inputs):
    import concourse.bacc as _bacc
    from concourse.bass_utils import run_bass_kernel_spmd as _run

    nc = _bacc.Bacc("TRN2", target_bir_lowering=False, num_devices=1)
    arrays, args, consts = {}, {}, {}
    for name in _INS:
        v = np.ascontiguousarray(inputs[name])
        arrays[f"in_{name}_dram"] = v
        args[name] = nc.dram_tensor(f"in_{name}_dram", v.shape, mybir.dt.from_np(v.dtype), kind="ExternalInput").ap()
    for name, v in constants().items():
        arrays[f"const_{name}_dram"] = v
        consts[name] = nc.dram_tensor(f"const_{name}_dram", v.shape, mybir.dt.from_np(v.dtype), kind="ExternalInput").ap()
    out = nc.dram_tensor("out_0_dram", (1, SEQ, D), F32, kind="ExternalOutput").ap()
    hybrid_two_block_kernel(nc, args, consts, out)
    r = _run(nc, [arrays], core_ids=[0])
    return r.results[0]["out_0_dram"]
```

```python
from contextlib import ExitStack

import numpy as np

import concourse.bass as bass
from concourse import mybir

F32 = mybir.dt.float32
F32R = mybir.dt.float32r
BF16 = mybir.dt.bfloat16
ALU = mybir.AluOpType
ACT = mybir.ActivationFunctionType
AX = mybir.AxisListType

P = 128
SEQ = 512
D = 1024
NT = SEQ // P
KD = D // P
HD = 64
EPS = 1e-6
LN_EPS = 1e-5
MASK = -1e30
FLOOR = -1e29
QSCALE = HD ** -0.5
FF = 2816
NCMP = 31
RING = 6

FQ, FV, FG = 0, 512, 772
MQ, MV, MG = 1028, 1540, 1796
SQ_, SV, SG_ = 2052, 2564, 2820
WQ, WG = 3076, 3588
CHUNKS1 = [
    [(FQ, 512)],
    [(FV, 260)],
    [(MQ, 512)],
    [(MV, 256), (SV, 256)],
    [(SQ_, 512)],
    [(WQ, 512)],
    [(FG, 256), (MG, 256)],
    [(SG_, 256), (WG, 256)],
]
CHUNKS2 = [[(512, 512)], [(0, 512)], [(1024, 280)], [(1816, 512)], [(1304, 512)]]
W_OUT = [[(0, 512)], [(512, 512)]]
GU_CHUNKS = FF // 256
DOWN_TILES = FF // P

HALVES = {"out2": (1, 0)}

BY_ROWS = {("out2", 1): 3, ("down", DOWN_TILES - 1): 2}

FULL = [[(3, 0, 4)], [(2, 0, 3), (0, 0, 1)], [(1, 0, 2)]]
BAND = [[(1, 0, 2), (2, 1, 2)], [(3, 2, 2), (0, 0, 1)]]
KEYS = [[0], [1, 3], [2]]
KEY_COLS = {0: 0, 1: 512, 3: 896, 2: 1024}
POS = {3: 0, 2: 1, 0: 2, 1: 3}


def rel_bucket_of(dist, max_distance):
    half = 16
    d = np.maximum(dist, 0)
    ratio = np.log(np.maximum(d, half).astype(np.float32) / np.float32(half)).astype(np.float32)
    large = half + (ratio / np.float32(np.log(max_distance / half)) * np.float32(half)).astype(np.int32)
    return np.where(d < half, d, np.minimum(large, 31))


def one_hot(dist, valid, max_distance):
    out = np.zeros((33, len(dist)), np.float32)
    b = rel_bucket_of(dist, max_distance)
    out[b[valid], np.nonzero(valid)[0]] = 1.0
    out[32, ~valid] = MASK
    return out


def constants():
    i = np.arange(P)
    tri = (i[:, None] <= i[None, :]).astype(np.float32)
    d_full = 511 - np.arange(640)
    d_band = 255 - np.arange(384)
    d_cmp = np.arange(1024) - 511
    return {
        "ident": np.eye(P, dtype=np.float32),
        "tri_ones": np.concatenate([tri, np.ones((P, 384), np.float32)], 1),
        "suffix": np.ascontiguousarray(tri.T),
        "causal": np.where(i[None, :] > i[:, None], np.float32(MASK), np.float32(0)),
        "strict": np.where(i[:, None] >= i[None, :], np.float32(MASK), np.float32(0)),
        "hot_full": one_hot(d_full, d_full >= 0, 1024),
        "hot_band": one_hot(d_band, (d_band >= 0) & (d_band < 128), 1024),
        "hot_t5": one_hot(d_full, d_full >= 0, 128),
        "hot_cmp": one_hot(d_cmp, d_cmp >= 0, 128),
    }


def slots_and_groups():
    groups, first = [], {}
    s = 0
    for phase, chunks in (("in1", CHUNKS1), ("out1", W_OUT), ("in2", CHUNKS2), ("out2", W_OUT)):
        for c, cols in enumerate(chunks):
            first[phase, c] = s
            for part in range(2):
                groups.append((phase, c, part, s, sum(w for _, w in cols)))
                s += 4
    for c in range(GU_CHUNKS):
        first["gu", c] = s
        for part in range(2):
            groups.append(("gu", c, part, s, 512))
            s += 4
    for g in range(DOWN_TILES // 2):
        first["down", 2 * g] = s
        first["down", 2 * g + 1] = s + 2
        groups.append(("down", g, 0, s, 512))
        s += 4
    return groups, first, s


def halves(phase):
    return HALVES.get(phase, (0, 1))


def k_tile(phase, n):
    return 4 * halves(phase)[n // 4] + n % 4


def make_timeline(first, n_slots):
    tl = []

    def hi_lo(s):
        if s + 4 < n_slots:
            tl.append(("split", s + 4))

    def mm(phase, c, n, per=1):
        for j in range(per):
            hi_lo(first[phase, c] + n * per + j)
        tl.append(("mm", phase, c, n))

    rank = {
        "gates1": -6, "gates": -5, "logf": -4, "qb": -3, "C": -3, "qa": -2, "gm_b": -1,
        "O": 0, "CO": 0, "CS": 0.8, "T": 1, "CT": 1,
        "OS": 1.5, "CS_b": 1.5, "F": 2, "sp_b": 2.5, "S": 3, "Z": 3, "sp": 4, "qt": 4.5,
        "blocks": 5, "hidden": 6, "gelu": 6, "cmpkv": 7, "gm_w": 8, "gm_a": 9, "gm": 10,
    }
    queue = {n: [] for n in range(200)}

    def at(tick, *steps):
        queue[tick] += list(steps)

    def softmax_head(tick, name, h, plan, lag_t=2, lag_o=4):
        for g in range(len(plan)):
            at(tick + g, ("S", name, h, g))
            at(tick + g + lag_t, ("T", name, h, g))
            at(tick + g + lag_o, ("O", name, h, g))

    for name, tick in (("fox", 8), ("moba", 24), ("swa", 48)):
        step = 2 if name == "fox" else 1
        for t in range(NT):
            at(tick + step * t, ("qa", name, t))
            at(tick + step * t + 1, ("qb", name, t))
            at(tick + step * t + 2, ("qt", name, t))
    at(16, ("logf",))
    at(56, ("gates1", 0))
    at(70, ("gates1", 1))
    for h in range(4):
        at(17 + h, ("C", h))
    for t in range(NT):
        at(40 + t, ("qt", "sb", t))
    for h in range(4):
        softmax_head(18 + 3 * h, "fox", h, FULL)
        softmax_head(31 + 3 * h, "moba", h, FULL)
        a = 45 + 3 * h
        for g in range(3):
            at(a + g, ("Z", h, g))
            at(a + g + 5, ("F", h, g))
        at(a + 2, ("sp", h))
        at(a + 4, ("sp_b", h))
        at(a + 8, ("OS", h))
        softmax_head(60 + 2 * h, "swa", h, BAND)

    def flush(tick, *product):
        def order(step):
            return 0.5 if step[:2] == ("qt", "cmp") else rank[step[0]]

        steps = sorted(queue[tick], key=order)
        tl.extend(x for x in steps if order(x) <= 1)
        if product:
            mm(*product)
            if product[2] == KD - 1:
                tl.append(("ev", *product[:2]))
        tl.extend(x for x in steps if order(x) > 1)
        queue[tick] = []

    def out_product(phase, after, begun):
        hf = halves(phase)[1]
        for c in range(2):
            for n in range(KD):
                if c == 0 and n == begun and after:
                    tl.extend(("gx", phase, t, hf) for t in range(2))
                if (phase, c, n) == ("out2", 1, KD - 1):
                    tl.append(("mm", phase, c, n))
                elif c or n >= begun:
                    mm(phase, c, n)
                if c == 0 and 1 <= n < 3:
                    for t in ((0,), (1, 2, 3))[n - 1]:
                        if after and t < 2:
                            tl.append(("gx", phase, t + 2, hf))
                        tl.append(("xt", phase, t, hf))
                if c == 1 and after:
                    if n == 3:
                        tl.extend(("gx", after, t, 0) for t in range(NT))
                    for t in {4: (0,), 5: (1, 2), 6: (3,)}.get(n, ()):
                        tl.append(("xt", after, t, 0))
            if phase == "out1" or c == 0:
                tl.append(("ev", phase, c))
            if phase == "out2" and c == 0:
                tl.extend(("sqa", t) for t in range(NT))

    tl.append(("gx", "in1", 0, 0))
    tl.append(("gx", "in1", 0, 1))
    for t in range(NT):
        for hf in range(2):
            if t + 1 < NT:
                tl.append(("gx", "in1", t + 1, hf))
            tl.append(("xt", "in1", t, hf))
        if t == 2:
            for s in range(4):
                tl.append(("split", s))
            tl.append(("rows",))
    for t in range(NT):
        tl.append(("sq", "in1", t))
    tl.append(("ms", "in1", 0))
    tl.append(("rows_out",))
    for c in range(len(CHUNKS1)):
        for k in range(KD):
            flush(8 * c + k, "in1", c, k)
            if 8 * c + k in (59, 60, 61, 62):
                tl.append(("gx", "out1", 8 * c + k - 59, 0))
    begun = 1
    for tick in range(64, 80):
        if 68 <= tick < 68 + begun:
            flush(tick, "out1", 0, tick - 68)
        else:
            flush(tick)
        if tick in (65, 66):
            for t in (2 * (tick - 65), 2 * (tick - 65) + 1):
                tl.append(("xt", "out1", t, 0))
    out_product("out1", "in2", begun)

    for t in range(NT):
        at(9 + t, ("qt", "cmp", t))
        at(21 + t // 2, ("qt", "slc", t))
        at(17 + t, ("qt", "q", t))
        at(24 + t, ("qt", "win", t))
    at(13, ("blocks",))
    at(17, ("hidden", 0))
    at(20, ("hidden", 1))
    at(21, ("cmpkv",))
    at(24, ("gates",))
    for i in range(NT):
        at(25 + i, ("CS", i))
        at(26 + i, ("CS_b", i))
        at(27 + i, ("CT", i))
        at(28 + i, ("CO", i))
    for h in range(16):
        softmax_head(29 + 3 * h, "slc" if h < 8 else "win", h % 8, FULL)
    at(33, ("gelu", 0))
    at(41, ("gelu", 1))
    at(48, ("gm_w", 0))
    at(49, ("gm_w", 1))
    for t in range(NT):
        at(34 + 2 * t, ("gm_a", t))
        at(45 + 3 * t, ("gm_b", t))
    for u in range(4):
        at(56 + u, ("gm", u))
    for c in range(len(CHUNKS2)):
        for k in range(KD):
            if c == 0 and k == 0:
                tl.extend([("gx", "in2", 0, 1), ("gx", "in2", 1, 1)])
            flush(8 * c + k, "in2", c, k)
            if c == 0 and k < 3:
                for t in ((0,), (1,), (2, 3))[k]:
                    tl.append(("xt", "in2", t, 1))
                    if t < 2:
                        tl.append(("gx", "in2", t + 2, 1))
                if k == 2:
                    for t in range(NT):
                        tl.append(("sq", "in2", t))
                    tl.append(("ms", "in2", 0))
            if c == 0 and k < 6:
                tl.append(("windows", k))
                if k == 5:
                    tl.append(("cmp_bias",))
    begun = 0
    for tick in range(40, 200):
        if tick >= 68 and tick % 4 == 0 and begun < 1 and queue[tick]:
            flush(tick, "out2", 0, begun)
            begun += 1
        else:
            flush(tick)
        if 62 <= tick < 62 + NT:
            tl.append(("xt", "out2", tick - 62, 1))
    out_product("out2", None, begun)
    mix = [[("sq", "mix", t), ("ms", "mix", t)] for t in range(NT)]
    post = [[("post", "mix", t)] for t in range(NT)]
    sq_gu = [[("sq", "gu", t), ("ms", "gu", t)] for t in range(NT)]
    gx_gu = [[("gx", "gu", t, 0), ("gx", "gu", t, 1)] for t in range(NT)]
    for steps in (mix[0], post[0], mix[1], post[1], sq_gu[0], mix[2], post[2], sq_gu[1], mix[3], post[3], gx_gu[0][:1], gx_gu[1][:1], sq_gu[2]):
        tl.extend(steps)
    for t in range(NT):
        if t == 0:
            tl.extend(sq_gu[3])
        if t + 2 < NT:
            tl.append(gx_gu[t + 2][0])
        tl.append(("xt", "gu", t, 0))
        if t == 1:
            tl.append(("split", first["gu", 0] + 3))
    for c in range(GU_CHUNKS):
        for k in range(KD):
            if c == 0 and k == 0:
                tl.extend(gx_gu[t][1] for t in range(2))
            mm("gu", c, k)
            if c == GU_CHUNKS - 1 and k in (4, 6):
                tl.append(("act", k // 2 - 2))
            if c == 0 and k < 3:
                for t in ((0,), (1,), (2, 3))[k]:
                    tl.append(("xt", "gu", t, 1))
                    if t < 2:
                        tl.append(gx_gu[t + 2][1])
        tl.append(("ev", "gu", c))
    for kt in range(DOWN_TILES):
        if kt + 2 < DOWN_TILES:
            tl.append(("act", kt + 2))
        mm("down", kt, 0, 2)
    ffn = [[("sq", "ffn", t), ("ms", "ffn", t)] for t in range(NT)]
    post = [[("post", "ffn", t)] for t in range(NT)]
    for steps in (ffn[0], post[0], ffn[1], post[1], ffn[2], post[2], ffn[3], post[3]):
        tl.extend(steps)
    return tl


def hybrid_two_block_kernel(nc, a, c, out):
    groups, first, n_slots = slots_and_groups()
    timeline = make_timeline(first, n_slots)

    nth, seen = {}, {}

    def kind(step):
        k = step[0]
        return {"S": "sc", "Z": "sc", "C": "sc", "CS": "sc", "hidden": "sc", "gm": "sc", "cmpkv": "sc",
                "T": "tr", "F": "tr", "CT": "tr", "qt": "tr", "gm_w": "tr",
                "OS": "o", "O": "o", "CO": "o", "qa": "ms", "gm_a": "ms"}.get(k, k)

    def by_pool(step):
        return step[1] == "in1" and step[3] == 1

    for step in timeline:
        k_ = "gx_pool" if step[0] == "gx" and by_pool(step) else kind(step)
        nth[step] = seen.get(k_, 0)
        seen[k_] = nth[step] + 1

    with ExitStack() as ctx:
        def sem(name):
            return ctx.enter_context(nc.semaphore(name))

        BASE = 16512

        def at(name, kb, shape, dtype=F32):
            return nc.alloc_sbuf_tensor_at(name, [P] + shape, dtype, offset=BASE + int(kb * 1024))

        XT = at("XT", 0, [KD, 2, SEQ], F32R)
        WR = at("WR", 32, [RING, 2, 512], F32R)
        RAW = at("RAW", 56, [2, 4, 512])
        R1 = at("R1", 72, [NT, D])
        R2 = at("R2", 88, [NT, D])
        ident = at("ident_sb", 104, [P])
        identb = at("identb", 104.5, [P], BF16)
        causal = at("causal_sb", 104.75, [P], BF16)
        strict = at("strict_sb", 105, [P], BF16)
        tri = at("tri_sb", 105.25, [512], F32R)
        suffix = at("suffix_sb", 107.25, [P], F32R)
        gain = [at("gain0", 107.75, [D]), at("gain1", 111.75, [D])]
        sq = at("sq", 115.75, [512])
        st = at("st", 117.75, [520])
        lf_parts = at("lf_parts", 117.75 + 520 / 256, [2, 16], F32R)
        cmp_bias = at("cmp_bias", 120, [NT, 8, 32])
        prob = at("prob", 124, [2, 1280])
        squares = at("squares", 124, [NT, 640])[:, :, 0:512]
        squares_gu = at("squares_gu", 134, [2, 1280])
        probT = at("probT", 134, [1280])
        V1 = at("V1", 139, [NT, 896])
        qk_nat = at("qk_nat", 153, [NT, 512])
        qkT1 = at("qkT1", 161, [2, 4, SEQ])
        bias_moba = at("bias_moba", 177, [4, 512])
        bias_swa = at("bias_swa", 185, [4, 256])
        fox_c = at("fox_c", 189, [4, 512])
        soft = at("soft", 189, [1280])
        soft_parts = at("soft_parts", 194, [2, 1280], F32R)
        tri_raw = at("tri_raw", 168, [640])
        x_again = at("x_again", 161, [NT, D])
        hots = at("hots", 161, [1664])
        hot_cmp = at("hot_cmp", 179, [1024])
        rows = at("rows", 199, [1664])
        stage = at("stage", 197.5, [384])
        V2 = at("V2", 139, [NT, 2, P])
        hot_parts = at("hot_parts", 183, [1024], F32R)
        tab_parts = at("tab_parts", 117.75 + 560 / 256, [16], F32R)
        nat2 = at("nat2", 143, [NT, 512])
        cmp_nat = at("cmp_nat", 151, [NT, 4, P])
        zv = at("zv", 151, [NT, 512])
        hidT = at("hidT", 151, [2, 2, 64])
        hidV = at("hidV", 152, [2, 2, P])
        w1 = at("w1", 159, [16, 256])
        qS = at("qS", 175, [8, SEQ], F32R)
        kS = [at("kS_slc", 159, [2, 2, SEQ], F32R), at("kS_win", 167, [2, 2, SEQ], F32R)]
        kcS = at("kcS", 115.25, [2, 2, 32], F32R)
        k_nat = at("k_nat", 124, [NT, 256])
        bias_t5 = at("bias_t5", 191, [8, 512])
        cmpT = at("cmpT", 72, [2, 2, SEQ])
        blocks = at("blocks", 80, [2, 16, 64])
        vbd = at("vbd", 111.75, [2, 4, HD])
        w2k = at("w2k", 113.75, [2, P])
        w2v = at("w2v", 114.75, [2, HD])
        ws_nat = at("ws_nat", 0, [8, P])
        wsT = at("wsT", 4, [8, P])
        ln_g = at("ln_g", 8, [512])
        ln_b = at("ln_b", 10, [512])
        gated = at("gated", 120, [2, 512])
        actT = at("actT", 124, [DOWN_TILES, SEQ])

        half = st[:, 0:4]
        qk_gain = st[:, 4:10]
        pos = st[:, 10:42]
        gmlp_b = st[:, 42:50]
        b_forget = st[:, 50:54]
        sinks = st[:, 54:58]
        ss = st[:, 58:62]
        rr = st[:, 62:66]
        ms8 = st[:, 66:74]
        rr8 = st[:, 74:82]
        lf = st[:, 82:98]
        lf_a = st[:, 98:114]
        lf_u = st[:, 114:130]
        mx = st[:, 130:146]
        nm = st[:, 146:162]
        sm = st[:, 162:178]
        es = st[:, 178:194]
        ri = st[:, 194:210]
        gates = st[:, 210:306]
        g_tmp = st[:, 306:402]
        cm8 = st[:, 402:410]
        cs8 = st[:, 410:418]
        cf8 = st[:, 418:450]
        tab1 = st[:, 450:458]
        tab2 = st[:, 458:466]
        negmu = st[:, 466:470]
        ss_g = st[:, 474:478]
        rr_g = st[:, 478:482]
        ss_a = st[:, 470:474]

        psum = ctx.enter_context(nc.psum_tensor("psum", [P, 8, 512], F32))
        MM = [psum[:, i, :] for i in range(4)]
        SC = [psum[:, 4, :], psum[:, 5, :]]
        TR = psum[:, 6, :]
        OB = psum[:, 7, :]
        XB = [psum[:, 4 + i, :] for i in range(4)]
        WINDOWS = psum[:, 6:8, :].rearrange("p b n -> p (b n)")
        SET = [[psum[:, i, :] for i in range(4)], [psum[:, 4 + i, :] for i in range(4)]]

        rows_d = nc.dram_tensor("rows_scratch", [20, 640], F32, kind="Internal").ap()
        rep_d = nc.dram_tensor("rep_scratch", [20, P, 640], F32, kind="Internal").ap()
        repb_d = nc.dram_tensor("repb_scratch", [4, P, 384], F32, kind="Internal").ap()

        s_x = [sem(f"x_landed{t}") for t in range(NT)]
        s_gain = sem("gain_landed")
        s_const = sem("consts_landed")
        s_tab = sem("tables_landed")
        s_raw = [sem("raw_landed0"), sem("raw_landed1")]
        s_rows = sem("rows_stored")
        s_rep = sem("rows_replicated")
        s_bias1 = sem("bias1_landed")
        s_bias2 = sem("bias2_landed")
        s_xa = sem("x_again_landed")
        s_w1 = sem("w1_landed")
        s_small2 = sem("small2_landed")
        s_gm_in = sem("gmlp_in_landed")
        s_out = sem("out_stored")
        w_hi = sem("w_hi")
        w_lo = sem("w_lo")
        w_used = sem("w_used")
        s_ident = sem("ident_landed")
        ev_act = sem("ev_act")
        ev_dve = sem("ev_dve")
        v_chain = sem("dve_chain")
        a_chain = sem("act_chain")
        ms_ready = sem("mean_square_ready")
        r_ready = sem("rsqrt_ready")
        bank_full = sem("bank_full")
        down_rows = sem("down_rows_complete")
        gate_silu = sem("gates_silu")
        gelu_done = sem("gelu_done")
        high_done = sem("qk_high_parts")
        sq_done = sem("squares_summed")
        sqa_done = sem("first_squares_summed")
        gx_done = sem("rows_times_gain")
        gx_pool = sem("rows_times_gain_by_pool")
        hot_r = sem("cmp_hots_copied")
        post_dve = sem("post_by_dve")
        post_scaled = sem("post_scaled")
        post_pool = sem("post_by_pool")
        xt_in = sem("xt_transposed")
        xt_hi = sem("xt_hi")
        xt_lo = sem("xt_lo")
        qn_done = sem("qk_normed")
        s_cmp = sem("cmp_hots_landed")
        cmp_in = sem("cmp_bias_in_psum")
        cmp_out = sem("cmp_bias_ready")
        sc_in = sem("scores_in_psum")
        sc_out = sem("scores_out_of_psum")
        tr_in = sem("transposes_in_psum")
        tr_out = sem("transposes_out_of_psum")
        o_in = sem("o_in_psum")
        o_out = sem("o_out_of_psum")
        e_done = sem("exp_done")
        lf_pre = sem("logf_abs")
        lf_act = sem("logf_ln")
        lf_done = sem("logf_done")
        sp_abs = sem("sp_abs")
        sp_ln = sem("sp_ln")
        sp_done = sem("sp_done")
        a_done = sem("sb_weights_exp")
        tab_done = sem("tables_in_psum")
        tab_out = sem("tables_out")
        setup_dve = sem("setup_dve")
        blk_done = sem("blocks_done")
        hid_act = sem("hidden_gelu")
        hid_rep = sem("hidden_replicated")
        gate_e = sem("gate_exp")
        cs_sub = sem("cmp_sub")
        cs_exp = sem("cmp_exp")
        gm_w = sem("gm_weights_ready")
        gm_n = sem("gm_norm_ready")
        act_hi = sem("act_hi")
        act_lo = sem("act_lo")
        gs_done = sem("ffn_gate_silu")

        def group_cols(phase, chunk):
            return {"in1": CHUNKS1, "out1": W_OUT, "in2": CHUNKS2, "out2": W_OUT}[phase][chunk]

        weights = {"in1": a["w_in"], "out1": a["w_out"], "in2": a["w_in_2"], "out2": a["w_out_2"],
                   "gu": a["w_gate_up_2"], "down": a["w_down_2"]}

        def evac_engine(phase, chunk, t):
            if phase == "out1":
                return "dve"
            return "act" if t % 2 == 0 else "dve"

        ev_count = {}
        n_act = n_dve = 0
        for step in timeline:
            if step[0] == "ev":
                if step[1] == "gu":
                    n_dve += 1
                else:
                    for t in range(NT):
                        if evac_engine(step[1], step[2], t) == "act":
                            n_act += 1
                        else:
                            n_dve += 1
                ev_count[step] = (n_act, n_dve)

        def wait_evacuated(eng, step):
            eng.wait_ge(ev_act, ev_count[step][0])
            eng.wait_ge(ev_dve, ev_count[step][1])

        HEADS = {"fox": (FULL, 4), "moba": (FULL, 4), "swa": (BAND, 4), "slc": (FULL, 8), "win": (FULL, 8)}

        def prev_head(name, h):
            if h:
                return (name, h - 1)
            return {"fox": None, "moba": ("fox", 3), "swa": ("sb", 3), "slc": ("cmp", 3), "win": ("slc", 7)}[name]

        def last_o(head):
            name, h = head
            if name == "sb":
                return ("OS", h)
            if name == "cmp":
                return ("CO", h)
            return ("O", name, h, len(HEADS[name][0]) - 1)

        def head_index(name, h):
            return {"fox": 0, "moba": 4, "swa": 12, "slc": 0, "win": 8}[name] + h

        def segments(plan, g):
            col = 0
            n = sum(len(x) for x in plan[:g])
            for i, j, m in plan[g]:
                yield i, j, m, col, n
                col += m * P
                n += 1

        def width(plan, g):
            return P * sum(m for _, _, m in plan[g])

        GROUP_AT = [0, 512, 1024]
        KINDS1 = {"fox": 0, "moba": 1, "sb": 2, "swa": 3}

        def q_of(name, h):
            e = 64 * (h % 2)
            if name in KINDS1:
                return qkT1[e:e + 64, KINDS1[name] % 2, h // 2, :]
            return qS[:, h, :]

        def k_of(name, h, x=0):
            e = 64 * (h % 2)
            if name in KINDS1:
                return qkT1[e:e + 64, KINDS1[name] % 2, 2 + h // 2, :]
            return kS[0 if name == "slc" else 1][:, x, h // 4, :]

        def v_of(name, h, j):
            if name in ("slc", "win"):
                return V2[:, j, 0 if name == "slc" else 1, :], h // 4
            if name == "swa":
                return V1[:, j, 768:896], h // 2
            lo = 256 * KINDS1[name] + P * (h // 2)
            return V1[:, j, lo:lo + P], h % 2

        def bias_of(name, h, i, m):
            if name == "fox":
                return fox_c[:, h, 0:m * P]
            if name == "moba":
                return bias_moba[:, h, 384 - P * i:512]
            if name == "swa":
                return bias_swa[:, h, 256 - m * P:256]
            return bias_t5[:, h, 384 - P * i:512]

        def q_ready(name):
            return {"slc": ("qt", "q", 3), "win": ("qt", "win", 3)}.get(name, ("qt", name, 3))

        high_index = {}
        for step in timeline:
            if step[0] == "qt" and step[1] in ("q", "slc", "win"):
                high_index[step] = len(high_index) + 1

        e_index = {}
        for step in timeline:
            if step[0] == "S":
                e_index[step[1:]] = len(e_index) + 1

        def evacuate(eng, phase, ch, t):
            act_ = eng is nc.scalar

            def copy(o, i):
                if phase == "out2":
                    return eng.activation(o, i, ACT.Copy) if act_ else eng.tensor_copy(o, i)
                r = rr[:, t:t + 1]
                return eng.activation(o, i, ACT.Copy, scale=r) if act_ else eng.tensor_scalar(o, i, r, None, ALU.mult)

            m = MM[t]
            if phase == "in1":
                if ch in (0, 2, 4):
                    yield copy(qk_nat[:, t, :], m)
                elif ch == 1:
                    yield copy(V1[:, t, 0:256], m[:, 0:256])
                    yield copy(lf_u[:, 4 * t:4 * t + 4], m[:, 256:260])
                elif ch == 3:
                    yield copy(V1[:, t, 256:768], m)
                elif ch == 5:
                    yield copy(qk_nat[:, t, 0:256], m[:, 0:256])
                    for e in range(2):
                        yield copy(qk_nat[:, t, 256:512].rearrange("p (g e d) -> p g e d", g=2, e=2)[:, :, e, :],
                                   m[:, 256:384].rearrange("p (g d) -> p g d", g=2))
                    yield copy(V1[:, t, 768:896], m[:, 384:512])
                else:
                    yield copy(R1[:, t, 512 * (ch - 6):512 * (ch - 6) + 512], m)
            elif phase == "in2":
                if ch == 0:
                    for e in range(2):
                        yield copy(cmp_nat[:, t, :, HD * e:HD * e + HD], m[:, 0:256].rearrange("p (g d) -> p g d", g=4))
                        yield copy(k_nat[:, t, :].rearrange("p (g e d) -> p g e d", g=2, e=2)[:, :, e, :],
                                   m[:, 256:384].rearrange("p (g d) -> p g d", g=2))
                    yield copy(V2[:, t, 0, :], m[:, 384:512])
                elif ch == 1:
                    yield copy(nat2[:, t, :], m)
                elif ch == 2:
                    for e in range(2):
                        yield copy(nat2[:, t, 0:256].rearrange("p (g e d) -> p g e d", g=2, e=2)[:, :, e, :],
                                   m[:, 0:128].rearrange("p (g d) -> p g d", g=2))
                    yield copy(V2[:, t, 1, :], m[:, 128:256])
                    yield copy(g_tmp.rearrange("p (c q) -> p c q", q=4)[:, :, POS[t]], m[:, 256:280])
                elif ch == 3:
                    yield copy(zv[:, t, :], m)
                elif ch == 4:
                    yield copy(R1[:, t, 512:1024], m)
            elif phase == "out2":
                yield copy(R1[:, t, 512 * ch:512 * ch + 512], m)

        chunk_ends = [step for step in timeline if step[0] == "mm" and step[3] == KD - 1 and step[1] not in ("gu", "down")]

        def wait_bank(eng, phase, ch, t):
            if t < NT - 1:
                eng.wait_ge(bank_full, (NT - 1) * chunk_ends.index(("mm", phase, ch, KD - 1)) + t + 1)
            else:
                eng.wait_ge(w_used, first[phase, ch] + KD)

        def by_dve(step):
            return step[3] == 0

        def take_transposed(eng, step):
            _, name, h, g = step
            w = width(HEADS[name][0], g)
            eng.wait_ge(tr_in, nth[step] + 1)
            prev = prev_head(name, h)
            if prev is not None:
                same = prev[0] in HEADS and HEADS[prev[0]][0] is HEADS[name][0]
                eng.wait_ge(o_in, nth[("O", *prev, g) if same else last_o(prev)] + 1)
            dst, src = probT[:, GROUP_AT[g]:GROUP_AT[g] + w], TR[:, 0:w]
            (eng.activation(dst, src, ACT.Copy) if eng is nc.scalar else eng.tensor_copy(dst, src)).then_inc(tr_out, 1)

        def xt_bank(step):
            _, phase, t, hf = step
            if (phase, hf) in (("in1", 0), ("in1", 1), ("out1", 0), ("out2", 1)):
                return ("mm", (2 * t + hf) % 4 if phase == "in1" else t)
            return ("xb", t % 2 if phase == "in2" else t)

        xt_before, by_bank = {}, {}
        for step in timeline:
            if step[0] == "xt":
                xt_before[step] = by_bank.get(xt_bank(step))
                by_bank[xt_bank(step)] = step

        def wait_rows(eng, phase, hf, count):
            eng.wait_ge(count, nth["xt", phase, 3, hf] + 1)

        o_heads = {}
        n_heads = 0
        for step in timeline:
            if step[0] in ("O", "OS", "CO") and (step[0] != "O" or step == last_o((step[1], step[2]))):
                n_heads += 1
            o_heads[step] = n_heads

        o_total1 = o_heads[last_o(("swa", 3))]

        block = ctx.enter_context(nc.Block())

        @block.sync
        def _(sp):
            def bcast(dst, src, n):
                return sp.dma_start(dst, src.rearrange("o n -> o n").broadcast_to([P, n]))

            x_v = a["x"].rearrange("o (t p) d -> p (o t) d", p=P)
            raw_count = [0, 0]

            def load_group(g):
                phase, chunk, n_part, s0, w = groups[g]
                part = n_part if phase == "down" else halves(phase)[n_part]
                if g >= 2:
                    sp.wait_ge(w_lo, groups[g - 2][3] + 4)
                W = weights[phase]
                dst = RAW[:, g % 2, :, :]
                if phase == "down":
                    src = W[0, 256 * chunk:256 * chunk + 256, :].rearrange("(k p) (h n) -> p k h n", p=P, h=2)
                    sp.dma_start(dst.rearrange("p (k h) n -> p k h n", h=2), src).then_inc(s_raw[g % 2], 16)
                    raw_count[g % 2] += 16
                    return
                kk = W[0, 512 * part:512 * part + 512, :].rearrange("(k p) n -> p k n", p=P)
                cols = group_cols(phase, chunk) if phase != "gu" else [(256 * chunk, 256), (FF + 256 * chunk, 256)]
                col = 0
                for start, n in cols:
                    sp.dma_start(dst[:, :, col:col + n], kk[:, :, start:start + n]).then_inc(s_raw[g % 2], 16)
                    raw_count[g % 2] += 16
                    col += n

            def load_tables():
                sp.dma_start(tab1[0:32, :], a["rel_bias"]).then_inc(s_tab, 16)
                sp.dma_start(tab2[0:32, :], a["rel_bias_2"]).then_inc(s_tab, 16)
                for name, lo, n in (("hot_full", 0, 640), ("hot_band", 640, 384), ("hot_t5", 1024, 640)):
                    sp.dma_start(hots[0:33, lo:lo + n], c[name]).then_inc(s_tab, 16)

            def small_loads():
                sp.dma_start(tri_raw[:, 0:512], c["tri_ones"]).then_inc(s_const, 16)
                sp.dma_start(tri_raw[:, 512:640], c["suffix"]).then_inc(s_const, 16)
                sp.dma_start(stage[:, 0:128], c["causal"]).then_inc(s_const, 16)
                sp.dma_start(stage[:, 128:256], c["strict"]).then_inc(s_const, 16)
                with nc.allow_non_contiguous_dma(reason="gains as columns: a few hundred words, once"):
                    for n, name in enumerate(("fox_qk_gain", "moba_qk_gain", "swa_qk_gain")):
                        for e in range(2):
                            sp.dma_start(qk_gain[64 * e:64 * e + 64, 2 * n:2 * n + 2],
                                         a[name].rearrange("o j d -> d (o j)")).then_inc(s_const, 16)
                bcast(b_forget, a["b_forget"], 4).then_inc(s_const, 16)
                bcast(sinks, a["sinks"], 4).then_inc(s_const, 16)

            def store_rows():
                sp.wait_ge(tab_out, 4)
                sp.dma_start(rows_d[0:4, 0:640], rows[0:4, 0:640]).then_inc(s_rows, 16)
                sp.dma_start(rows_d[4:8, 0:384], rows[4:8, 640:1024]).then_inc(s_rows, 16)
                sp.dma_start(rows_d[8:16, 0:640], rows[0:8, 1024:1664]).then_inc(s_rows, 16)

            def replicate_rows():
                sp.wait_ge(s_rows, 48)
                for lo, n in ((0, 4), (8, 8)):
                    for h in range(lo, lo + n):
                        sp.dma_start(rep_d[h], rows_d[h:h + 1, :].broadcast_to([P, 640])).then_inc(s_rep, 16)
                for h in range(4):
                    sp.dma_start(repb_d[h], rows_d[4 + h:5 + h, 0:384].broadcast_to([P, 384])).then_inc(s_rep, 16)

            def skewed(dst, rep, h, n, pitch):
                return sp.dma_start(dst, bass.AP(rep.tensor, h * P * pitch + P - 1, [[pitch - 1, P], [1, n]]))

            def load_bias1():
                sp.wait_ge(s_rep, 16 * 16)
                for h in range(4):
                    skewed(bias_moba[:, h, :], rep_d, h, 512, 640).then_inc(s_bias1, 16)
                for h in range(4):
                    skewed(bias_swa[:, h, :], repb_d, h, 256, 384).then_inc(s_bias1, 16)

            def load_bias2():
                sp.wait_ge(tr_in, nth["F", 3, 2] + 1)
                sp.wait_ge(sp_done, 4)
                for h in range(8):
                    skewed(bias_t5[:, h, :], rep_d, 8 + h, 512, 640).then_inc(s_bias2, 16)

            def load_hot_cmp():
                sp.wait_ge(sc_out, nth["S", "moba", 3, 2] + 1)
                sp.dma_start(hot_cmp[0:33, :], c["hot_cmp"]).then_inc(s_cmp, 16)

            def load_x_again():
                sp.wait_ge(sc_in, nth["S", "swa", 3, 1] + 1)
                sp.dma_start(x_again[:, :, :], x_v).then_inc(s_xa, 16)

            def load_w1(which):
                if which == "k":
                    wait_evacuated(sp, ("ev", "out1", 1))
                else:
                    sp.wait_ge(sc_in, nth["hidden", 0] + 1)
                src = a[f"cmp_w1_{which}_2"]
                sp.dma_start(w1[:, :, :], src.rearrange("o (m p) f -> p (o m) f", p=P)).then_inc(s_w1, 16)

            def load_small2():
                for e in range(2):
                    sp.dma_start(w2k[:, :, 64 * e:64 * e + 64],
                                 a["cmp_w2_k_2"].rearrange("o (f p) d -> p (o f) d", p=P)).then_inc(s_small2, 16)
                sp.dma_start(w2v[:, :, :], a["cmp_w2_v_2"].rearrange("o (f p) d -> p (o f) d", p=P)).then_inc(s_small2, 16)
                with nc.allow_non_contiguous_dma(reason="position rows as columns, once"):
                    for n, name in enumerate(("cmp_pos_k_2", "cmp_pos_v_2")):
                        v = a[name].rearrange("o (m e) d -> e d (o m)", e=2)
                        for e in range(2):
                            sp.dma_start(pos[64 * e:64 * e + 64, 16 * n:16 * n + 16], v[e]).then_inc(s_small2, 16)
                    sp.dma_start(gmlp_b, a["gmlp_b_s_2"].rearrange("o g t -> t (o g)")).then_inc(s_small2, 16)

            def load_gmlp():
                sp.wait_ge(w_used, first["in2", 4] + KD)
                sp.dma_start(ws_nat[:, :, :], a["gmlp_w_s_2"].rearrange("o g t s -> t (o g) s")).then_inc(s_gm_in, 16)
                bcast(ln_g[:, :], a["gmlp_ln_g_2"], 512).then_inc(s_gm_in, 16)
                bcast(ln_b[:, :], a["gmlp_ln_b_2"], 512).then_inc(s_gm_in, 16)

            def load_gain(n, name, pre):
                if pre is not None:
                    sp.wait_ge(pre[0], pre[1])
                bcast(gain[n][:, :], a[name], D).then_inc(s_gain, 16)

            index = {(phase, chunk, part): g for g, (phase, chunk, part, _, _) in enumerate(groups)}
            before = {
                index["in1", 1, 0]: [small_loads],
                index["in1", 1, 1]: [store_rows],
                index["in1", 2, 0]: [replicate_rows],
                index["in1", 2, 1]: [load_bias1],
                index["in1", 4, 0]: [load_small2],
                index["out1", 0, 0]: [lambda: load_gain(0, "norm_mix_pre_2", (gx_pool, NT)),
                                      load_hot_cmp],
                index["out1", 1, 0]: [load_x_again, load_bias2],
                index["in2", 1, 0]: [lambda: load_w1("k")],
                index["in2", 3, 0]: [lambda: load_w1("v"),
                                     lambda: load_gain(0, "norm_ffn_pre_2", (gx_done, nth["gx", "in2", 3, 1] + 1))],
                index["out2", 1, 0]: [load_gmlp, lambda: load_gain(1, "norm_mix_post_2", (o_in, nth["CO", 3] + 1))],
                index["gu", 2, 0]: [lambda: load_gain(1, "norm_ffn_post_2", (post_dve, NT))],
            }
            sp.dma_start(R1[:, 0, :], x_v[:, 0, :]).then_inc(s_x[0], 16)
            bcast(gain[0][:, :], a["norm_gain"], D).then_inc(s_gain, 16)
            sp.dma_start(ident[:, :], c["ident"]).then_inc(s_ident, 16)
            load_tables()
            for t in range(1, NT):
                sp.dma_start(R1[:, t, :], x_v[:, t, :]).then_inc(s_x[t], 16)
            for g in range(len(groups)):
                for f in before.get(g, []):
                    f()
                load_group(g)
            out_v = out.rearrange("o (t p) d -> p (o t) d", p=P)
            for t in range(NT):
                sp.wait_ge(post_dve, NT + t + 1)
                sp.wait_ge(post_pool, NT + t + 1)
                sp.dma_start(out_v[:, t, :], R2[:, t, :]).then_inc(s_out, 16)
            sp.wait_ge(s_rows, 48)
            sp.wait_ge(s_rep, 256)
            sp.wait_ge(s_out, 16 * NT)

        @block.tensor
        def _(pe):
            def product(outp, stationary, moving, start, stop):
                for n, (x, y) in enumerate(((0, 0), (0, 1), (1, 0))):
                    last = pe.matmul(outp, stationary(x), moving(y), start=start and n == 0, stop=stop and n == 2)
                return last

            def distance_rows():
                pe.wait_ge(s_tab, 80)
                pe.wait_ge(setup_dve, 1)
                for n, (bank, table) in enumerate(((SC[0], tab1), (SC[1], tab1), (TR, tab2), (OB, tab2))):
                    lo, hi = (0, 512, 1024, 1536, 1664)[n:n + 2]
                    pe.matmul(bank[0:8, 0:hi - lo], table[0:33, :], hots[0:33, lo:hi], start=True, stop=True).then_inc(tab_done, 1)

            def wait_tr(step):
                if nth[step]:
                    pe.wait_ge(tr_out, nth[step])
                else:
                    pe.wait_ge(tab_out, 3)

            def wait_sc(step):
                if nth[step] >= 2:
                    pe.wait_ge(sc_out, nth[step] - 1)

            for step in timeline:
                what = step[0]
                if what == "rows":
                    distance_rows()
                elif what == "windows":
                    part = step[1]
                    if part == 0:
                        pe.wait_ge(hot_r, 1)
                        pe.wait_ge(tr_out, nth["T", "swa", 3, 1] + 1)
                        pe.wait_ge(o_out, o_total1)
                        pe.wait_ge(xt_lo, nth["xt", "out1", 3, 1] + 1)
                    for u in range(10 * part, min(10 * part + 10, 55)):
                        at_ = 864 - 16 * u
                        last = pe.matmul(WINDOWS[:, 16 * u:16 * u + 16], hot_parts[0:33, at_:at_ + P], tab_parts[0:33, :],
                                         start=True, stop=True)
                    if part == 5:
                        last.then_inc(cmp_in, 1)
                elif what == "xt":
                    _, phase, t, hf = step
                    kind_, i = xt_bank(step)
                    bank = MM[i] if kind_ == "mm" else XB[i]
                    if xt_before[step]:
                        pe.wait_ge(xt_lo, nth[xt_before[step]] + 1)
                    if t == 0:
                        if phase == "in1":
                            pe.wait_ge(s_ident, 16)
                        elif (phase, hf) == ("out1", 0):
                            wait_evacuated(pe, ("ev", "in1", 7))
                        elif (phase, hf) == ("out2", 1):
                            wait_evacuated(pe, ("ev", "in2", 4))
                            pe.wait_ge(sc_out, nth["gm", 3] + 1)
                        elif (phase, hf) == ("out1", 1):
                            pe.wait_ge(tr_out, nth["T", "swa", 3, 1] + 1)
                            pe.wait_ge(sc_out, nth["S", "swa", 3, 1] + 1)
                            pe.wait_ge(o_out, o_total1)
                        elif (phase, hf) == ("out2", 0):
                            pe.wait_ge(tr_out, seen["tr"])
                            pe.wait_ge(sc_out, seen["sc"])
                            pe.wait_ge(o_out, n_heads)
                    if phase == "out2":
                        src = R1[:, t, :]
                    else:
                        pe.wait_ge(gx_pool if by_pool(step) else gx_done, nth["gx", phase, t, hf] + 1)
                        src = {"in1": R2, "out1": R2, "in2": R1, "gu": R1}[phase][:, t, :]
                    for q in range(4):
                        k = 4 * hf + q
                        last = pe.transpose(bank[:, P * q:P * q + P], src[:, P * k:P * k + P], ident[:, :])
                    last.then_inc(xt_in, 1)
                elif what == "mm":
                    _, phase, ch, n = step
                    s = first[phase, ch] + n
                    if phase == "down":
                        if DOWN_TILES - BY_ROWS["down", DOWN_TILES - 1] <= ch < DOWN_TILES - 1:
                            continue
                        tiles = [ch]
                        if ch == DOWN_TILES - 1:
                            tiles = range(DOWN_TILES - BY_ROWS["down", ch], DOWN_TILES)
                        pe.wait_ge(w_lo, first[phase, ch] + 2)
                        pe.wait_ge(act_lo, ch + 1)
                        order = [(ch, hf, t) for hf in ((1, 0) if ch == 0 else (0, 1)) for t in range(NT)]
                        if ch == DOWN_TILES - 1:
                            order = [(kt, hf, t) for t in range(NT) for kt in tiles for hf in range(2)]
                        if ch == 0:
                            wait_evacuated(pe, ("ev", "gu", GU_CHUNKS - 2))
                        for kt, hf, t in order:
                            if (ch, hf, t) == (0, 0, 0):
                                wait_evacuated(pe, ("ev", "gu", GU_CHUNKS - 1))
                            last = product(SET[hf][t], lambda x, t=t, kt=kt: XT[:, kt % 8, x, P * t:P * t + P],
                                           lambda y, hf=hf, kt=kt: WR[:, (first[phase, kt] + hf) % RING, y, :],
                                           kt == 0, kt == DOWN_TILES - 1)
                            if ch == 0:
                                if (hf, t) == (0, NT - 1):
                                    last.then_inc(w_used, 2)
                            elif ch < DOWN_TILES - 1:
                                if t == NT - 1:
                                    last.then_inc(w_used, 1)
                            elif kt == ch and hf == 1:
                                last.then_inc(down_rows, 1)
                        continue
                    by_rows = BY_ROWS.get((phase, ch), 1)
                    if KD - by_rows <= n < KD - 1:
                        continue
                    k = k_tile(phase, n)
                    pe.wait_ge(w_lo, s + 1)
                    if ch == 0 and n % 4 == 0:
                        wait_rows(pe, phase, 1 if phase == "in1" else halves(phase)[n // 4], xt_lo)
                    if phase == "gu" and n == 0:
                        if ch == 0:
                            pe.wait_ge(post_dve, NT)
                        if ch >= 2:
                            wait_evacuated(pe, ("ev", phase, ch - 2))
                    prev = ("ev", phase, ch - 1) if ch else {"in2": ("ev", "out1", 1)}.get(phase)
                    for t in range(NT):
                        if n == 0 and prev and phase != "gu":
                            who = evac_engine(prev[1], prev[2], t)
                            done = ev_count[prev][0 if who == "act" else 1]
                            mine = [u for u in range(NT) if evac_engine(prev[1], prev[2], u) == who]
                            pe.wait_ge(ev_act if who == "act" else ev_dve, done - len(mine) + mine.index(t) + 1)
                        if phase == "gu":
                            last = product(SET[ch % 2][t], lambda x, t=t: WR[:, s % RING, x, P * t:P * t + P],
                                           lambda y: XT[:, k, y, :], n == 0, n == KD - 1)
                        else:
                            w = sum(n_ for _, n_ in group_cols(phase, ch))
                            for back in reversed(range(by_rows if n == KD - 1 else 1)):
                                kb, sb = k_tile(phase, n - back), s - back
                                last = product(MM[t][:, 0:w], lambda x, t=t: XT[:, kb, x, P * t:P * t + P],
                                               lambda y: WR[:, sb % RING, y, 0:w], n - back == 0, n - back == KD - 1)
                                if t == NT - 1 and back:
                                    last.then_inc(w_used, 1)
                            if n == KD - 1 and t < NT - 1:
                                last.then_inc(bank_full, 1)
                    last.then_inc(w_used, 1)
                elif what == "qt":
                    _, name, t = step
                    wait_tr(step)
                    tok = slice(P * t, P * t + P)
                    if name in KINDS1:
                        if name == "sb":
                            wait_evacuated(pe, ("ev", "in1", 4))
                        else:
                            pe.wait_ge(qn_done, nth["qb", name, t] + 1)
                        srcs = [qk_nat[:, t, P * q:P * q + P] for q in range(4)]
                    elif name == "cmp":
                        wait_evacuated(pe, ("ev", "in2", 0))
                        pe.wait_ge(cmp_out, 1)
                        srcs = [cmp_nat[:, t, q, :] for q in range(4)]
                    elif name == "q":
                        wait_evacuated(pe, ("ev", "in2", 1))
                        srcs = [nat2[:, t, P * q:P * q + P] for q in range(4)]
                    else:
                        wait_evacuated(pe, ("ev", "in2", 0 if name == "slc" else 2))
                        srcs = [(k_nat if name == "slc" else nat2)[:, t, P * q:P * q + P] for q in range(2)]
                    for q, src in enumerate(srcs):
                        last = pe.transpose(TR[:, P * q:P * q + P], src, ident[:, :])
                    last.then_inc(tr_in, 1)
                elif what == "C":
                    h = step[1]
                    wait_sc(step)
                    if h == 0:
                        pe.wait_ge(lf_done, 1)
                        pe.wait_ge(tab_out, 2)
                        pe.wait_ge(setup_dve, 3)
                    for kb in range(NT):
                        for x in range(2):
                            last = pe.matmul(SC[nth[step] % 2][:, P * kb:SEQ],
                                             lf_parts[:, x, 4 * kb + h:4 * kb + h + 1].broadcast_to([P, P]),
                                             tri[:, 0:SEQ - P * kb], start=kb == 0 and x == 0, stop=True, skip_group_check=True)
                    last.then_inc(sc_in, 1)
                elif what == "S":
                    _, name, h, g = step
                    plan = HEADS[name][0]
                    wait_sc(step)
                    if h == 0 and g == 0:
                        pe.wait_ge(tr_out, nth[q_ready(name)] + 1)
                        if name == "slc":
                            pe.wait_ge(tr_out, nth["qt", "slc", 3] + 1)
                        if name == "fox":
                            pe.wait_ge(setup_dve, 3)
                    bank = SC[nth[step] % 2]
                    for i, j, m, col, n in segments(plan, g):
                        two = name in ("slc", "win")
                        for x in range(2 if two else 1):
                            last = pe.matmul(bank[:, col:col + m * P], q_of(name, h)[:, P * i:P * i + P],
                                             k_of(name, h, x)[:, P * j:P * (j + m)], start=x == 0, stop=x == 1 or not two)
                        if name == "fox":
                            d = col + (m - 1) * P
                            last = pe.matmul(bank[:, d:d + P], identb[:, :], causal[:, :], start=False, stop=True, skip_group_check=True)
                    last.then_inc(sc_in, 1)
                elif what == "T":
                    _, name, h, g = step
                    plan = HEADS[name][0]
                    wait_tr(step)
                    pe.wait_ge(e_done, e_index[name, h, g])
                    buf = prob[:, head_index(name, h) % 2, GROUP_AT[g]:GROUP_AT[g] + width(plan, g)]
                    for q in range(width(plan, g) // P):
                        last = pe.transpose(TR[:, P * q:P * q + P], buf[:, P * q:P * q + P], ident[:, :])
                    last.then_inc(tr_in, 1)
                elif what == "O":
                    _, name, h, g = step
                    plan = HEADS[name][0]
                    pe.wait_ge(tr_out, nth["T", name, h, g] + 1)
                    if g == 0:
                        if name == "fox" and h == 0:
                            wait_evacuated(pe, ("ev", "in1", 1))
                            pe.wait_ge(tab_out, 4)
                        elif o_heads[step]:
                            pe.wait_ge(o_out, o_heads[step])
                        if name == "moba" and h == 0:
                            wait_evacuated(pe, ("ev", "in1", 3))
                        if name == "swa" and h == 0:
                            wait_evacuated(pe, ("ev", "in1", 5))
                        if name == "slc" and h == 0:
                            wait_evacuated(pe, ("ev", "in2", 0))
                        if name == "win" and h == 0:
                            wait_evacuated(pe, ("ev", "in2", 2))
                    for i, j, m, col, n in segments(plan, g):
                        for b in range(m):
                            at_ = GROUP_AT[g] + col + b * P
                            last = pe.matmul(OB[:, P * n:P * n + P], probT[:, at_:at_ + P], v_of(name, h, j + b)[0],
                                             start=b == 0, stop=b == m - 1)
                    last.then_inc(o_in, 1)
                elif what == "Z":
                    _, h, g = step
                    wait_sc(step)
                    if h == 0 and g == 0:
                        pe.wait_ge(tr_out, nth["qt", "sb", 3] + 1)
                    bank = SC[nth[step] % 2]
                    for j in KEYS[g]:
                        col = KEY_COLS[j] - GROUP_AT[g]
                        w = SEQ - P * j
                        pe.matmul(bank[:, col:col + w], k_of("sb", h)[:, P * j:P * j + P], q_of("sb", h)[:, P * j:SEQ],
                                  start=True, stop=True)
                        last = pe.matmul(bank[:, col:col + P], identb[:, :], strict[:, :], start=False, stop=True, skip_group_check=True)
                    last.then_inc(sc_in, 1)
                elif what == "F":
                    _, h, g = step
                    wait_tr(step)
                    pe.wait_ge(sp_done, h + 1)
                    for j in KEYS[g]:
                        col = KEY_COLS[j] - GROUP_AT[g]
                        for jj in range(j, NT):
                            w = SEQ - P * jj
                            off = P * (jj - j)
                            for x in range(2):
                                last = pe.matmul(TR[:, col + off:col + off + w], suffix[:, :] if jj == j else tri[:, P:2 * P],
                                                 soft_parts[:, x, KEY_COLS[jj]:KEY_COLS[jj] + w],
                                                 start=jj == j and x == 0, stop=True, skip_group_check=True)
                    last.then_inc(tr_in, 1)
                elif what == "OS":
                    h = step[1]
                    pe.wait_ge(a_done, 3 * h + 3)
                    pe.wait_ge(o_out, o_heads[step] - 1)
                    if h == 0:
                        wait_evacuated(pe, ("ev", "in1", 3))
                    for i in range(NT):
                        for j in range(i + 1):
                            at_ = KEY_COLS[j] + P * (i - j)
                            last = pe.matmul(OB[:, P * i:P * i + P], probT[:, at_:at_ + P], v_of("sb", h, j)[0],
                                             start=j == 0, stop=j == i)
                    last.then_inc(o_in, 1)
                elif what == "hidden":
                    kv = step[1]
                    wait_sc(step)
                    pe.wait_ge(s_w1, 16 * (kv + 1))
                    pe.wait_ge(blk_done, 1)
                    for f in range(2):
                        for m in range(16):
                            last = pe.matmul(SC[nth[step] % 2][:, 64 * f:64 * f + 64], w1[:, m, P * f:P * f + P],
                                             blocks[:, kv, m, :], start=m == 0, stop=m == 15)
                    last.then_inc(sc_in, 1)
                elif what == "cmpkv":
                    wait_sc(step)
                    pe.wait_ge(hid_rep, 1)
                    pe.wait_ge(hid_act, 2)
                    pe.wait_ge(s_small2, 16 * 8)
                    bank = SC[nth[step] % 2]
                    for f in range(2):
                        pe.matmul(bank[:, 0:64], w2k[:, f, :], hidT[:, 0, f, :], start=f == 0, stop=f == 1)
                    for g in range(2):
                        for f in range(2):
                            last = pe.matmul(bank[:, 64 + 64 * g:128 + 64 * g], hidV[:, f, g, :], w2v[:, f, :], start=f == 0, stop=f == 1)
                    last.then_inc(sc_in, 1)
                elif what == "CS":
                    i = step[1]
                    wait_sc(step)
                    if i == 0:
                        pe.wait_ge(sc_out, nth["cmpkv",] + 1)
                        pe.wait_ge(tr_out, nth["qt", "q", 3] + 1)
                    for h in range(8):
                        last = pe.matmul(SC[nth[step] % 2][:, 64 * h:64 * h + 64], qS[:, h, P * i:P * i + P],
                                         kcS[:, h // 4, :, :].rearrange("p x n -> p (x n)"), start=True, stop=True)
                    last.then_inc(sc_in, 1)
                elif what == "CT":
                    i = step[1]
                    wait_tr(step)
                    pe.wait_ge(cs_exp, i + 1)
                    for g in range(2):
                        last = pe.transpose(TR[:, P * g:P * g + P], prob[:, 0, 256 * i + P * g:256 * i + P * g + P], ident[:, :])
                    last.then_inc(tr_in, 1)
                elif what == "CO":
                    i = step[1]
                    pe.wait_ge(tr_out, nth["CT", i] + 1)
                    pe.wait_ge(o_out, o_heads[step] - 1)
                    for g in range(2):
                        last = pe.matmul(OB[:, 256 * g:256 * g + 256], probT[:, P * g:P * g + P],
                                         vbd[:, g, :, :].rearrange("p r d -> p (r d)"), start=True, stop=True)
                    last.then_inc(o_in, 1)
                elif what == "gm_w":
                    u = step[1]
                    wait_tr(step)
                    pe.wait_ge(s_gm_in, 48)
                    for q in range(4):
                        last = pe.transpose(TR[:, P * q:P * q + P], ws_nat[:, 4 * u + q, :], ident[:, :])
                    last.then_inc(tr_in, 1)
                elif what == "gm":
                    u = step[1]
                    wait_sc(step)
                    pe.wait_ge(gm_n, NT)
                    pe.wait_ge(tr_out, nth["gm_w", 1] + 1)
                    for q in range(2):
                        g = 2 * u + q
                        last = pe.matmul(SC[nth[step] % 2][:, 256 * q:256 * q + 256], wsT[:, g, :],
                                         zv[:, :, HD * g:HD * g + HD], start=True, stop=True)
                    last.then_inc(sc_in, 1)

        @block.scalar
        def _(act):
            link_n = [0]

            def link(ins):
                link_n[0] += 1
                ins.then_inc(a_chain, 1)
                act.wait_ge(a_chain, link_n[0])

            raw_seen = [0, 0]
            group_of = {}
            for g, (phase, chunk, part, s0, w) in enumerate(groups):
                n = 1 if phase == "down" else (2 if phase == "gu" else len(group_cols(phase, chunk)))
                raw_seen[g % 2] += 16 * n
                for q in range(4):
                    group_of[s0 + q] = (g, q, w, raw_seen[g % 2])

            for step in timeline:
                what = step[0]
                if what == "split":
                    s = step[1]
                    g, q, w, landed = group_of[s]
                    act.wait_ge(s_raw[g % 2], landed)
                    if s >= RING:
                        act.wait_ge(w_used, s - RING + 1)
                    act.activation(WR[:, s % RING, 0, 0:w], RAW[:, g % 2, q, 0:w], ACT.Copy).then_inc(w_hi, 1)
                elif what == "xt":
                    _, phase, t, hf = step
                    act.wait_ge(xt_in, nth[step] + 1)
                    if t == 0 and phase != "in1":
                        p0, c0 = {"out1": ("in1", 7), "in2": ("out1", 1), "out2": ("in2", 4), "gu": ("out2", 1)}[phase]
                        act.wait_ge(w_used, first[p0, c0] + 4 * (halves(p0).index(hf) + 1))
                        if (phase, hf) == ("out2", 0):
                            act.wait_ge(sc_in, nth["gm", 3] + 1)
                            act.wait_ge(gm_n, NT)
                    kind_, i = xt_bank(step)
                    act.activation(XT[:, 4 * hf:4 * hf + 4, 0, P * t:P * t + P],
                                   (MM[i] if kind_ == "mm" else XB[i]).rearrange("p (q n) -> p q n", q=4), ACT.Copy).then_inc(xt_hi, 1)
                elif what == "qt" and step[1] in ("q", "slc", "win"):
                    _, name, t = step
                    tok = slice(P * t, P * t + P)
                    act.wait_ge(tr_in, nth[step] + 1)
                    if name == "q":
                        for e in range(2):
                            own = slice(64 * e, 64 * e + 64)
                            last = act.activation(qS[own, :, tok].rearrange("p (q e) n -> p q e n", e=2)[:, :, e, :],
                                                  TR[own].rearrange("p (q n) -> p q n", q=4), ACT.Copy, scale=QSCALE)
                    else:
                        if name == "slc" and t == 0:
                            act.wait_ge(sc_in, nth["hidden", 1] + 1)
                        last = act.activation(kS[0 if name == "slc" else 1][:, 0, :, tok],
                                              TR[:, 0:256].rearrange("p (g n) -> p g n", g=2), ACT.Copy)
                    last.then_inc(high_done, 1)
                elif what == "sqa":
                    t = step[1]
                    if t == 0:
                        wait_evacuated(act, ("ev", "out2", 0))
                        act.wait_ge(tr_in, seen["tr"])
                    act.activation(squares[:, t, :], R1[:, t, 0:512], ACT.Square, accum_out=ss_a[:, t:t + 1]).then_inc(sqa_done, 1)
                elif what == "sq":
                    _, name, t = step
                    junk = (squares_gu if name == "gu" else prob)[:, t % 2, 0:D]
                    if name in ("in1", "in2", "gu") and t >= 2:
                        act.wait_ge(sq_done, nth["sq", name, t - 2] + 1)
                    if name == "ffn" and t:
                        act.wait_ge(sq_done, nth[step])
                    if name == "in1":
                        act.wait_ge(s_x[t], 16)
                        act.activation(junk, R1[:, t, :], ACT.Square, accum_out=ss[:, t:t + 1]).then_inc(sq_done, 1)
                    elif name == "in2":
                        if t == 0:
                            act.wait_ge(tr_in, nth["T", "swa", 3, 1] + 1)
                            wait_evacuated(act, ("ev", "out1", 1))
                        act.activation(junk, R2[:, t, :], ACT.Square, accum_out=ss[:, t:t + 1]).then_inc(sq_done, 1)
                    elif name == "mix":
                        wait_bank(act, "out2", 1, t)
                        if t == 0:
                            act.wait_ge(sqa_done, NT)
                        act.activation(squares[:, t, :], MM[t], ACT.Square, accum_out=ss[:, t:t + 1]).then_inc(sq_done, 1)
                    elif name == "gu":
                        if t == 0:
                            act.wait_ge(o_in, seen["o"])
                        act.wait_ge(post_dve, t + 1)
                        act.wait_ge(post_pool, t + 1)
                        act.activation(junk, R2[:, t, :], ACT.Square, accum_out=ss[:, t:t + 1]).then_inc(sq_done, 1)
                    else:
                        act.wait_ge(down_rows, t + 1)
                        act.activation(gated[:, 0, :], SET[0][t], ACT.Square, accum_out=ss_a[:, t:t + 1])
                        act.activation(gated[:, 1, :], SET[1][t], ACT.Square, accum_out=ss[:, t:t + 1]).then_inc(sq_done, 1)
                elif what == "ev":
                    _, phase, ch = step
                    if phase == "gu":
                        act.wait_ge(w_used, first[phase, ch] + KD)
                        for m in range(2):
                            if ch:
                                act.wait_ge(ev_dve, ev_count["ev", "gu", ch - 1][1])
                            act.activation(gated[:, m, :], SET[ch % 2][m], ACT.Silu).then_inc(gs_done, 1)
                        continue
                    if (phase, ch) in (("in1", 0), ("in2", 0)):
                        act.wait_ge(r_ready, nth["ms", phase, 0] + 1)
                    if (phase, ch) == ("in2", 0):
                        act.wait_ge(sq_done, nth["sq", "in2", 3] + 1)
                    if (phase, ch) == ("in1", 4):
                        act.wait_ge(tr_in, nth["qt", "moba", 3] + 1)
                    if (phase, ch) == ("in1", 2):
                        act.wait_ge(tr_in, nth["qt", "fox", 3] + 1)
                    if (phase, ch) == ("in1", 5):
                        act.wait_ge(tr_in, nth["qt", "sb", 3] + 1)
                    if (phase, ch) == ("in1", 6):
                        act.wait_ge(gx_done, nth["gx", "in1", 3, 0] + 1)
                        act.wait_ge(gx_pool, NT)
                    if (phase, ch) == ("in2", 2):
                        act.wait_ge(tr_in, nth["qt", "q", 3] + 1)
                    if (phase, ch) == ("in2", 3):
                        act.wait_ge(sc_in, nth["hidden", 1] + 1)
                        act.wait_ge(sc_out, nth["cmpkv",] + 1)
                    if (phase, ch) == ("out2", 0):
                        act.wait_ge(xt_in, nth["xt", "out2", 3, 0] + 1)
                    for t in range(NT):
                        if evac_engine(phase, ch, t) != "act":
                            continue
                        wait_bank(act, phase, ch, t)
                        for ins in evacuate(act, phase, ch, t):
                            last = ins
                        last.then_inc(ev_act, 1)
                elif what == "logf":
                    act.wait_ge(lf_pre, 1)
                    link(act.activation(lf_a, lf_a, ACT.Exp))
                    act.activation(lf_a, lf_a, ACT.Ln, bias=1.0).then_inc(lf_act, 1)
                elif what == "S":
                    _, name, h, g = step
                    plan = HEADS[name][0]
                    act.wait_ge(sc_out, nth[step] + 1)
                    hi = head_index(name, h)
                    buf = prob[:, hi % 2, GROUP_AT[g]:GROUP_AT[g] + width(plan, g)]
                    sl = 4 * (hi % 4)
                    for i, j, m, col, n in segments(plan, g):
                        last = act.activation(buf[:, col:col + m * P], buf[:, col:col + m * P], ACT.Exp,
                                              bias=nm[:, sl + n:sl + n + 1], accum_out=sm[:, sl + n:sl + n + 1])
                        if name == "swa":
                            last = act.activation(es[:, sl + n:sl + n + 1], nm[:, sl + n:sl + n + 1], ACT.Exp, bias=sinks[:, h:h + 1])
                    last.then_inc(e_done, 1)
                elif what == "sp":
                    h = step[1]
                    act.wait_ge(sp_abs, h + 1)
                    link(act.activation(soft[:, :], soft[:, :], ACT.Exp))
                    act.activation(soft[:, :], soft[:, :], ACT.Ln, bias=1.0).then_inc(sp_ln, 1)
                elif what == "F":
                    _, h, g = step
                    act.wait_ge(tr_out, nth[step] + 1)
                    if g == 0:
                        act.wait_ge(o_in, nth[last_o(("sb", h - 1) if h else ("moba", 3))] + 1)
                    lo = GROUP_AT[g]
                    w = sum(SEQ - P * j for j in KEYS[g])
                    act.activation(probT[:, lo:lo + w], prob[:, h % 2, lo:lo + w], ACT.Exp).then_inc(a_done, 1)
                elif what == "T" and not by_dve(step):
                    take_transposed(act, step)
                elif what == "hidden":
                    kv = step[1]
                    act.wait_ge(sc_in, nth[step] + 1)
                    if kv == 0:
                        act.wait_ge(tr_in, nth["qt", "cmp", 3] + 1)
                    act.activation(hidT[:, kv, :, :], SC[nth[step] % 2][:, 0:128].rearrange("p (f n) -> p f n", f=2),
                                   ACT.Gelu_apprx_tanh).then_inc(hid_act, 1)
                elif what == "gates1":
                    hf = step[1]
                    wait_evacuated(act, ("ev", "in1", 6 + hf))
                    for t in range(NT):
                        v = R1[:, t, 512 * hf:512 * hf + 512]
                        act.activation(v, v, ACT.Silu).then_inc(gate_silu, 1)
                elif what == "gelu":
                    wait_evacuated(act, ("ev", "in2", 3 + step[1]))
                    for t in range(NT):
                        v = R1[:, t, 512:D] if step[1] else zv[:, t, :]
                        act.activation(v, v, ACT.Gelu_apprx_tanh).then_inc(gelu_done, 1)
                elif what == "gates":
                    wait_evacuated(act, ("ev", "in2", 2))
                    act.activation(g_tmp, g_tmp, ACT.Exp, scale=-1.0).then_inc(gate_e, 1)
                elif what == "CS":
                    i = step[1]
                    act.wait_ge(cs_sub, i + 1)
                    act.activation(prob[:, 0, 256 * i:256 * i + 256], prob[:, 0, 256 * i:256 * i + 256], ACT.Exp).then_inc(cs_exp, 1)
                elif what == "act":
                    kt = step[1]
                    act.wait_ge(ev_dve, ev_count["ev", "gu", kt // 2][1])
                    if kt < 8:
                        act.wait_ge(w_used, first["gu", GU_CHUNKS - 1] + kt + 1)
                    if kt >= 8:
                        act.wait_ge(w_used, first["down", kt - 8] + 2)
                    act.activation(XT[:, kt % 8, 0, :], actT[:, kt, :], ACT.Copy).then_inc(act_hi, 1)

        @block.vector
        def _(dve):
            link_n = [0]

            def link(ins):
                link_n[0] += 1
                ins.then_inc(v_chain, 1)
                dve.wait_ge(v_chain, link_n[0])

            dve.memset(half, -0.5)
            dve.memset(tab1[32:33, :], 1.0)
            dve.memset(tab2[32:33, :], 1.0).then_inc(setup_dve, 1)
            dve.sem_inc(setup_dve, 1)

            def setup():
                dve.wait_ge(s_const, 16 * 12)
                dve.wait_ge(s_ident, 16)
                dve.tensor_copy(identb[:, :], ident[:, :])
                dve.tensor_copy(causal[:, :], stage[:, 0:128])
                dve.tensor_copy(tri[:, :], tri_raw[:, 0:512])
                dve.tensor_copy(suffix[:, :], tri_raw[:, 512:640])
                dve.tensor_copy(strict[:, :], stage[:, 128:256])
                for n in range(3):
                    last = dve.tensor_scalar(qk_gain[:, 2 * n:2 * n + 1], qk_gain[:, 2 * n:2 * n + 1], QSCALE, None, ALU.mult)
                last.then_inc(setup_dve, 1)
                dve.wait_ge(setup_dve, 3)

            for step in timeline:
                what = step[0]
                if what == "rows_out":
                    for n, bank in enumerate((SC[0], SC[1], TR, OB)):
                        lo, hi = (0, 512, 1024, 1536, 1664)[n:n + 2]
                        dve.wait_ge(tab_done, n + 1)
                        dve.tensor_copy(rows[0:8, lo:hi], bank[0:8, 0:hi - lo]).then_inc(tab_out, 1)
                if step == ("ev", "in1", 0):
                    setup()
                if step == ("gx", "in2", 0, 0):
                    dve.wait_ge(s_cmp, 16)
                    dve.wait_ge(sc_in, nth["S", "swa", 3, 1] + 1)
                    dve.tensor_copy(hot_parts[0:33, :], hot_cmp[0:33, :])
                    link(dve.tensor_copy(tab_parts[0:33, 0:8], tab2[0:33, :]))
                    dve.tensor_tensor(tab_parts[0:33, 8:16], tab2[0:33, :], tab_parts[0:33, 0:8].bitcast(F32),
                                      ALU.subtract).then_inc(hot_r, 1)
                if what == "gx" and not by_pool(step):
                    _, phase, t, hf = step
                    cols = slice(512 * hf, 512 * hf + 512)
                    if phase == "in1":
                        dve.wait_ge(s_x[t], 16)
                        if t == 0:
                            dve.wait_ge(s_gain, 16)
                        ins = dve.tensor_tensor(R2[:, t, cols], R1[:, t, cols], gain[0][:, cols], ALU.mult)
                    elif phase == "out1":
                        if t == 0:
                            dve.wait_ge(gate_silu, NT * (hf + 1))
                            last_head = ("O", "moba", 3, 2) if hf == 0 else ("O", "swa", 3, 1)
                            dve.wait_ge(o_out, o_heads[last_head])
                        ins = dve.tensor_tensor(R2[:, t, cols], R2[:, t, cols], R1[:, t, cols], ALU.mult)
                    elif phase == "in2":
                        if t == 0:
                            wait_evacuated(dve, ("ev", "out1", hf))
                            dve.wait_ge(s_gain, 32)
                        ins = dve.tensor_tensor(R1[:, t, cols], R2[:, t, cols], gain[0][:, cols], ALU.mult)
                    else:
                        if hf == 0:
                            dve.wait_ge(r_ready, nth["ms", "gu", t] + 1)
                        if t == 0:
                            dve.wait_ge(s_gain, 64)
                        ins = dve.scalar_tensor_tensor(out=R1[:, t, cols], in0=R2[:, t, cols], scalar=rr[:, t:t + 1],
                                                       in1=gain[0][:, cols], op0=ALU.mult, op1=ALU.mult)
                    ins.then_inc(gx_done, 1)
                elif what == "ms":
                    _, name, t = step
                    if name in ("in1", "in2"):
                        dve.wait_ge(sq_done, nth["sq", name, 3] + 1)
                        dve.tensor_scalar(ss, ss, 1.0 / D, EPS, ALU.mult, ALU.add).then_inc(ms_ready, 1)
                    else:
                        dve.wait_ge(sq_done, nth["sq", name, t] + 1)
                        if name != "gu":
                            link(dve.tensor_tensor(ss[:, t:t + 1], ss[:, t:t + 1], ss_a[:, t:t + 1], ALU.add))
                        dve.tensor_scalar(ss[:, t:t + 1], ss[:, t:t + 1], 1.0 / D, EPS, ALU.mult, ALU.add).then_inc(ms_ready, 1)
                elif what == "cmp_bias":
                    dve.wait_ge(cmp_in, 1)
                    link(dve.memset(cmp_bias[:, :, :, :], MASK))
                    for i in range(NT):
                        at_ = 16 * (24 - 8 * i)
                        w = WINDOWS[:, at_:at_ + 16 * NCMP].rearrange("p (n x h) -> p n x h", x=2, h=8)
                        dst = cmp_bias[:, i, :, 0:NCMP].rearrange("p h n -> p n h")
                        link(dve.tensor_copy(dst, w[:, :, 1, :]))
                        last = dve.tensor_tensor(dst, dst, w[:, :, 0, :], ALU.add)
                    last.then_inc(cmp_out, 1)
                elif what == "xt":
                    _, phase, t, hf = step
                    kind_, i = xt_bank(step)
                    dve.wait_ge(xt_hi, nth[step] + 1)
                    hi_part = XT[:, 4 * hf:4 * hf + 4, 0, P * t:P * t + P]
                    dve.tensor_tensor(XT[:, 4 * hf:4 * hf + 4, 1, P * t:P * t + P],
                                      (MM[i] if kind_ == "mm" else XB[i]).rearrange("p (q n) -> p q n", q=4), hi_part.bitcast(F32),
                                      ALU.subtract).then_inc(xt_lo, 1)
                elif what == "ev":
                    _, phase, ch = step
                    if phase == "gu":
                        for m in range(2):
                            dve.wait_ge(gs_done, 2 * ch + m + 1)
                            if ch == 0:
                                dve.wait_ge(tr_in, seen["tr"])
                            last = dve.tensor_tensor(actT[:, 2 * ch + m, :], SET[ch % 2][2 + m], gated[:, m, :], ALU.mult)
                        last.then_inc(ev_dve, 1)
                        continue
                    if (phase, ch) == ("in1", 6):
                        dve.wait_ge(gx_done, nth["gx", "in1", 3, 0] + 1)
                        dve.wait_ge(gx_pool, NT)
                    if (phase, ch) == ("in1", 2):
                        dve.wait_ge(tr_in, nth["qt", "fox", 3] + 1)
                    if (phase, ch) == ("in1", 4):
                        dve.wait_ge(tr_in, nth["qt", "moba", 3] + 1)
                    if (phase, ch) == ("in1", 5):
                        dve.wait_ge(tr_in, nth["qt", "sb", 3] + 1)
                    if (phase, ch) == ("in2", 2):
                        dve.wait_ge(tr_in, nth["qt", "q", 3] + 1)
                    if (phase, ch) == ("in2", 3):
                        dve.wait_ge(sc_in, nth["hidden", 1] + 1)
                        dve.wait_ge(sc_out, nth["cmpkv",] + 1)
                    if (phase, ch) == ("out2", 0):
                        dve.wait_ge(xt_in, nth["xt", "out2", 3, 0] + 1)
                    if (phase, ch) in (("in1", 0), ("in2", 0)):
                        dve.wait_ge(r_ready, nth["ms", phase, 0] + 1)
                    if (phase, ch) == ("in2", 0):
                        dve.wait_ge(sq_done, nth["sq", "in2", 3] + 1)
                    for t in range(NT):
                        if evac_engine(phase, ch, t) != "dve":
                            continue
                        wait_bank(dve, phase, ch, t)
                        if phase == "out1":
                            dve.wait_ge(s_xa, 16)
                            cols = slice(512 * ch, 512 * ch + 512)
                            dve.tensor_tensor(R2[:, t, cols], MM[t], x_again[:, t, cols], ALU.add).then_inc(ev_dve, 1)
                            continue
                        for ins in evacuate(dve, phase, ch, t):
                            last = ins
                        last.then_inc(ev_dve, 1)
                elif what == "qa":
                    _, name, t = step
                    wait_evacuated(dve, ("ev", "in1", {"fox": 0, "moba": 2, "swa": 5}[name]))
                    link(dve.tensor_tensor(sq[:, :], qk_nat[:, t, :], qk_nat[:, t, :], ALU.mult))
                    link(dve.tensor_reduce(ms8, sq[:, :].rearrange("p (h d) -> p h d", d=HD), AX.X, ALU.add))
                    dve.tensor_scalar(ms8, ms8, 1.0 / HD, EPS, ALU.mult, ALU.add).then_inc(ms_ready, 1)
                elif what == "qb":
                    _, name, t = step
                    dve.wait_ge(r_ready, nth["qa", name, t] + 1)
                    v = qk_nat[:, t, :].rearrange("p (h d) -> p h d", d=HD)
                    dve.tensor_tensor(v, v, rr8.unsqueeze(2).broadcast_to([P, 8, HD]), ALU.mult).then_inc(qn_done, 1)
                elif what == "qt":
                    _, name, t = step
                    dve.wait_ge(tr_in, nth[step] + 1)
                    tok = slice(P * t, P * t + P)
                    if name in KINDS1:
                        kd = KINDS1[name]
                        if t == 0 and name == "sb":
                            dve.wait_ge(sc_in, nth["S", "fox", 3, 2] + 1)
                        if t == 0 and name == "swa":
                            dve.wait_ge(sc_in, nth["S", "moba", 3, 2] + 1)
                        for part in range(2):
                            dst = qkT1[:, kd % 2, 2 * part:2 * part + 2, tok]
                            src = TR[:, 256 * part:256 * part + 256].rearrange("p (q n) -> p q n", q=2)
                            if name == "sb":
                                last = dve.tensor_scalar(dst, src, QSCALE if part == 0 else 1.0, None, ALU.mult)
                            else:
                                gcol = 2 * {"fox": 0, "moba": 1, "swa": 2}[name] + part
                                last = dve.tensor_scalar(dst, src, qk_gain[:, gcol:gcol + 1], None, ALU.mult)
                    elif name == "q":
                        dve.wait_ge(high_done, high_index[step])
                        for e in range(2):
                            own, other = slice(64 * e, 64 * e + 64), slice(64 - 64 * e, 128 - 64 * e)
                            v = qS[:, :, tok].rearrange("p (q e) n -> p q e n", e=2)[:, :, e, :]
                            last = dve.scalar_tensor_tensor(out=v[other], in0=TR[own].rearrange("p (q n) -> p q n", q=4), scalar=QSCALE,
                                                            in1=v[own].bitcast(F32), op0=ALU.mult, op1=ALU.subtract)
                    elif name == "cmp":
                        if t == 0:
                            dve.wait_ge(xt_in, nth["xt", "in2", 3, 1] + 1)
                        src = TR.rearrange("p (v g n) -> p v g n", v=2, g=2)
                        for v in range(2):
                            dve.tensor_copy(cmpT[0:64, v, :, tok], src[0:64, v])
                            lo = 1 if t == 0 else 0
                            last = dve.tensor_copy(cmpT[64:128, v, :, P * t - 1 + lo:P * t + P - 1], src[64:128, v, :, lo:P])
                    else:
                        dve.wait_ge(high_done, high_index[step])
                        v = kS[0 if name == "slc" else 1][:, :, :, tok]
                        last = dve.tensor_tensor(v[:, 1], TR[:, 0:256].rearrange("p (g n) -> p g n", g=2), v[:, 0].bitcast(F32), ALU.subtract)
                    last.then_inc(tr_out, 1)
                elif what == "logf":
                    wait_evacuated(dve, ("ev", "in1", 1))
                    link(dve.tensor_tensor(lf_u.rearrange("p (t h) -> p t h", h=4), lf_u.rearrange("p (t h) -> p t h", h=4),
                                           b_forget.unsqueeze(1).broadcast_to([P, 4, 4]), ALU.add))
                    dve.scalar_tensor_tensor(out=lf_a, in0=lf_u, scalar=-1.0, in1=lf_u, op0=ALU.mult, op1=ALU.min).then_inc(lf_pre, 1)
                    dve.wait_ge(lf_pre, 1)
                    link(dve.tensor_scalar(lf_u, lf_u, -1.0, 0.0, ALU.mult, ALU.max))
                    dve.wait_ge(lf_act, 1)
                    link(dve.tensor_tensor(lf, lf_u, lf_a, ALU.add))
                    link(dve.tensor_copy(lf_parts[:, 0, :], lf))
                    dve.tensor_tensor(lf_parts[:, 1, :], lf, lf_parts[:, 0, :].bitcast(F32), ALU.subtract).then_inc(lf_done, 1)
                elif what == "C":
                    h = step[1]
                    dve.wait_ge(sc_in, nth[step] + 1)
                    dve.tensor_copy(fox_c[:, h, :], SC[nth[step] % 2]).then_inc(sc_out, 1)
                elif what == "S":
                    _, name, h, g = step
                    plan = HEADS[name][0]
                    hi = head_index(name, h)
                    buf = prob[:, hi % 2, GROUP_AT[g]:GROUP_AT[g] + width(plan, g)]
                    sl = 4 * (hi % 4)
                    dve.wait_ge(sc_in, nth[step] + 1)
                    if name == "swa" and h < 2:
                        if g == 0:
                            dve.wait_ge(a_done, 3 * (2 + h) + 3)
                    elif name == "slc" and h < 2:
                        dve.wait_ge(tr_in, nth["CT", NT - 1] + 1)
                    elif name == "fox" and h < 2:
                        dve.wait_ge(sq_done, 4)
                        if h == 0 and g == 0:
                            dve.wait_ge(sc_out, nth["C", 0] + 1)
                    elif name in ("moba", "win") and h < 2:
                        dve.wait_ge(tr_in, nth["T", "fox" if name == "moba" else "slc", HEADS["fox" if name == "moba" else "slc"][1] - 2 + h, g] + 1)
                    else:
                        dve.wait_ge(tr_in, nth["T", name, h - 2, g] + 1)
                    if h == 0 and g == 0 and name in ("moba", "swa"):
                        dve.wait_ge(s_bias1, 128)
                    if h == 0 and g == 0 and name == "slc":
                        dve.wait_ge(s_bias2, 128)
                    if name == "fox" and g == 0:
                        dve.wait_ge(sc_out, nth["C", h] + 1)
                    first_n = None
                    for i, j, m, col, n in segments(plan, g):
                        first_n = n if first_n is None else first_n
                        last = dve.tensor_tensor_reduce(buf[:, col:col + m * P], SC[nth[step] % 2][:, col:col + m * P],
                                                        bias_of(name, h, i, m), 1.0, -3e38, ALU.add, ALU.max,
                                                        mx[:, sl + n:sl + n + 1])
                    link(last)
                    ns = slice(sl + first_n, sl + n + 1)
                    if name == "swa":
                        dve.tensor_scalar(nm[:, ns], mx[:, ns], sinks[:, h:h + 1], -1.0, ALU.max, ALU.mult).then_inc(sc_out, 1)
                    else:
                        dve.tensor_scalar(nm[:, ns], mx[:, ns], -1.0, None, ALU.mult).then_inc(sc_out, 1)
                elif what == "T" and by_dve(step):
                    take_transposed(dve, step)
                elif what == "O":
                    _, name, h, g = step
                    plan = HEADS[name][0]
                    if step != last_o((name, h)):
                        continue
                    sl = 4 * (head_index(name, h) % 4)
                    dve.wait_ge(o_in, nth[step] + 1)
                    if name == "swa":
                        link(dve.tensor_tensor(sm[:, sl:sl + 4], sm[:, sl:sl + 4], es[:, sl:sl + 4], ALU.add))
                    link(dve.reciprocal(ri[:, sl:sl + 4], sm[:, sl:sl + 4]))
                    if name in ("slc", "win"):
                        gc = 4 * (3 * h + (1 if name == "slc" else 2))
                        link(dve.tensor_tensor(ri[:, sl:sl + 4], ri[:, sl:sl + 4], gates[:, gc:gc + 4], ALU.mult))
                    for gg in range(len(plan)):
                        for i, j, m, col, n in segments(plan, gg):
                            at_ = P * n + HD * v_of(name, h, 0)[1]
                            src = OB[:, at_:at_ + HD]
                            f = ri[:, sl + n:sl + n + 1]
                            if name in ("slc", "win"):
                                dst = R1[:, i, HD * h:HD * h + HD]
                                last = dve.scalar_tensor_tensor(out=dst, in0=src, scalar=f, in1=dst, op0=ALU.mult, op1=ALU.add)
                            else:
                                lo = 256 * KINDS1[name] + HD * h
                                last = dve.tensor_scalar(R2[:, i, lo:lo + HD], src, f, None, ALU.mult)
                    last.then_inc(o_out, 1)
                elif what == "Z":
                    _, h, g = step
                    lo = GROUP_AT[g]
                    w = sum(SEQ - P * j for j in KEYS[g])
                    dve.wait_ge(sc_in, nth[step] + 1)
                    if h < 2:
                        dve.wait_ge(tr_in, nth["T", "moba", 2 + h, 2] + 1)
                    else:
                        dve.wait_ge(a_done, 3 * (h - 2) + g + 1)
                    dve.tensor_copy(prob[:, h % 2, lo:lo + w], SC[nth[step] % 2][:, 0:w]).then_inc(sc_out, 1)
                elif what == "sp":
                    h = step[1]
                    dve.wait_ge(sc_out, nth["Z", h, 2] + 1)
                    if h:
                        dve.wait_ge(sp_done, h)
                    dve.scalar_tensor_tensor(out=soft[:, :], in0=prob[:, h % 2, :], scalar=-1.0, in1=prob[:, h % 2, :],
                                             op0=ALU.mult, op1=ALU.min).then_inc(sp_abs, 1)
                elif what == "sp_b":
                    h = step[1]
                    dve.wait_ge(sp_ln, h + 1)
                    link(dve.scalar_tensor_tensor(out=soft[:, :], in0=prob[:, h % 2, :], scalar=0.0, in1=soft[:, :],
                                                  op0=ALU.max, op1=ALU.add))
                    if h:
                        dve.wait_ge(tr_in, nth["F", h - 1, 2] + 1)
                    link(dve.tensor_copy(soft_parts[:, 0, :], soft[:, :]))
                    dve.tensor_tensor(soft_parts[:, 1, :], soft[:, :], soft_parts[:, 0, :].bitcast(F32), ALU.subtract).then_inc(sp_done, 1)
                elif what == "F":
                    _, h, g = step
                    lo = GROUP_AT[g]
                    w = sum(SEQ - P * j for j in KEYS[g])
                    dve.wait_ge(tr_in, nth[step] + 1)
                    dve.tensor_tensor(prob[:, h % 2, lo:lo + w], prob[:, h % 2, lo:lo + w], TR[:, 0:w], ALU.subtract).then_inc(tr_out, 1)
                elif what == "OS":
                    h = step[1]
                    dve.wait_ge(o_in, nth[step] + 1)
                    lo = 512 + HD * h
                    e = HD * (h % 2)
                    dve.tensor_copy(R2[:, :, lo:lo + HD], OB.rearrange("p (i d) -> p i d", i=4)[:, :, e:e + HD]).then_inc(o_out, 1)
                elif what == "blocks":
                    dve.wait_ge(tr_out, nth["qt", "cmp", 3] + 1)
                    dve.wait_ge(s_small2, 16 * 8)
                    for v in range(2):
                        for g in range(2):
                            dve.memset(blocks[:, v, :, 32 * g + NCMP:32 * g + 32], 0.0)
                            src = cmpT[:, v, g, 0:480 + 32].rearrange("p (i u) -> p i u", u=16)
                            for hb in range(2):
                                s_ = src[:, hb:hb + NCMP, :].rearrange("p i (m e) -> p m i e", e=2)[:, :, :, 0]
                                dst = blocks[:, v, 8 * hb:8 * hb + 8, 32 * g:32 * g + NCMP]
                                pp = pos[:, 16 * v + 8 * hb:16 * v + 8 * hb + 8].unsqueeze(2).broadcast_to([P, 8, NCMP])
                                last = dve.tensor_tensor(dst, s_, pp, ALU.add)
                    last.then_inc(blk_done, 1)
                elif what == "hidden":
                    kv = step[1]
                    dve.wait_ge(hid_act, kv + 1)
                    dve.sem_inc(sc_out, 1)
                    if kv == 1:
                        for f in range(2):
                            for g in range(2):
                                last = dve.tensor_copy(hidV[:, f, g, :].rearrange("p (r i) -> p r i", r=4),
                                                       hidT[:, 1, f, 32 * g:32 * g + 32].unsqueeze(1).broadcast_to([P, 4, 32]))
                        last.then_inc(hid_rep, 1)
                elif what == "cmpkv":
                    dve.wait_ge(sc_in, nth[step] + 1)
                    bank = SC[nth[step] % 2]
                    link(dve.memset(vbd[:, :, :, :], 0.0))
                    kc = bank[:, 0:64].rearrange("p (g n) -> p g n", g=2)
                    link(dve.tensor_copy(kcS[:, :, 0, :], kc))
                    dve.tensor_tensor(kcS[:, :, 1, :], kc, kcS[:, :, 0, :].bitcast(F32), ALU.subtract)
                    for r in range(4):
                        last = dve.tensor_copy(vbd[32 * r:32 * r + 32, :, r, :], bank[32 * r:32 * r + 32, 64:192].rearrange("p (g d) -> p g d", g=2))
                    last.then_inc(sc_out, 1)
                elif what == "gates":
                    wait_evacuated(dve, ("ev", "in2", 2))
                    dve.wait_ge(gate_e, 1)
                    link(dve.tensor_scalar(g_tmp, g_tmp, 1.0, None, ALU.add))
                    link(dve.reciprocal(gates, g_tmp))
                elif what == "CS":
                    i = step[1]
                    p3 = prob[:, 0, 256 * i:256 * i + 256].rearrange("p (h n) -> p h n", h=8)
                    dve.wait_ge(sc_in, nth[step] + 1)
                    if i == 0:
                        dve.wait_ge(tr_in, nth["qt", "slc", 3] + 1)
                    parts = SC[nth[step] % 2].rearrange("p (h x n) -> p h x n", h=8, x=2)
                    link(dve.tensor_tensor(p3, parts[:, :, 0, :], cmp_bias[:, i, :, :], ALU.add))
                    dve.tensor_tensor(p3, p3, parts[:, :, 1, :], ALU.add).then_inc(sc_out, 1)
                    dve.wait_ge(sc_out, nth[step] + 1)
                    link(dve.tensor_reduce(cm8, p3, AX.X, ALU.max))
                    link(dve.tensor_scalar(cm8, cm8, FLOOR, None, ALU.max))
                    dve.tensor_tensor(p3, p3, cm8.unsqueeze(2).broadcast_to([P, 8, 32]), ALU.subtract).then_inc(cs_sub, 1)
                elif what == "CS_b":
                    i = step[1]
                    p3 = prob[:, 0, 256 * i:256 * i + 256].rearrange("p (h n) -> p h n", h=8)
                    dve.wait_ge(cs_exp, i + 1)
                    link(dve.tensor_reduce(cs8, p3, AX.X, ALU.add))
                    link(dve.tensor_scalar(cs8, cs8, 1e-30, None, ALU.max))
                    link(dve.reciprocal(cs8, cs8))
                    gv = gates.rearrange("p (h b q) -> p h b q", h=8, b=3)[:, :, 0, POS[i]]
                    link(dve.tensor_tensor(cf8[:, 8 * i:8 * i + 8], cs8, gv, ALU.mult))
                elif what == "CT":
                    i = step[1]
                    dve.wait_ge(tr_in, nth[step] + 1)
                    dve.wait_ge(o_in, nth["CO", i - 1] + 1 if i else nth[last_o(("swa", 3))] + 1)
                    dve.tensor_copy(probT[:, 0:256], TR[:, 0:256]).then_inc(tr_out, 1)
                elif what == "CO":
                    i = step[1]
                    dve.wait_ge(o_in, nth[step] + 1)
                    if i == 0:
                        dve.wait_ge(sc_in, nth["hidden", 1] + 1)
                    dve.tensor_tensor(R1[:, i, 0:512].rearrange("p (h d) -> p h d", h=8), OB.rearrange("p (h d) -> p h d", h=8),
                                      cf8[:, 8 * i:8 * i + 8].unsqueeze(2).broadcast_to([P, 8, HD]), ALU.mult).then_inc(o_out, 1)
                elif what == "gm_w":
                    u = step[1]
                    dve.wait_ge(tr_in, nth[step] + 1)
                    dve.tensor_tensor(wsT[:, 4 * u:4 * u + 4, :], TR.rearrange("p (q n) -> p q n", q=4),
                                      tri[:, 0:P].bitcast(F32).unsqueeze(1).broadcast_to([P, 4, P]), ALU.mult).then_inc(tr_out, 1)
                elif what == "gm_a":
                    t = step[1]
                    dve.wait_ge(gelu_done, t + 1)
                    z = zv[:, t, :]
                    link(dve.tensor_reduce(negmu[:, t:t + 1], z, AX.X, ALU.add))
                    link(dve.tensor_scalar(negmu[:, t:t + 1], negmu[:, t:t + 1], 1.0 / 512, None, ALU.mult))
                    link(dve.tensor_scalar(z, z, negmu[:, t:t + 1], None, ALU.subtract))
                    link(dve.tensor_tensor_reduce(sq[:, :], z, z, 1.0, 0.0, ALU.mult, ALU.add, ss_g[:, t:t + 1]))
                    dve.tensor_scalar(ss_g[:, t:t + 1], ss_g[:, t:t + 1], 1.0 / 512, LN_EPS, ALU.mult, ALU.add).then_inc(ms_ready, 1)
                elif what == "gm_b":
                    t = step[1]
                    z = zv[:, t, :]
                    dve.wait_ge(r_ready, nth["gm_a", t] + 1)
                    dve.wait_ge(s_gm_in, 48)
                    link(dve.scalar_tensor_tensor(out=z, in0=z, scalar=rr_g[:, t:t + 1], in1=ln_g[:, :], op0=ALU.mult, op1=ALU.mult))
                    dve.tensor_tensor(z, z, ln_b[:, :], ALU.add).then_inc(gm_n, 1)
                elif what == "gm":
                    u = step[1]
                    dve.wait_ge(sc_in, nth[step] + 1)
                    dve.wait_ge(gelu_done, 2 * NT)
                    for q in range(2):
                        g = 2 * u + q
                        dst = R1[:, :, 512 + HD * g:512 + HD * g + HD]
                        last = dve.scalar_tensor_tensor(out=dst, in0=SC[nth[step] % 2][:, 256 * q:256 * q + 256].rearrange("p (n d) -> p n d", n=4),
                                                        scalar=gmlp_b[:, g:g + 1], in1=dst, op0=ALU.add, op1=ALU.mult)
                    last.then_inc(sc_out, 1)
                elif what == "act":
                    kt = step[1]
                    dve.wait_ge(act_hi, kt + 1)
                    dve.tensor_tensor(XT[:, kt % 8, 1, :], actT[:, kt, :], XT[:, kt % 8, 0, :].bitcast(F32), ALU.subtract).then_inc(act_lo, 1)
                elif what == "sqa":
                    t = step[1]
                    if t == 0:
                        dve.wait_ge(s_gain, 64)
                    dve.wait_ge(sqa_done, t + 1)
                    link(dve.tensor_tensor(R1[:, t, 0:512], R1[:, t, 0:512], gain[1][:, 0:512], ALU.mult))
                elif what == "post" and step[1] == "mix":
                    t = step[2]
                    wait_bank(dve, "out2", 1, t)
                    dve.wait_ge(r_ready, nth["ms", "mix", t] + 1)
                    dve.scalar_tensor_tensor(out=R1[:, t, 512:D], in0=MM[t], scalar=rr[:, t:t + 1], in1=gain[1][:, 512:D],
                                             op0=ALU.mult, op1=ALU.mult).then_inc(post_scaled, 1)
                    dve.scalar_tensor_tensor(out=R2[:, t, 0:512], in0=R1[:, t, 0:512], scalar=rr[:, t:t + 1], in1=R2[:, t, 0:512],
                                             op0=ALU.mult, op1=ALU.add).then_inc(post_dve, 1)
                elif what == "post":
                    t = step[2]
                    if t == 0:
                        dve.wait_ge(s_gain, 80)
                    dve.wait_ge(r_ready, nth["ms", "ffn", t] + 1)
                    dve.scalar_tensor_tensor(out=R1[:, t, 0:512], in0=SET[0][t], scalar=rr[:, t:t + 1], in1=gain[1][:, 0:512],
                                             op0=ALU.mult, op1=ALU.mult).then_inc(post_scaled, 1)
                    link(dve.scalar_tensor_tensor(out=R1[:, t, 512:D], in0=SET[1][t], scalar=rr[:, t:t + 1], in1=gain[1][:, 512:D],
                                                  op0=ALU.mult, op1=ALU.mult))
                    dve.tensor_tensor(R2[:, t, 512:D], R2[:, t, 512:D], R1[:, t, 512:D], ALU.add).then_inc(post_dve, 1)

        @block.gpsimd
        def _(pool):
            group_of = {}
            for g, (phase, chunk, part, s0, w) in enumerate(groups):
                for q in range(4):
                    group_of[s0 + q] = (g, q, w)
            for step in timeline:
                what = step[0]
                if what == "split":
                    s = step[1]
                    g, q, w = group_of[s]
                    pool.wait_ge(w_hi, s + 1)
                    pool.tensor_tensor(WR[:, s % RING, 1, 0:w], RAW[:, g % 2, q, 0:w], WR[:, s % RING, 0, 0:w].bitcast(F32),
                                       ALU.subtract).then_inc(w_lo, 1)
                    continue
                if what == "gx":
                    if by_pool(step):
                        _, phase, t, hf = step
                        pool.wait_ge(s_x[t], 16)
                        pool.wait_ge(s_gain, 16)
                        pool.tensor_tensor(R2[:, t, 512:D], R1[:, t, 512:D], gain[0][:, 512:D], ALU.mult).then_inc(gx_pool, 1)
                    continue
                if what == "post":
                    t = step[2]
                    cols = slice(512, D) if step[1] == "mix" else slice(0, 512)
                    pool.wait_ge(post_scaled, nth[step] + 1)
                    pool.tensor_tensor(R2[:, t, cols], R2[:, t, cols], R1[:, t, cols], ALU.add).then_inc(post_pool, 1)
                    continue
                if what == "ms" and step[1] in ("in1", "in2"):
                    src, dst, n = ss, rr, NT
                elif what == "ms":
                    src, dst, n = ss[:, step[2]:step[2] + 1], rr[:, step[2]:step[2] + 1], 1
                elif what == "gm_a":
                    src, dst, n = ss_g[:, step[1]:step[1] + 1], rr_g[:, step[1]:step[1] + 1], 1
                elif what == "qa":
                    src, dst, n = ms8, rr8, 8
                else:
                    continue
                pool.wait_ge(ms_ready, nth[step] + 1)
                pool.tensor_tensor(dst, src, half[:, 0:1].broadcast_to([P, n]) if n > 1 else half[:, 0:1], ALU.pow).then_inc(r_ready, 1)


_INS = [
    "x", "norm_gain", "w_in", "b_forget", "fox_qk_gain", "moba_qk_gain", "swa_qk_gain", "sinks", "w_out",
    "rel_bias", "rel_bias_2", "norm_mix_pre_2", "norm_mix_post_2", "norm_ffn_pre_2", "norm_ffn_post_2",
    "w_in_2", "cmp_pos_k_2", "cmp_w1_k_2", "cmp_w2_k_2", "cmp_pos_v_2", "cmp_w1_v_2", "cmp_w2_v_2",
    "gmlp_ln_g_2", "gmlp_ln_b_2", "gmlp_w_s_2", "gmlp_b_s_2", "w_out_2", "w_gate_up_2", "w_down_2",
]


def kernel(**inputs):
    import concourse.bacc as _bacc
    from concourse.bass_utils import run_bass_kernel_spmd as _run

    nc = _bacc.Bacc("TRN2", target_bir_lowering=False, num_devices=1)
    arrays, args, consts = {}, {}, {}
    for name in _INS:
        v = np.ascontiguousarray(inputs[name])
        arrays[f"in_{name}_dram"] = v
        args[name] = nc.dram_tensor(f"in_{name}_dram", v.shape, mybir.dt.from_np(v.dtype), kind="ExternalInput").ap()
    for name, v in constants().items():
        arrays[f"const_{name}_dram"] = v
        consts[name] = nc.dram_tensor(f"const_{name}_dram", v.shape, mybir.dt.from_np(v.dtype), kind="ExternalInput").ap()
    out = nc.dram_tensor("out_0_dram", (1, SEQ, D), F32, kind="ExternalOutput").ap()
    hybrid_two_block_kernel(nc, args, consts, out)
    r = _run(nc, [arrays], core_ids=[0])
    return r.results[0]["out_0_dram"]
```
